# Optimizing a Trainium2 kernel written in Bass

```python
import math
import jax, jax.numpy as jnp
from jax import lax
import numpy as np

D_MODEL = 2048
BATCH = 1
SEQ = 256
DEPTH = 1

N_BRANCH = 4
BRANCH_WIDTH = 512

GLA_HEADS = 4
GLA_DK = 64
GLA_DV = 128
GLA_LOWRANK = 16
GLA_NORMALIZER = 16.0
GLA_CHUNK = 64

LRU_WIDTH = 512
LRU_BLOCKS = 4
LRU_BLOCK_DIM = LRU_WIDTH // LRU_BLOCKS
LRU_CONV = 4
LRU_C = 8.0

NSA_HEADS = 4
NSA_DH = 128
NSA_CMP_LEN = 32
NSA_CMP_STRIDE = 16
NSA_SEL_BLOCK = 64
NSA_SEL_TOPK = 16
NSA_WINDOW = 512
NSA_QBLOCK = 128

RWKV_HEADS = 8
RWKV_DH = 64
RWKV_WIDTH = RWKV_HEADS * RWKV_DH
RWKV_W_LORA = 96
RWKV_A_LORA = 96
RWKV_G_LORA = 256
RWKV_SPLITS = (RWKV_WIDTH, RWKV_WIDTH, RWKV_WIDTH, RWKV_W_LORA, RWKV_A_LORA, RWKV_G_LORA)
RWKV_IN = sum(RWKV_SPLITS)

NUM_BUCKETS = 32
MAX_DISTANCE = 128

D_FF = 5632
FFN_CONV = 3

IN_SPLITS = (
    GLA_HEADS * GLA_DK, GLA_HEADS * GLA_DK, GLA_HEADS * GLA_DV, GLA_HEADS * GLA_DV, GLA_LOWRANK,
    LRU_WIDTH, LRU_WIDTH,
    NSA_HEADS * NSA_DH, 6 * NSA_DH, 3 * NSA_HEADS,
    RWKV_IN,
    N_BRANCH * D_MODEL,
)
IN_TOTAL = sum(IN_SPLITS)
NEG_BIG = 1e9


def rms_norm(x, g, eps=1e-6):
    xf = x.astype(jnp.float32)
    y = xf * lax.rsqrt(jnp.mean(xf * xf, axis=-1, keepdims=True) + eps)
    return (y * g.astype(jnp.float32)).astype(x.dtype)

def causal_dwconv(x, w, b):
    k, c = w.shape
    y = lax.conv_general_dilated(x, w[:, None, :].astype(x.dtype), window_strides=(1,), padding=[(k - 1, 0)],
                                 dimension_numbers=('NWC', 'WIO', 'NWC'), feature_group_count=c)
    return y + b.astype(x.dtype)

def split_cols(t, widths):
    parts, start = [], 0
    for w in widths:
        parts.append(t[..., start:start + w])
        start += w
    return parts

def masked_softmax(logits, mask):
    logits = jnp.where(mask, logits.astype(jnp.float32), -NEG_BIG)
    m = jnp.max(logits, axis=-1, keepdims=True)
    p = jnp.where(mask, jnp.exp(logits - m), 0.0)
    return p / jnp.maximum(jnp.sum(p, axis=-1, keepdims=True), 1e-30)

def t5_bucket(dist):
    n = jnp.maximum(dist, 0)
    max_exact = NUM_BUCKETS // 2
    nf = jnp.maximum(n, 1).astype(jnp.float32)
    large = max_exact + (jnp.log(nf / max_exact) / math.log(MAX_DISTANCE / max_exact)
                         * (NUM_BUCKETS - max_exact)).astype(jnp.int32)
    large = jnp.minimum(large, NUM_BUCKETS - 1)
    return jnp.where(n < max_exact, n, large)

def gla_mixer(q, k, v, g, lr, w_gk, b_gk, out_gain):
    B, S, _ = q.shape
    H, dk, dv, C = GLA_HEADS, GLA_DK, GLA_DV, GLA_CHUNK
    nc = S // C
    f32 = jnp.float32
    log_a = jax.nn.log_sigmoid((lr @ w_gk + b_gk).astype(f32)) / GLA_NORMALIZER

    def chunks(t, d):
        return t.astype(f32).reshape(B, nc, C, H, d).transpose(1, 0, 3, 2, 4)

    qc = chunks(q, dk) * dk ** -0.5
    kc = chunks(k, dk)
    vc = chunks(v, dv)
    bc = jnp.cumsum(chunks(log_a, dk), axis=3)
    causal = jnp.tril(jnp.ones((C, C), dtype=bool))[:, :, None]

    def step(state, inp):
        qi, ki, vi, bi = inp
        o_inter = jnp.einsum('bhtd,bhdv->bhtv', qi * jnp.exp(bi), state)
        decay = jnp.exp(jnp.where(causal, bi[:, :, :, None, :] - bi[:, :, None, :, :], -jnp.inf))
        scores = jnp.einsum('bhtd,bhsd,bhtsd->bhts', qi, ki, decay)
        o = o_inter + jnp.einsum('bhts,bhsv->bhtv', scores, vi)
        b_last = bi[:, :, -1:, :]
        state = jnp.exp(b_last[:, :, 0, :, None]) * state + jnp.einsum('bhsd,bhsv->bhdv', ki * jnp.exp(b_last - bi), vi)
        return state, o

    s0 = jnp.zeros((B, H, dk, dv), f32)
    _, o = lax.scan(step, s0, (qc, kc, vc, bc))
    o = o.transpose(1, 0, 3, 2, 4).reshape(B, S, H, dv)
    o = rms_norm(o, out_gain) * jax.nn.silu(g.astype(f32)).reshape(B, S, H, dv)
    return o.reshape(B, S, H * dv).astype(q.dtype)

def rglru_mixer(xb, gb, conv_w, conv_b, w_a, b_a, w_i, b_i, lam):
    B, S, _ = xb.shape
    f32 = jnp.float32
    xc = causal_dwconv(xb, conv_w, conv_b)
    xh = xc.reshape(B, S, LRU_BLOCKS, LRU_BLOCK_DIM)
    r = jax.nn.sigmoid(jnp.einsum('bsni,nij->bsnj', xh, w_a).reshape(B, S, LRU_WIDTH) + b_a).astype(f32)
    i = jax.nn.sigmoid(jnp.einsum('bsni,nij->bsnj', xh, w_i).reshape(B, S, LRU_WIDTH) + b_i).astype(f32)
    log_a = LRU_C * r * jax.nn.log_sigmoid(lam.astype(f32))
    a = jnp.exp(log_a)
    u = jnp.sqrt(-jnp.expm1(2.0 * log_a)) * (i * xc.astype(f32))
    _, h = lax.associative_scan(lambda e, l: (e[0] * l[0], l[0] * e[1] + l[1]), (a, u), axis=1)
    return (h * jax.nn.gelu(gb.astype(f32))).astype(xb.dtype)

def nsa_mixer(q, kv, gate, rel_bias, cmp_pos, cmp_k1, cmp_k2, cmp_v1, cmp_v2, q_gain, k_gain):
    B, S, _ = q.shape
    H, dh = NSA_HEADS, NSA_DH
    L, D, SB, QB, W = NSA_CMP_LEN, NSA_CMP_STRIDE, NSA_SEL_BLOCK, NSA_QBLOCK, NSA_WINDOW
    f32 = jnp.float32
    scale = dh ** -0.5
    pos = jnp.arange(S)
    qh = rms_norm(q.reshape(B, S, H, dh), q_gain).transpose(0, 2, 1, 3)
    k_cmp, v_cmp, k_slc, v_slc, k_win, v_win = split_cols(kv, (dh,) * 6)

    n_cmp = (S - L) // D + 1
    cmp_start = jnp.arange(n_cmp) * D
    idx = cmp_start[:, None] + jnp.arange(L)[None, :]

    def compress(t, w1, w2):
        blocks = (t[:, idx, :] + cmp_pos).reshape(B, n_cmp, L * dh)
        return jax.nn.gelu(blocks @ w1) @ w2

    kc = rms_norm(compress(k_cmp, cmp_k1, cmp_k2), k_gain)
    vc = compress(v_cmp, cmp_v1, cmp_v2)
    dist_c = pos[:, None] - (cmp_start + L - 1)[None, :]
    bias_c = rel_bias[t5_bucket(dist_c)].transpose(2, 0, 1).astype(f32)
    logit_c = jnp.einsum('bhsd,bnd->bhsn', qh, kc).astype(f32) * scale + bias_c
    p_c = masked_softmax(logit_c, dist_c >= 0)
    o_cmp = jnp.einsum('bhsn,bnd->bhsd', p_c, vc.astype(f32))

    n_sel = S // SB
    top_k = min(NSA_SEL_TOPK, n_sel)
    sel_start = jnp.arange(n_sel) * SB
    overlap = ((cmp_start[:, None] < sel_start[None, :] + SB) &
               (cmp_start[:, None] + L > sel_start[None, :])).astype(f32)
    score = jnp.einsum('bhsn,nj->bsj', p_c, overlap)
    blk = jnp.arange(n_sel)[None, :]
    cur = (pos // SB)[:, None]
    forced = (blk == 0) | (blk == cur) | (blk == cur - 1)
    score = jnp.where(forced, NEG_BIG, jnp.where(sel_start[None, :] <= pos[:, None], score, -NEG_BIG))
    _, sel_idx = lax.top_k(score, top_k)

    k_blocks = rms_norm(k_slc, k_gain).reshape(B, n_sel, SB, dh)
    v_blocks = v_slc.reshape(B, n_sel, SB, dh)
    nq = S // QB
    q_blocks = qh.reshape(B, H, nq, QB, dh).transpose(2, 0, 1, 3, 4)
    idx_blocks = sel_idx.reshape(B, nq, QB, top_k).transpose(1, 0, 2, 3)
    pos_blocks = pos.reshape(nq, QB)
    gather = jax.vmap(lambda blocks, ids: blocks[ids])

    def select_block(args):
        qb, ib, pb = args
        kg = gather(k_blocks, ib).reshape(B, QB, top_k * SB, dh)
        vg = gather(v_blocks, ib).reshape(B, QB, top_k * SB, dh)
        kpos = (ib[..., None] * SB + jnp.arange(SB)).reshape(B, QB, top_k * SB)
        dist = pb[None, :, None] - kpos
        bias = rel_bias[t5_bucket(dist)].transpose(0, 3, 1, 2).astype(f32)
        logit = jnp.einsum('bhtd,btkd->bhtk', qb, kg).astype(f32) * scale + bias
        p = masked_softmax(logit, (dist >= 0)[:, None])
        return jnp.einsum('bhtk,btkd->bhtd', p, vg.astype(f32))

    o_sel = lax.map(select_block, (q_blocks, idx_blocks, pos_blocks))
    o_sel = o_sel.transpose(1, 2, 0, 3, 4).reshape(B, H, S, dh)

    nw = W // QB

    def band(t):
        tp = jnp.pad(t, ((0, 0), (W, 0), (0, 0))).reshape(B, nq + nw, QB, dh)
        return jnp.concatenate([tp[:, j:j + nq] for j in range(nw + 1)], axis=2)

    kw = band(rms_norm(k_win, k_gain))
    vw = band(v_win)
    kpos_w = jnp.arange(nq)[:, None] * QB - W + jnp.arange((nw + 1) * QB)[None, :]
    dist_w = pos_blocks[:, :, None] - kpos_w[:, None, :]
    mask_w = (dist_w >= 0) & (dist_w < W) & (kpos_w[:, None, :] >= 0)
    bias_w = rel_bias[t5_bucket(dist_w)].transpose(3, 0, 1, 2).astype(f32)
    logit_w = jnp.einsum('bhnqd,bnkd->bhnqk', qh.reshape(B, H, nq, QB, dh), kw).astype(f32) * scale + bias_w
    p_w = masked_softmax(logit_w, mask_w)
    o_win = jnp.einsum('bhnqk,bnkd->bhnqd', p_w, vw.astype(f32)).reshape(B, H, S, dh)

    g = jax.nn.sigmoid(gate.astype(f32)).reshape(B, S, 3, H).transpose(2, 0, 3, 1)[..., None]
    o = g[0] * o_cmp + g[1] * o_sel + g[2] * o_win
    return o.transpose(0, 2, 1, 3).reshape(B, S, H * dh).astype(q.dtype)

def rwkv7_mixer(feat, mu, w0, w_lora, a0, a_lora, g_lora, k_k, k_a, r_k, ln_w, ln_b):
    B, S, _ = feat.shape
    H, N = RWKV_HEADS, RWKV_DH
    f32 = jnp.float32
    out_dtype = feat.dtype
    feat = feat.astype(f32)
    prev = jnp.pad(feat, ((0, 0), (1, 0), (0, 0)))[:, :-1]
    xm = feat + (prev - feat) * mu
    r, k, v, xw, xa, xg = split_cols(xm, RWKV_SPLITS)
    log_w = -math.exp(-0.5) * jax.nn.sigmoid(w0 + jnp.tanh(xw) @ w_lora)
    a = jax.nn.sigmoid(a0 + xa @ a_lora)
    g = jax.nn.sigmoid(xg) @ g_lora
    heads = lambda t: t.reshape(B, S, H, N)
    kk = heads(k * k_k)
    kk = kk / jnp.maximum(jnp.linalg.norm(kk, axis=-1, keepdims=True), 1e-12)
    k = k * (1.0 + (a - 1.0) * k_a)
    tm = lambda t: t.transpose(1, 0, 2, 3)

    def step(state, inp):
        r_t, w_t, k_t, v_t, kk_t, a_t = inp
        sa = jnp.einsum('bhij,bhj->bhi', state, -kk_t)
        state = (state * w_t[:, :, None, :] + sa[..., None] * (kk_t * a_t)[:, :, None, :]
                 + v_t[..., None] * k_t[:, :, None, :])
        return state, jnp.einsum('bhij,bhj->bhi', state, r_t)

    s0 = jnp.zeros((B, H, N, N), f32)
    xs = (tm(heads(r)), tm(heads(jnp.exp(log_w))), tm(heads(k)), tm(heads(v)), tm(kk), tm(heads(a)))
    _, y = lax.scan(step, s0, xs)
    y = y.transpose(1, 0, 2, 3)
    mean = jnp.mean(y, axis=-1, keepdims=True)
    var = jnp.mean(jnp.square(y - mean), axis=-1, keepdims=True)
    y = (y - mean) * lax.rsqrt(var + 64e-5) * ln_w.reshape(H, N) + ln_b.reshape(H, N)
    y = y + jnp.sum(heads(r) * heads(k) * r_k, axis=-1, keepdims=True) * heads(v)
    return (y.reshape(B, S, H * N) * g).astype(out_dtype)

def first_inputs(seed: int = 0) -> dict:
    key = jax.random.key(seed)
    ks = iter(jax.random.split(key, 40))
    f32 = jnp.float32

    def nrm(shape, scale):
        return jax.random.normal(next(ks), shape, f32) * scale

    def gain(shape):
        return 1.0 + nrm(shape, 0.05)

    Lh = DEPTH
    res_scale = (2 * DEPTH) ** -0.5
    x = nrm((BATCH, SEQ, D_MODEL), 1.0)
    rel_bias = nrm((NUM_BUCKETS, NSA_HEADS), 0.5)
    attn_norm = gain((Lh, D_MODEL))
    ffn_norm = gain((Lh, D_MODEL))
    w_in = nrm((Lh, D_MODEL, IN_TOTAL), D_MODEL ** -0.5)
    gla_w_gk = nrm((Lh, GLA_LOWRANK, GLA_HEADS * GLA_DK), GLA_LOWRANK ** -0.5)
    gla_b_gk = nrm((Lh, GLA_HEADS * GLA_DK), 0.5)
    gla_out_norm = gain((Lh, GLA_DV))
    lru_conv_w = nrm((Lh, LRU_CONV, LRU_WIDTH), LRU_CONV ** -0.5)
    lru_conv_b = nrm((Lh, LRU_WIDTH), 0.02)
    lru_w_a = nrm((Lh, LRU_BLOCKS, LRU_BLOCK_DIM, LRU_BLOCK_DIM), LRU_BLOCK_DIM ** -0.5)
    lru_b_a = nrm((Lh, LRU_WIDTH), 0.1)
    lru_w_i = nrm((Lh, LRU_BLOCKS, LRU_BLOCK_DIM, LRU_BLOCK_DIM), LRU_BLOCK_DIM ** -0.5)
    lru_b_i = nrm((Lh, LRU_WIDTH), 0.1)
    a_base = jax.random.uniform(next(ks), (Lh, LRU_WIDTH), f32, minval=0.9, maxval=0.999)
    s = a_base ** (1.0 / LRU_C)
    lru_lambda = jnp.log(s) - jnp.log1p(-s)
    nsa_cmp_pos = nrm((Lh, NSA_CMP_LEN, NSA_DH), 0.1)
    nsa_cmp_k1 = nrm((Lh, NSA_CMP_LEN * NSA_DH, NSA_DH), (NSA_CMP_LEN * NSA_DH) ** -0.5)
    nsa_cmp_k2 = nrm((Lh, NSA_DH, NSA_DH), NSA_DH ** -0.5)
    nsa_cmp_v1 = nrm((Lh, NSA_CMP_LEN * NSA_DH, NSA_DH), (NSA_CMP_LEN * NSA_DH) ** -0.5)
    nsa_cmp_v2 = nrm((Lh, NSA_DH, NSA_DH), NSA_DH ** -0.5)
    nsa_q_norm = gain((Lh, NSA_DH))
    nsa_k_norm = gain((Lh, NSA_DH))
    rwkv_mu = jax.random.uniform(next(ks), (Lh, RWKV_IN), f32)
    rwkv_w0 = nrm((Lh, RWKV_WIDTH), 1.0)
    rwkv_w_lora = nrm((Lh, RWKV_W_LORA, RWKV_WIDTH), RWKV_W_LORA ** -0.5)
    rwkv_a0 = nrm((Lh, RWKV_WIDTH), 0.5)
    rwkv_a_lora = nrm((Lh, RWKV_A_LORA, RWKV_WIDTH), RWKV_A_LORA ** -0.5)
    rwkv_g_lora = nrm((Lh, RWKV_G_LORA, RWKV_WIDTH), RWKV_G_LORA ** -0.5)
    rwkv_k_k = 0.85 + nrm((Lh, RWKV_WIDTH), 0.05)
    rwkv_k_a = gain((Lh, RWKV_WIDTH))
    rwkv_r_k = nrm((Lh, RWKV_HEADS, RWKV_DH), 0.1)
    rwkv_ln_w = gain((Lh, RWKV_WIDTH))
    rwkv_ln_b = nrm((Lh, RWKV_WIDTH), 0.02)
    w_branch = nrm((Lh, N_BRANCH, BRANCH_WIDTH, D_MODEL), BRANCH_WIDTH ** -0.5)
    w_out = nrm((Lh, D_MODEL, D_MODEL), D_MODEL ** -0.5 * res_scale)
    ffn_up = nrm((Lh, D_MODEL, 2 * D_FF), D_MODEL ** -0.5)
    ffn_conv_w = nrm((Lh, FFN_CONV, 2 * D_FF), FFN_CONV ** -0.5)
    ffn_conv_b = nrm((Lh, 2 * D_FF), 0.02)
    ffn_down = nrm((Lh, D_FF, D_MODEL), D_FF ** -0.5 * res_scale)
    return {'x': x, 'rel_bias': rel_bias, 'attn_norm': attn_norm, 'ffn_norm': ffn_norm, 'w_in': w_in,
            'gla_w_gk': gla_w_gk, 'gla_b_gk': gla_b_gk, 'gla_out_norm': gla_out_norm,
            'lru_conv_w': lru_conv_w, 'lru_conv_b': lru_conv_b, 'lru_w_a': lru_w_a, 'lru_b_a': lru_b_a,
            'lru_w_i': lru_w_i, 'lru_b_i': lru_b_i, 'lru_lambda': lru_lambda,
            'nsa_cmp_pos': nsa_cmp_pos, 'nsa_cmp_k1': nsa_cmp_k1, 'nsa_cmp_k2': nsa_cmp_k2,
            'nsa_cmp_v1': nsa_cmp_v1, 'nsa_cmp_v2': nsa_cmp_v2, 'nsa_q_norm': nsa_q_norm, 'nsa_k_norm': nsa_k_norm,
            'rwkv_mu': rwkv_mu, 'rwkv_w0': rwkv_w0, 'rwkv_w_lora': rwkv_w_lora, 'rwkv_a0': rwkv_a0,
            'rwkv_a_lora': rwkv_a_lora, 'rwkv_g_lora': rwkv_g_lora, 'rwkv_k_k': rwkv_k_k, 'rwkv_k_a': rwkv_k_a,
            'rwkv_r_k': rwkv_r_k, 'rwkv_ln_w': rwkv_ln_w, 'rwkv_ln_b': rwkv_ln_b,
            'w_branch': w_branch, 'w_out': w_out, 'ffn_up': ffn_up, 'ffn_conv_w': ffn_conv_w,
            'ffn_conv_b': ffn_conv_b, 'ffn_down': ffn_down}

def first_block(x, rel_bias, attn_norm, ffn_norm, w_in, gla_w_gk, gla_b_gk, gla_out_norm,
              lru_conv_w, lru_conv_b, lru_w_a, lru_b_a, lru_w_i, lru_b_i, lru_lambda,
              nsa_cmp_pos, nsa_cmp_k1, nsa_cmp_k2, nsa_cmp_v1, nsa_cmp_v2, nsa_q_norm, nsa_k_norm,
              rwkv_mu, rwkv_w0, rwkv_w_lora, rwkv_a0, rwkv_a_lora, rwkv_g_lora, rwkv_k_k, rwkv_k_a,
              rwkv_r_k, rwkv_ln_w, rwkv_ln_b, w_branch, w_out, ffn_up, ffn_conv_w, ffn_conv_b, ffn_down):
    B, S, _ = x.shape
    for l in range(DEPTH):
        h = rms_norm(x, attn_norm[l])
        proj = h @ w_in[l]
        (gla_q, gla_k, gla_v, gla_g, gla_lr, lru_x, lru_g,
         nsa_q, nsa_kv, nsa_gate, rwkv_feat, merge_gate) = split_cols(proj, IN_SPLITS)
        y_a = gla_mixer(gla_q, gla_k, gla_v, gla_g, gla_lr, gla_w_gk[l], gla_b_gk[l], gla_out_norm[l])
        y_b = rglru_mixer(lru_x, lru_g, lru_conv_w[l], lru_conv_b[l], lru_w_a[l], lru_b_a[l],
                          lru_w_i[l], lru_b_i[l], lru_lambda[l])
        y_c = nsa_mixer(nsa_q, nsa_kv, nsa_gate, rel_bias, nsa_cmp_pos[l], nsa_cmp_k1[l], nsa_cmp_k2[l],
                        nsa_cmp_v1[l], nsa_cmp_v2[l], nsa_q_norm[l], nsa_k_norm[l])
        y_d = rwkv7_mixer(rwkv_feat, rwkv_mu[l], rwkv_w0[l], rwkv_w_lora[l], rwkv_a0[l], rwkv_a_lora[l],
                          rwkv_g_lora[l], rwkv_k_k[l], rwkv_k_a[l], rwkv_r_k[l], rwkv_ln_w[l], rwkv_ln_b[l])
        gates = jax.nn.sigmoid(merge_gate).reshape(B, S, N_BRANCH, D_MODEL)
        merged = jnp.zeros_like(x)
        for n, y in enumerate((y_a, y_b, y_c, y_d)):
            merged = merged + gates[:, :, n] * (y @ w_branch[l, n])
        x = x + merged @ w_out[l]
        h = rms_norm(x, ffn_norm[l])
        u = causal_dwconv(h @ ffn_up[l], ffn_conv_w[l], ffn_conv_b[l])
        u_gate, u_val = jnp.split(u, 2, axis=-1)
        x = x + (jax.nn.silu(u_gate) * u_val) @ ffn_down[l]
    return x


DEPTH_2 = 2

HEAD_DIM = 64
MIX_WIDTH = D_MODEL // 4
BRANCH_W = MIX_WIDTH // 2
N_HEADS = BRANCH_W // HEAD_DIM
N_IN_PARTS = 8
ROPE_THETA = 10000.0
DIL_PAIRS = ((128, 1), (512, 4), (2048, 16))
DIL_STEPS = 128
MOBA_BLOCK = 256
MOBA_TOPK = 3
DIFF_HEAD_DIM = HEAD_DIM // 2
Q_BLOCK = 128
RMS_EPS = 1e-6
N_ODD = DEPTH_2 // 2


def _rmsnorm(x, g):
    xf = x.astype(jnp.float32)
    y = xf * lax.rsqrt(jnp.mean(xf * xf, axis=-1, keepdims=True) + RMS_EPS)
    return (y * g.astype(jnp.float32)).astype(x.dtype)

def _rope(t, pos):
    d = t.shape[-1]
    half = d // 2
    inv = ROPE_THETA ** (-jnp.arange(half, dtype=jnp.float32) / half)
    ang = pos.astype(jnp.float32)[:, None] * inv[None, :]
    cos, sin = jnp.cos(ang), jnp.sin(ang)
    tf = t.astype(jnp.float32)
    t1, t2 = tf[..., :half], tf[..., half:]
    return jnp.concatenate([t1 * cos - t2 * sin, t1 * sin + t2 * cos], axis=-1).astype(t.dtype)

def _heads(t):
    b, s, _ = t.shape
    return t.reshape(b, s, N_HEADS, -1).transpose(0, 2, 1, 3)

def _merge(t):
    b, h, s, d = t.shape
    return t.transpose(0, 2, 1, 3).reshape(b, s, h * d)

def _dilated_branch(q, k, v, r):
    b, h, s, d = q.shape
    L = -(-s // (r * DIL_STEPS)) * DIL_STEPS
    pad = L * r - s
    nb = L // DIL_STEPS

    def to_phase(t):
        t = jnp.pad(t, ((0, 0), (0, 0), (0, pad), (0, 0)))
        t = t.reshape(b, h, L, r, d).transpose(0, 1, 3, 2, 4)
        return t.reshape(b, h, r, nb, DIL_STEPS, d)

    qb, kb, vb = to_phase(q), to_phase(k), to_phase(v)
    prev = lambda t: jnp.pad(t, ((0, 0), (0, 0), (0, 0), (1, 0), (0, 0), (0, 0)))[:, :, :, :-1]
    kk = jnp.concatenate([prev(kb), kb], axis=4)
    vv = jnp.concatenate([prev(vb), vb], axis=4)
    sc = jnp.einsum('bhrnqd,bhrnkd->bhrnqk', qb, kk).astype(jnp.float32) / math.sqrt(d)
    i = jnp.arange(DIL_STEPS)[:, None]
    j = jnp.arange(2 * DIL_STEPS)[None, :]
    band = (j >= i) & (j <= i + DIL_STEPS)
    exists = (jnp.arange(nb)[:, None, None] > 0) | (j[None] >= DIL_STEPS)
    mask = band[None] & exists
    sc = jnp.where(mask, sc, -jnp.inf)
    m = jnp.max(sc, axis=-1, keepdims=True)
    p = jnp.exp(sc - m)
    den = jnp.sum(p, axis=-1)
    o = jnp.einsum('bhrnqk,bhrnkd->bhrnqd', p, vv.astype(jnp.float32)) / den[..., None]
    lse = m[..., 0] + jnp.log(den)
    o = o.reshape(b, h, r, L, d).transpose(0, 1, 3, 2, 4).reshape(b, h, L * r, d)[:, :, :s]
    lse = lse.reshape(b, h, r, L).transpose(0, 1, 3, 2).reshape(b, h, L * r)[:, :, :s]
    return o, lse

def _dilated_mixture(q, k, v):
    outs, lses = [], []
    for _, r in DIL_PAIRS:
        o, l = _dilated_branch(q, k, v, r)
        outs.append(o)
        lses.append(l)
    w = jax.nn.softmax(jnp.stack(lses, axis=0), axis=0)[..., None]
    return jnp.sum(w * jnp.stack(outs, axis=0), axis=0).astype(q.dtype)

def _moba(q, k, v):
    b, h, s, d = q.shape
    sp = -(-s // MOBA_BLOCK) * MOBA_BLOCK
    nblk = sp // MOBA_BLOCK
    kp = jnp.pad(k, ((0, 0), (0, 0), (0, sp - s), (0, 0)))
    vp = jnp.pad(v, ((0, 0), (0, 0), (0, sp - s), (0, 0)))
    kb = kp.reshape(b, h, nblk, MOBA_BLOCK, d)
    vb = vp.reshape(b, h, nblk, MOBA_BLOCK, d)
    kmean = jnp.mean(kb.astype(jnp.float32), axis=3)
    n_sel = min(MOBA_TOPK, nblk)
    nch = s // Q_BLOCK
    qc = q.reshape(b, h, nch, Q_BLOCK, d).transpose(2, 0, 1, 3, 4)
    starts = jnp.arange(nch, dtype=jnp.int32) * Q_BLOCK
    b_ix = jnp.arange(b)[:, None, None, None]
    h_ix = jnp.arange(h)[None, :, None, None]
    scale = 1.0 / math.sqrt(d)
    kpos_blk = jnp.arange(MOBA_BLOCK)

    def chunk(args):
        qch, t0 = args
        cur = t0 // MOBA_BLOCK
        gate = jnp.einsum('bhqd,bhnd->bhqn', qch.astype(jnp.float32), kmean)
        gate = jnp.where(jnp.arange(nblk) < cur, gate, -jnp.inf)
        _, sel = lax.top_k(gate, n_sel)
        kg = kb[b_ix, h_ix, sel]
        vg = vb[b_ix, h_ix, sel]
        k_own = lax.dynamic_slice_in_dim(kp, cur * MOBA_BLOCK, MOBA_BLOCK, axis=2)
        v_own = lax.dynamic_slice_in_dim(vp, cur * MOBA_BLOCK, MOBA_BLOCK, axis=2)
        s_sel = jnp.einsum('bhqd,bhqnkd->bhqnk', qch, kg).astype(jnp.float32) * scale
        s_sel = jnp.where((jnp.arange(n_sel) < cur)[:, None], s_sel, -jnp.inf)
        s_own = jnp.einsum('bhqd,bhkd->bhqk', qch, k_own).astype(jnp.float32) * scale
        qpos = t0 + jnp.arange(Q_BLOCK)
        s_own = jnp.where(cur * MOBA_BLOCK + kpos_blk[None, :] <= qpos[:, None], s_own, -jnp.inf)
        n_sk = n_sel * MOBA_BLOCK
        p = jax.nn.softmax(jnp.concatenate([s_sel.reshape(b, h, Q_BLOCK, n_sk), s_own], axis=-1), axis=-1)
        p_sel = p[..., :n_sk].reshape(b, h, Q_BLOCK, n_sel, MOBA_BLOCK).astype(v.dtype)
        p_own = p[..., n_sk:].astype(v.dtype)
        return (jnp.einsum('bhqnk,bhqnkd->bhqd', p_sel, vg)
                + jnp.einsum('bhqk,bhkd->bhqd', p_own, v_own))

    out = lax.map(chunk, (qc, starts))
    return out.transpose(1, 2, 0, 3, 4).reshape(b, h, s, d)

def _diff_attention(q, k, v, lam, subln_g, lambda_init):
    s = k.shape[-2]
    scale = 1.0 / math.sqrt(q.shape[-1])
    lf = lam.astype(jnp.float32)
    lam_val = jnp.exp(jnp.sum(lf[0] * lf[1])) - jnp.exp(jnp.sum(lf[2] * lf[3])) + lambda_init
    outs = []
    for t0 in range(0, s, Q_BLOCK):
        kl = t0 + Q_BLOCK
        sc = jnp.einsum('bhiqd,bhikd->bhiqk', q[:, :, :, t0:kl], k[:, :, :, :kl]).astype(jnp.float32) * scale
        causal = jnp.arange(kl)[None, :] <= (t0 + jnp.arange(Q_BLOCK))[:, None]
        p = jax.nn.softmax(jnp.where(causal, sc, -jnp.inf), axis=-1)
        a = p[:, :, 0] - lam_val * p[:, :, 1]
        outs.append(jnp.einsum('bhqk,bhkd->bhqd', a.astype(v.dtype), v[:, :, :kl]))
    o = _rmsnorm(jnp.concatenate(outs, axis=2), subln_g)
    return (o.astype(jnp.float32) * (1.0 - lambda_init)).astype(v.dtype)

def _stick_breaking(q, k, v):
    b, h, s, d = q.shape
    scale = 1.0 / math.sqrt(d)
    ar = jnp.arange(Q_BLOCK)
    tri = (ar[:, None] > ar[None, :]).astype(jnp.float32)
    outs = []
    for i, t0 in enumerate(range(0, s, Q_BLOCK)):
        nc = i + 1
        kl = nc * Q_BLOCK
        z = jnp.einsum('bhqd,bhkd->bhqk', q[:, :, t0:kl], k[:, :, :kl]).astype(jnp.float32) * scale
        before = jnp.arange(kl)[None, :] < (t0 + ar)[:, None]
        ln1m = jnp.where(before, jax.nn.log_sigmoid(-z), 0.0)
        ln1m_c = ln1m.reshape(b, h, Q_BLOCK, nc, Q_BLOCK)
        tri_c = (jnp.arange(nc)[:, None] > jnp.arange(nc)[None, :]).astype(jnp.float32)
        tail = (jnp.einsum('bhqcj,js->bhqcs', ln1m_c, tri)
                + jnp.einsum('bhqe,ec->bhqc', jnp.sum(ln1m_c, axis=-1), tri_c)[..., None])
        log_a = jnp.where(before, z + ln1m + tail.reshape(b, h, Q_BLOCK, kl), -jnp.inf)
        outs.append(jnp.einsum('bhqk,bhkd->bhqd', jnp.exp(log_a).astype(v.dtype), v[:, :, :kl]))
    return jnp.concatenate(outs, axis=2)

def second_inputs(seed: int = 0) -> dict:
    key = jax.random.key(seed)
    ks = jax.random.split(key, 8)
    x = jax.random.normal(ks[0], (BATCH, SEQ, D_MODEL), jnp.float32)
    norm_g = 1.0 + 0.02 * jax.random.normal(ks[1], (DEPTH_2, D_MODEL), jnp.float32)
    w_in = jax.random.normal(ks[2], (DEPTH_2, D_MODEL, N_IN_PARTS * BRANCH_W), jnp.float32) * D_MODEL ** -0.5
    w_out = jax.random.normal(ks[3], (DEPTH_2, MIX_WIDTH, D_MODEL), jnp.float32) * MIX_WIDTH ** -0.5
    diff_lam = 0.1 * jax.random.normal(ks[4], (N_ODD, 4, DIFF_HEAD_DIM), jnp.float32)
    diff_subln_g = 1.0 + 0.02 * jax.random.normal(ks[5], (N_ODD, HEAD_DIM), jnp.float32)
    final_norm_g = 1.0 + 0.02 * jax.random.normal(ks[6], (D_MODEL,), jnp.float32)
    return {"x": x, "norm_g": norm_g, "w_in": w_in, "w_out": w_out,
            "diff_lam": diff_lam, "diff_subln_g": diff_subln_g,
            "final_norm_g": final_norm_g}

def second_block(x, norm_g, w_in, w_out, diff_lam, diff_subln_g, final_norm_g):
    b, s, _ = x.shape
    pos = jnp.arange(s)
    for layer in range(DEPTH_2):
        h = _rmsnorm(x, norm_g[layer])
        proj = jnp.einsum('bsd,de->bse', h, w_in[layer])
        parts = jnp.split(proj, N_IN_PARTS, axis=-1)
        if layer % 2 == 0:
            qa, ka, va, ga, qb, kb, vb, gb = parts
            oa = _dilated_mixture(_rope(_heads(qa), pos), _rope(_heads(ka), pos), _heads(va))
            ob = _moba(_rope(_heads(qb), pos), _rope(_heads(kb), pos), _heads(vb))
            y = jnp.concatenate([_merge(oa) * jax.nn.silu(ga),
                                 _merge(ob) * jax.nn.silu(gb)], axis=-1)
        else:
            qc, kc, vc, gc, qd, kd, vd, gd = parts
            li = layer // 2
            lambda_init = 0.8 - 0.6 * math.exp(-0.3 * layer)
            split2 = lambda t: t.reshape(b, s, N_HEADS, 2, DIFF_HEAD_DIM).transpose(0, 2, 3, 1, 4)
            oc = _diff_attention(_rope(split2(qc), pos), _rope(split2(kc), pos), _heads(vc),
                                 diff_lam[li], diff_subln_g[li], lambda_init)
            od = _stick_breaking(_heads(qd), _heads(kd), _heads(vd))
            y = jnp.concatenate([_merge(oc) * jax.nn.silu(gc),
                                 _merge(od) * jax.nn.silu(gd)], axis=-1)
        x = x + jnp.einsum('bse,ed->bsd', y.astype(x.dtype), w_out[layer])
    return _rmsnorm(x, final_norm_g)


def setup_inputs(seed=0):
    out = dict(first_inputs(seed))
    for name, value in second_inputs(seed + 1).items():
        if name != "x":
            out[name + "_2"] = value
    return out


def reference(
    x, rel_bias, attn_norm, ffn_norm, w_in, gla_w_gk, gla_b_gk, gla_out_norm, lru_conv_w,
    lru_conv_b, lru_w_a, lru_b_a, lru_w_i, lru_b_i, lru_lambda, nsa_cmp_pos, nsa_cmp_k1,
    nsa_cmp_k2, nsa_cmp_v1, nsa_cmp_v2, nsa_q_norm, nsa_k_norm, rwkv_mu, rwkv_w0, rwkv_w_lora,
    rwkv_a0, rwkv_a_lora, rwkv_g_lora, rwkv_k_k, rwkv_k_a, rwkv_r_k, rwkv_ln_w, rwkv_ln_b,
    w_branch, w_out, ffn_up, ffn_conv_w, ffn_conv_b, ffn_down, norm_g_2, w_in_2, w_out_2,
    diff_lam_2, diff_subln_g_2, final_norm_g_2,
):
    x = first_block(
        x, rel_bias, attn_norm, ffn_norm, w_in, gla_w_gk, gla_b_gk, gla_out_norm, lru_conv_w,
        lru_conv_b, lru_w_a, lru_b_a, lru_w_i, lru_b_i, lru_lambda, nsa_cmp_pos, nsa_cmp_k1,
        nsa_cmp_k2, nsa_cmp_v1, nsa_cmp_v2, nsa_q_norm, nsa_k_norm, rwkv_mu, rwkv_w0,
        rwkv_w_lora, rwkv_a0, rwkv_a_lora, rwkv_g_lora, rwkv_k_k, rwkv_k_a, rwkv_r_k, rwkv_ln_w,
        rwkv_ln_b, w_branch, w_out, ffn_up, ffn_conv_w, ffn_conv_b, ffn_down,
    )
    return second_block(
        x, norm_g_2, w_in_2, w_out_2, diff_lam_2, diff_subln_g_2, final_norm_g_2,
    )


_drawn_inputs = setup_inputs


def setup_inputs(seed=0):
    import zlib

    import numpy as np

    out = dict(_drawn_inputs(seed))
    spreads = {}
    factors = {'gla_out_norm': 4.087,
     'lru_b_a': 8.0,
     'lru_b_i': 8.0,
     'nsa_cmp_pos': 3.434,
     'nsa_q_norm': 8.0,
     'nsa_k_norm': 8.0,
     'rwkv_k_k': 8.0,
     'rwkv_k_a': 3.949,
     'rwkv_ln_w': 4.517,
     'rwkv_ln_b': 8.0,
     'ffn_conv_b': 4.5,
     'norm_g_2': 4.515,
     'diff_lam_2': 4.853,
     'diff_subln_g_2': 31.97,
     'final_norm_g_2': 8.094}
    for name, (base, spread) in spreads.items():
        noise = np.random.default_rng([zlib.crc32(name.encode()), seed]).standard_normal(out[name].shape)
        drawn = base * np.exp(spread * noise) if base else spread * noise
        out[name] = __import__('jax').numpy.asarray(drawn.astype(out[name].dtype))
    for name, factor in factors.items():
        out[name] = (out[name] * factor).astype(out[name].dtype)
    return out
```

```python
import math
from contextlib import ExitStack

import numpy as np

import concourse.bass as bass
from concourse import mybir

F32 = mybir.dt.float32
ALU = mybir.AluOpType
ACT = mybir.ActivationFunctionType
AX = mybir.AxisListType

P = 128
S = 256
D = 2048
KT = D // P
FF = 5632
FB = FF // P
DOWN_K = 11
DOWN_SLABS = FB // DOWN_K
RING = 4
SLAB = KT * P
NEG = -1.0e9
PRE = 1280
EPS = 1e-6
KAPPA = -math.exp(-0.5)
LAMBDA_INIT = 0.8 - 0.6 * math.exp(-0.3)

B_MISC, B_KV, B_Q, B_LX, B_LG = 0, 1, 7, 11, 15
B_GQ, B_GK, B_GV, B_GG = 19, 21, 23, 27
B_R, B_K, B_V, B_XW, B_XA, B_XG = 31, 35, 39, 43, 44, 45
N_MIX = 47
N_GATES = 64
GATE_ROW = 32

G_IN_A = 0
G_CMP = 12
G_IN_B = 16
G_GATES = G_IN_B + N_MIX - 12
G_BRANCH = G_GATES + N_GATES
G_OUT = G_BRANCH + KT
G_UP = G_OUT + KT
G_DOWN = G_UP + 2 * FB
G_IN2 = [G_DOWN + KT * DOWN_SLABS, G_DOWN + KT * DOWN_SLABS + KT + 4]
G_OUT2 = [G_IN2[0] + KT, G_IN2[1] + KT]
G_END = G_OUT2[1] + 4

COLS = {}


def _columns():
    at = 0
    for name, n in (("attn_norm", 16), ("ffn_norm", 16), ("norm2_0", 16), ("norm2_1", 16), ("final", 16),
                    ("gk_b", 2), ("gla_gain", 1), ("conv_w", 16), ("conv_b", 4), ("b_a", 4), ("b_i", 4),
                    ("lam", 4), ("q_gain", 1), ("k_gain", 1), ("mu", 16), ("w0", 4), ("a0", 4), ("k_k", 4),
                    ("k_a", 4), ("r_k", 4), ("ln_w", 4), ("ln_b", 4), ("fconv_w", 6 * FB), ("fconv_b", 2 * FB),
                    ("dlam", 128), ("subln", 1), ("pos", 32)):
        COLS[name] = (at, n)
        at += n
    return at


N_COLS = _columns()

SMALL = {"w_gk": (0, 256), "lru_a": (256, 512), "lru_i": (768, 512), "w_lora": (1280, 512),
         "a_lora": (1792, 512), "g_lora": (2304, 1024), "cmp_k2": (3328, 128), "cmp_v2": (3456, 128),
         "rel": (3584, 4)}
N_SMALL = 3588

C_ID, C_ONES, C_BLK, C_STRICT, C_INCL, C_LEVEL, C_RESET = 0, 128, 256, 384, 512, 640, 1408
N_CONST1 = 1664
C2_R64, C2_R32, C2_COS64, C2_SIN64, C2_COS32, C2_SIN32 = 0, 128, 256, 512, 768, 1024
C2_CAUSAL, C2_DIL, C2_STRICT, C2_BEFORE = 1280, 1536, 1792, 2048
N_CONST2 = 2304


def build(nc, xT, cols, small, const1, const2, bucket, flip, w_mix, w_cmp, w_gate, w_branch, w_out, w_up, w_down,
          w_in2, w_out2, bias_scratch, out):
    ctx = ExitStack()
    with ctx:
        def sb(name, shape):
            return ctx.enter_context(nc.sbuf_tensor(name, shape, F32))

        signals = {}

        def sig(name):
            if name not in signals:
                signals[name] = ctx.enter_context(nc.semaphore(name))
            return signals[name]

        ring = sb("ring", [P, RING, KT, P])
        x_sb = sb("x_sb", [P, KT, S])
        h_sb = sb("h_sb", [P, KT, S])
        y_sb = sb("y_sb", [P, KT, S])
        c1 = sb("c1", [P, N_CONST1])
        cv = sb("cv", [P, N_COLS])
        G = sb("G", [P, 16384])
        W = sb("W", [P, PRE + 256 * N_MIX])
        rs = sb("rs", [P, S])
        sq_sum = sb("sq_sum", [P, S])
        tiny = sb("tiny", [P, 96])
        stream = ctx.enter_context(nc.psum_tensor("stream", [P, 2, 512], F32))
        M = ctx.enter_context(nc.psum_tensor("M", [P, 6, 512], F32))

        ident = c1[:, C_ID:C_ID + P]
        ones = c1[:, C_ONES:C_ONES + P]
        blk64 = c1[:, C_BLK:C_BLK + P]
        strict_incl = c1[:, C_STRICT:C_STRICT + 256]
        incl = c1[:, C_INCL:C_INCL + P]
        reset = c1[:, C_RESET:C_RESET + S]

        def level(n):
            return c1[:, C_LEVEL + P * n:C_LEVEL + P * (n + 1)]

        def col(name, i=0, n=1):
            a = COLS[name][0] + i
            return cv[:, a:a + n]

        def spread(ap, n):
            return ap.unsqueeze(2).to_broadcast([P, ap.shape[1], n])

        def over(ap, n):
            return ap.unsqueeze(1).to_broadcast([P, n, ap.shape[1]])

        def blocks(b, n=1):
            return W[:, PRE + 256 * b:PRE + 256 * (b + n)]

        def g_at(a, n):
            return G[:, a:a + n]

        def w_at(a, n):
            return W[:, a:a + n]

        def bank(a, n=1):
            return M[:, a:a + n, :].rearrange("p a b -> p (a b)")

        sm0 = 12796

        def small_w(name, a=0, n=None):
            o, w = SMALL[name]
            return G[:, sm0 + o + a:sm0 + o + (a + n if n is not None else w)]

        n_bias = g_at(0, 1024).rearrange("p (h s) -> p h s", h=4)
        n_vtok = g_at(1024, 512).rearrange("p (a t d) -> p a t d", a=2, t=2)
        n_prob = g_at(1536, 2048)
        n_probT = g_at(3584, 2048)
        n_sq, n_rs = g_at(1536, 1536), g_at(3584, 1536)
        n_hot, n_ext = g_at(5120, 1024), g_at(6144, 512)
        n_blk = g_at(5632 + 1536 + 4096, 960)
        n_pcT = g_at(5632, 1024)
        n_vc, n_hk, n_hv, n_kc, n_kc2 = (g_at(6656, 128), g_at(6784, 16), g_at(6800, 16), g_at(6816, 16),
                                         g_at(6832, 16))
        n_gate = g_at(6848, 24)
        n_pc = g_at(6872, 64)
        n_nmax, n_sum, n_wt = g_at(6936, 12), g_at(6948, 12), g_at(6960, 12)
        n_flip, n_skew = g_at(12224, P), g_at(7168, 1024)
        l_xc, l_a, l_u, l_t = g_at(7168, 1024), g_at(8192, 1024), g_at(9216, 1024), g_at(10240, 1024)
        a_b, a_e1, a_e2, a_eb = g_at(0, 512), g_at(512, 512), g_at(1024, 512), g_at(1536, 512)
        a_qs, a_ks, a_qi, a_kl = g_at(2048, 512), g_at(2560, 512), g_at(3072, 512), g_at(3584, 512)
        a_kltok = g_at(4096, 512).rearrange("p (r f) -> p r f", r=2)
        a_vtok = g_at(4608, 1024).rearrange("p (r h v) -> p r h v", r=2, h=4)
        a_sc = g_at(5632, 1024).rearrange("p (h r t) -> p h r t", h=4, r=2)
        a_st = g_at(6656, 768).rearrange("p (j c v) -> p j c v", j=2, c=3)
        a_o, a_sq = g_at(512, 1024), g_at(1536, 1024)
        a_bm = g_at(7424, 512)
        r_sig, r_a, r_g, r_kk = w_at(0, 1024), w_at(1024, 1024), w_at(2048, 1024), w_at(3072, 1024)
        r_qr = w_at(4096, 2048).rearrange("p (j r q t) -> p j r q t", j=4, r=2, q=2)
        r_p, r_kt, r_bonus = w_at(6144, 1024), w_at(7168, 1024), w_at(8192, 1024)
        r_rhs = blocks(B_XG, 2)
        r_shift = g_at(8192, 4096)
        r_cs = blocks(B_XG - 2, 4)
        r_ar = g_at(8192, 2048).rearrange("p (h t) -> p h t", h=8)
        r_bk = g_at(10240, 2048).rearrange("p (h t) -> p h t", h=8)
        r_x, r_xt, r_t1 = g_at(12796, 1024), g_at(13820, 1024), g_at(14844, 1024)
        r_stc = [blocks(b).rearrange("p (j i) -> p j i", j=4) for b in (B_XW, B_XA)]
        r_dec = g_at(16124, 16).rearrange("p (j c) -> p j c", j=4)
        r_mt = r_kk

        def hm(hd):
            return 4 * (hd % 2) + hd // 2

        r_vtok, r_ptok = w_at(1024, 512), w_at(1536, 512)
        r_ktok = blocks(B_R, 2)
        r_u = blocks(B_R + 2, 2)
        r_y = blocks(B_K, 4)
        r_tmp = w_at(0, 1024)

        def c2(a, n):
            return W[:, PRE + 8192 + a:PRE + 8192 + a + n]

        def p_blocks(b, n=1):
            return G[:, S * b:S * (b + n)]

        p_probs = [g_at(4096, 1024), g_at(5120, 2048)]
        p_probT, p_vtok, p_y = g_at(7168, 1536), g_at(8704, 512), g_at(9216, 1024)
        p_o, p_sq, p_tmp = g_at(11264, 1024), g_at(12288, 512), g_at(12800, 3072)
        p_stat = g_at(10240, 96)

        def prob(t):
            return two_tiles(g_at(4096, 1536), t)

        def prob_maps(maps, t):
            return p_probs[t].rearrange("p (m s) -> p m s", m=8) if maps == 8 else prob(t)

        def logit_banks(rows, t):
            if rows == 4:
                return [M[:, 0, :], M[:, 1, :], stream[:, 0, :], stream[:, 1, :]] if t == 0 else \
                    [M[:, 2 + i, :] for i in range(4)]
            return [M[:, 1, :], M[:, 3, :]] if t == 0 else [M[:, 4, :], M[:, 5, :]]

        def am(hd):
            return 2 * (hd % 2) + hd // 2

        p_stick = w_at(4096, 1536)

        def two_tiles(ap, t):
            return ap[:, 512 * t:512 + 1024 * t].rearrange("p (m s) -> p m s", m=4)

        def stick_z(t):
            return two_tiles(g_at(4096, 1536), t)

        def stick_s(t):
            return two_tiles(p_tmp[:, 0:1536], t)

        def stick_r(t):
            return two_tiles(p_stick, t)

        def diff_tmp(t):
            return two_tiles(p_tmp[:, 0:1536], t)

        ones_row = w_at(6144, 256)
        merge_tmp = w_at(2048, 1024).rearrange("p (b t) -> p b t", b=4)
        ffn_buf = w_at(0, 1024).rearrange("p (u v t) -> p u v t", u=2, v=2)
        up_bank = [stream[:, 0, 0:S], stream[:, 1, 0:S], M[:, 2, 0:S], M[:, 3, 0:S]]
        r_y2, r_ssum = g_at(8192, 1024), w_at(0, 256).rearrange("p (j i) -> p j i", j=4)
        written = {}

        def nth(name):
            written[name] = written.get(name, 0) + 1
            return written[name]

        def fill(g, it=0):
            return 16 * (g // RING + 1) + 16 * it

        def slot_in(g):
            return sig(f"slab_in_slot{g % RING}")

        block = ctx.enter_context(nc.Block())

        @block.sync
        def _(sp):
            sp.dma_start(x_sb[:], xT).then_inc(sig("x_in"), 16)
            sp.dma_start(cv[:], cols).then_inc(sig("cols_in"), 16)
            sp.dma_start(c1[:], const1).then_inc(sig("const1_in"), 16)

            def load(g, src, it=0, free=0, n=KT):
                if free or g >= RING:
                    sp.wait_ge(sig("slab_done"), g - RING + 1 + RING * it)
                sp.dma_start(ring[:, g % RING, 0:n, :], src).then_inc(slot_in(g), 16)

            def load_run(g0, dram, first, groups, n=KT):
                with sp.Fori(0, groups) as it:
                    for u in range(RING):
                        src = dram[first + u + RING * it]
                        load(g0 + u, src, it, 1, n)

            for b in range(RING):
                load(G_IN_A + b, w_mix[b])
            sp.dma_start(G[:, sm0:sm0 + N_SMALL], small).then_inc(sig("small_in"), 16)
            load_run(G_IN_A + RING, w_mix, RING, 2)
            load_run(G_CMP, w_cmp, 0, 1)
            load_run(G_IN_B, w_mix, 12, 8)
            for b in range(44, N_MIX):
                load(G_IN_B + b - 12, w_mix[b])
            load_run(G_GATES, w_gate, 0, N_GATES // RING)
            load_run(G_BRANCH, w_branch, 0, KT // RING)
            load_run(G_OUT, w_out, 0, KT // RING)
            load_run(G_UP, w_up, 0, 2 * FB // RING)
            load_run(G_DOWN, w_down, 0, KT * DOWN_SLABS // RING, DOWN_K)
            for layer in range(2):
                load_run(G_IN2[layer], w_in2, KT * layer, KT // RING)
                load_run(G_OUT2[layer], w_out2, 4 * layer, 1)
            for q in range(4):
                sp.wait_ge(sig("h_ready"), KT * 4 + 4 * (q + 1))
                sp.dma_start(out[:, 4 * q:4 * q + 4, :], h_sb[:, 4 * q:4 * q + 4, :]).then_inc(sig("out_done"), 16)
            sp.wait_ge(sig("out_done"), 64)

        @block.gpsimd
        def _(pool):
            pool.dma_start(n_hot[0:32, :], bucket).then_inc(sig("bucket_in"), 16)
            pool.dma_start(n_flip, flip).then_inc(sig("flip_in"), 16)
            pool.wait_ge(sig("bias_row"), 1)
            pool.dma_start(bias_scratch, n_ext[0:4, :]).then_inc(sig("bias_out"), 16)
            pool.wait_ge(sig("bias_out"), 16)
            skewed = bass.AP(bias_scratch.tensor, 0, [[1, P], [512, 4], [1, S]])
            pool.dma_start(n_skew.rearrange("p (h s) -> p h s", h=4), skewed).then_inc(sig("bias_in"), 16)
            pool.wait_ge(sig("rwkv_y"), 1)
            pool.dma_start(c2(0, N_CONST2), const2).then_inc(sig("const2_in"), 16)

            done = [0]
            pool_sq = W[:, PRE + 7936:PRE + 8192]

            def squares(first, n):
                pool.wait_ge(sig("norm_sum"), first // KT + 1)

                def one(u, it):
                    pool.wait_ge(sig("res_add"), 2 + first + u + 1 + it)
                    xb = x_sb[:, u + it, :]
                    if u == 0:
                        nc.gpsimd.tensor_tensor(sq_sum[:, :], xb, xb, ALU.mult).then_inc(sig("pool_sq"), 1)
                        return
                    pool.wait_ge(sig("pool_sq"), done[0] + 1 + 2 * (u - 1) + 2 * it)
                    nc.gpsimd.tensor_tensor(pool_sq[:, :], xb, xb, ALU.mult).then_inc(sig("pool_sq"), 1)
                    pool.wait_ge(sig("pool_sq"), done[0] + 2 + 2 * (u - 1) + 2 * it)
                    nc.gpsimd.tensor_tensor(sq_sum[:, :], sq_sum[:, :], pool_sq[:, :], ALU.add) \
                        .then_inc(sig("pool_sq"), 1)
                one(0, 0)
                with pool.Fori(0, n - 1) as it:
                    one(1, it)
                done[0] += 2 * n - 1

            for n in range(4):
                squares(KT * n, KT)

        @block.tensor
        def _(pe):
            mm = nc.tensor.matmul

            def block_sum(dst, src, w):
                n = src.shape[1]
                for a in range(0, n, 512):
                    last = mm(dst[:, a:min(a + 512, n)], w, src[:, a:min(a + 512, n)], start=True, stop=True)
                return last

            def norm_sum(k):
                if k == 0:
                    pe.wait_ge(sig("x_sq"), 1)
                else:
                    pe.wait_ge(sig("pool_sq"), (2 * KT - 1) * k)
                mm(M[:, 0, 0:S], ones, sq_sum[:, :], start=True, stop=True).then_inc(sig("norm_sum"), 1)

            def slab(g, out_ap, rhs, it=0, n=KT, start=True, stop=True, ready=None):
                pe.wait_ge(slot_in(g), fill(g, it))
                for k in range(n):
                    if ready is not None:
                        pe.wait_ge(sig(ready[0]), ready[1] + k + 1)
                    last = mm(out_ap, ring[:, g % RING, k, :], rhs(k), start=start and k == 0,
                              stop=stop and k == n - 1)
                last.then_inc(sig("slab_done"), 1)

            def h(k):
                return h_sb[:, k, :]

            def project(g0, e0, groups, norm=None):
                def one(u, it):
                    if e0 + u >= 2:
                        pe.wait_ge(sig("block_out"), e0 + u - 1 + RING * it)
                    slab(g0 + u, stream[:, (e0 + u) % 2, 0:S], h, it,
                         ready=norm if isinstance(it, int) and u == 0 else None)
                if groups == 1:
                    for u in range(RING):
                        one(u, 0)
                else:
                    with pe.Fori(0, groups) as it:
                        for u in range(RING):
                            one(u, it)

            def nsa_compress():
                pe.wait_ge(sig("cmp_in"), 4)
                for a in range(2):
                    x = n_blk[:, 480 * a:480 * (a + 1)].rearrange("p (l n) -> p l n", n=15)
                    for half in range(2):
                        slab(G_CMP + 2 * a + half, M[:, a, 0:15], lambda k: x[:, 16 * half + k, :],
                             start=half == 0, stop=half == 1)

            def nsa_norms():
                pe.wait_ge(sig("nsa_sq"), 3)
                block_sum(bank(2, 3), n_sq, ones).then_inc(sig("nsa_ssq"), 1)
                for a in range(2):
                    v = blocks(B_KV + 3 + 2 * a)
                    for t in range(2):
                        last = nc.tensor.transpose(M[:, 5, 256 * a + 128 * t:256 * a + 128 * (t + 1)],
                                                   v[:, 128 * t:128 * (t + 1)], ident)
                last.then_inc(sig("nsa_vT"), 1)

            def nsa_small():
                pe.wait_ge(sig("cmp_hidden"), 2)
                pe.wait_ge(sig("nsa_rs"), 1)
                pe.wait_ge(sig("small_in"), 16)
                mm(M[:, 0, 0:15], small_w("cmp_k2"), n_hk[:, 0:15], start=True, stop=True)
                mm(M[0:15, 1, 0:P], n_hv[:, 0:15], small_w("cmp_v2"), start=True, stop=True)
                pe.wait_ge(sig("bucket_in"), 16)
                mm(M[0:4, 2, :], small_w("rel")[0:32, :], n_hot[0:32, 0:512], start=True, stop=True)
                for t in range(2):
                    last = nc.tensor.transpose(M[:, 3, 128 * t:128 * (t + 1)],
                                               blocks(B_MISC)[:, 128 * t:128 * (t + 1)], ident)
                last.then_inc(sig("nsa_small"), 1)
                pe.wait_ge(sig("kc_sq"), 1)
                mm(M[:, 4, 0:15], ones, n_kc2[:, 0:15], start=True, stop=True).then_inc(sig("kc_ssq"), 1)

            def nsa_bias():
                pe.wait_ge(sig("bias_in"), 16)
                pe.wait_ge(sig("flip_in"), 16)
                pe.wait_ge(sig("nsa_vtok"), 1)
                mm(M[:, 5, :], n_flip, n_skew[:, 0:512], start=True, stop=True)
                mm(M[:, 3, :], n_flip, n_skew[:, 512:1024], start=True, stop=True).then_inc(sig("nsa_skew"), 1)

            def nsa_scores(t):
                w = P * (t + 1)
                pe.wait_ge(sig("nsa_qk"), 4)
                pe.wait_ge(sig("nsa_bias"), 1)
                if t == 1:
                    pe.wait_ge(sig("nsa_PT"), 1), pe.wait_ge(sig("nsa_PT_dve"), 1)
                for a in range(2):
                    k = blocks(B_KV + 2 + 2 * a)
                    o = bank(2 * a, 2).rearrange("p (h s) -> p h s", h=4)
                    for hd in range(4):
                        mm(o[:, hd, 0:w], blocks(B_Q + hd)[:, P * t:P * (t + 1)], k[:, 0:w],
                           start=True, stop=True)
                for hd in range(4):
                    last = mm(M[:, 4, 16 * hd:16 * hd + 15], blocks(B_Q + hd)[:, P * t:P * (t + 1)],
                              n_kc[:, 0:15], start=True, stop=True)
                last.then_inc(sig("nsa_logits"), 1)

            def nsa_turn(t):
                pe.wait_ge(sig("nsa_weighted"), t + 1)
                pr = n_prob.rearrange("p (a h s) -> p a h s", a=2, h=4)
                n = 0
                for a in range(2):
                    for hd in range(4):
                        for st in range(t + 1):
                            nc.tensor.transpose(bank(0, 4)[:, P * n:P * (n + 1)],
                                                pr[:, a, hd, P * st:P * (st + 1)], ident)
                            n += 1
                for hd in range(4):
                    last = nc.tensor.transpose(M[0:16, 4, P * hd:P * (hd + 1)], n_pc[:, 16 * hd:16 * hd + 16],
                                               ident)
                last.then_inc(sig("nsa_turned"), 1)

            def nsa_values(t):
                pe.wait_ge(sig("nsa_PT"), t + 1)
                pe.wait_ge(sig("nsa_PT_dve"), t + 1)
                if t == 1:
                    pe.wait_ge(sig("nsa_y"), 1)
                if t == 0:
                    pe.wait_ge(sig("nsa_vtok"), 1)
                for hd in range(4):
                    o = M[:, 5, P * hd:P * (hd + 1)]
                    mm(o, n_vc[0:15, :], n_pcT[0:15, P * hd:P * (hd + 1)], start=True, stop=False)
                    for a in range(2):
                        for st in range(t + 1):
                            n = (a * 4 + hd) * (t + 1) + st
                            last = mm(o, n_vtok[:, a, st, :], n_probT[:, P * n:P * (n + 1)], start=False,
                                      stop=a == 1 and st == t)
                last.then_inc(sig("nsa_o"), 1)

            def lru_gates():
                pe.wait_ge(sig("lru_conv"), 12)
                pe.wait_ge(sig("nsa_y"), 2)
                for j in range(4):
                    mm(bank(0, 2)[:, S * j:S * (j + 1)], small_w("lru_a", P * j, P), l_xc[:, S * j:S * (j + 1)],
                       start=True, stop=True)
                for j in range(4):
                    last = mm(bank(2, 2)[:, S * j:S * (j + 1)], small_w("lru_i", P * j, P),
                              l_xc[:, S * j:S * (j + 1)], start=True, stop=True)
                last.then_inc(sig("lru_pre"), 1)

            def gla_decay():
                pe.wait_ge(sig("lru_gated"), 2)
                for j in range(2):
                    last = mm(M[:, 0, S * j:S * (j + 1)], small_w("w_gk", P * j, P)[0:16, :],
                              blocks(B_MISC)[0:16, :], start=True, stop=True)
                last.then_inc(sig("gla_z"), 1)
                pe.wait_ge(sig("block_out"), B_GV + 4)
                for hd in range(4):
                    for r in range(2):
                        last = nc.tensor.transpose(bank(2, 2)[:, 512 * r + P * hd:512 * r + P * (hd + 1)],
                                                   blocks(B_GV + hd)[:, P * r:P * (r + 1)], ident)
                last.then_inc(sig("gla_vT"), 1)

            def gla_scores():
                pe.wait_ge(sig("gla_qk"), 4)
                for hd in range(4):
                    lo, j = 64 * (hd % 2), hd // 2
                    for r in range(2):
                        c = S * j + P * r
                        last = mm(M[:, hd % 2, (2 * j + r) * P:(2 * j + r + 1) * P], a_ks[lo:lo + 64, c:c + P],
                                  a_qs[lo:lo + 64, c:c + P], start=True, stop=True)
                last.then_inc(sig("gla_sc"), 1)
                for j in range(2):
                    for r in range(2):
                        last = nc.tensor.transpose(M[:, 4, S * r + P * j:S * r + P * (j + 1)],
                                                   a_kl[:, S * j + P * r:S * j + P * (r + 1)], ident)
                last.then_inc(sig("gla_klT"), 1)

            def gla_states():
                pe.wait_ge(sig("gla_kltok"), 1)
                pe.wait_ge(sig("gla_vtok"), 1)
                for hd in range(4):
                    lo, j = 64 * (hd % 2), hd // 2
                    for c in range(3):
                        cb, r = 64 * (c % 2), c // 2
                        last = mm(M[lo:lo + 64, 4 + c % 2, S * j + P * r:S * j + P * (r + 1)],
                                  a_kltok[cb:cb + 64, r, 64 * hd:64 * hd + 64], a_vtok[cb:cb + 64, r, hd, :],
                                  start=True, stop=True)
                last.then_inc(sig("gla_dS"), 1)

            def gla_out():
                pe.wait_ge(sig("gla_masked"), 1)
                pe.wait_ge(sig("gla_S"), 1)
                for hd in range(4):
                    lo, j = 64 * (hd % 2), hd // 2
                    for r in range(2):
                        o = M[:, hd % 2, S * j + P * r:S * j + P * (r + 1)]
                        mm(o, a_vtok[:, r, hd, :], a_sc[:, 2 * (hd % 2) + j, r, :], start=True, stop=False)
                        for c in (2 * r, 2 * r + 1):
                            if c:
                                last = mm(o[:, 64 * (c % 2):64 * (c % 2) + 64], a_st[lo:lo + 64, j, c - 1, :],
                                          a_qi[lo:lo + 64, S * j + 64 * c:S * j + 64 * (c + 1)],
                                          start=False, stop=c == 2 * r + 1)
                last.then_inc(sig("gla_o"), 1)
                pe.wait_ge(sig("gla_osq"), 1)
                block_sum(bank(2, 2), a_sq, ones).then_inc(sig("gla_ssq"), 1)

            def rwkv_lora():
                pe.wait_ge(sig("gla_done"), 1)
                pe.wait_ge(sig("rw_act"), 2)
                for j in range(4):
                    mm(bank(0, 2)[:, S * j:S * (j + 1)], small_w("w_lora", P * j, P)[0:96, :],
                       blocks(B_XW)[0:96, :], start=True, stop=True)
                for j in range(4):
                    mm(bank(2, 2)[:, S * j:S * (j + 1)], small_w("a_lora", P * j, P)[0:96, :],
                       blocks(B_XA)[0:96, :], start=True, stop=True)
                for j in range(4):
                    for k in range(2):
                        last = mm(bank(4, 2)[:, S * j:S * (j + 1)], small_w("g_lora", 512 * k + P * j, P),
                                  blocks(B_XG + k), start=k == 0, stop=k == 1)
                last.then_inc(sig("rw_lora"), 1)

            def rwkv_sums():
                pe.wait_ge(sig("rw_sig"), 1)
                pe.wait_ge(sig("rw_kksq"), 1)
                block_sum(bank(0, 2), r_tmp, blk64).then_inc(sig("rw_kkss"), 1)
                pe.wait_ge(sig("rw_rk"), 1)
                block_sum(bank(2, 2), r_bonus, blk64).then_inc(sig("rw_rks"), 1)

            def rwkv_pair(r):
                pe.wait_ge(sig("rw_feat"), 1)
                if r == 1:
                    pe.wait_ge(sig("rw_state"), 2), pe.wait_ge(sig("rw_ycopy"), 2)
                for n, src in enumerate((r_p, r_kt)):
                    if n == 1:
                        pe.wait_ge(sig("rw_ar"), r + 1)
                    for hd in range(8):
                        lo, j = 64 * (hd % 2), hd // 2
                        last = mm(bank(0, 4)[:, S * hm(hd):S * (hm(hd) + 1)], src[lo:lo + 64, S * j + P * r:S * j + P * (r + 1)],
                                  r_qr[lo:lo + 64, j, r, :, :].rearrange("p q t -> p (q t)"),
                                  start=True, stop=True)
                    last.then_inc(sig("rw_scores"), 1)
                for n, src in enumerate((r_p, r_kt, blocks(B_V, 4))):
                    if n == 2:
                        pe.wait_ge(sig("rw_tok"), 3 * r + 1)
                    b = (4, 5, 4)[n]
                    for j in range(4):
                        last = nc.tensor.transpose(M[:, b, P * j:P * (j + 1)], src[:, S * j + P * r:S * j + P * (r + 1)],
                                                   ident)
                    last.then_inc(sig("rw_turned"), 1)

            def rwkv_level(r, n):
                pe.wait_ge(sig("rw_mt"), 6 * r + n + 1)
                if n == 0:
                    pe.wait_ge(sig("rw_bk"), r + 1)
                    pe.wait_ge(sig("rw_tok"), 3 * r + 3)
                else:
                    pe.wait_ge(sig("rw_x"), 5 * r + n)
                for hd in range(8):
                    rhs = ident if n == 0 else r_x[:, P * hd:P * (hd + 1)]
                    last = mm(bank(0, 2)[:, P * hd:P * (hd + 1)], r_mt[:, P * hd:P * (hd + 1)], rhs,
                              start=True, stop=True)
                last.then_inc(sig("rw_t1p"), 1)
                if n == 0:
                    return
                pe.wait_ge(sig("rw_t1"), 5 * r + n)
                if n < 5:
                    for hd in range(8):
                        mm(bank(2, 2)[:, P * hd:P * (hd + 1)], r_xt[:, P * hd:P * (hd + 1)],
                           r_t1[:, P * hd:P * (hd + 1)], start=True, stop=True)
                for hd in range(8):
                    last = mm(bank(4, 2)[:, P * hd:P * (hd + 1)], r_t1[:, P * hd:P * (hd + 1)],
                              r_xt[:, P * hd:P * (hd + 1)], start=True, stop=True)
                last.then_inc(sig("rw_dx"), 1)

            def rwkv_chunk_a(c):
                r, cb = c // 2, 64 * (c % 2)
                if c % 2 == 0:
                    pe.wait_ge(sig("rw_xt"), r + 1)
                else:
                    pe.wait_ge(sig("rw_state"), c), pe.wait_ge(sig("rw_ycopy"), c)
                for hd in range(8):
                    lo, j = 64 * (hd % 2), hd // 2
                    o = M[cb:cb + 64, hd % 2, 64 * j:64 * j + 64]
                    if c:
                        mm(o, r_qr[lo:lo + 64, j, r, 0, cb:cb + 64], r_stc[c % 2][lo:lo + 64, j, :], start=True, stop=False)
                    last = mm(o, r_bk[:, hm(hd), cb:cb + 64], r_vtok[:, 64 * hd:64 * hd + 64],
                              start=c == 0, stop=True)
                last.then_inc(sig("rw_rhsp"), 1)

            def rwkv_chunk_b(c):
                r, cb = c // 2, 64 * (c % 2)
                pe.wait_ge(sig("rw_rhs"), c + 1)
                for hd in range(8):
                    x0 = P * hm(hd) + cb
                    last = mm(M[cb:cb + 64, 4, 64 * hd:64 * hd + 64], r_xt[cb:cb + 64, x0:x0 + 64],
                              r_rhs[cb:cb + 64, 64 * hm(hd):64 * hm(hd) + 64], start=True, stop=True)
                last.then_inc(sig("rw_up"), 1)

            def rwkv_chunk_c(c):
                r, cb = c // 2, 64 * (c % 2)
                pe.wait_ge(sig("rw_u"), c + 1)
                if c < 3:
                    for hd in range(8):
                        lo, j = 64 * (hd % 2), hd // 2
                        o = M[lo:lo + 64, 3, 64 * j:64 * j + 64]
                        mm(o, r_ptok[cb:cb + 64, 64 * hd:64 * hd + 64], r_u[cb:cb + 64, 64 * hd:64 * hd + 64],
                           start=True, stop=False)
                        last = mm(o, r_ktok[cb:cb + 64, 64 * hd:64 * hd + 64], r_vtok[cb:cb + 64, 64 * hd:64 * hd + 64],
                                  start=False, stop=True)
                    last.then_inc(sig("rw_sp"), 1)
                for hd in range(8):
                    lo, j = 64 * (hd % 2), hd // 2
                    o = M[lo:lo + 64, 2, 64 * j:64 * j + 64]
                    mm(o, r_u[:, 64 * hd:64 * hd + 64], r_ar[:, hm(hd), P + cb:P + cb + 64],
                       start=True, stop=False)
                    last = mm(o, r_vtok[:, 64 * hd:64 * hd + 64], r_bk[:, hm(hd), P + cb:P + cb + 64],
                              start=False, stop=c == 0)
                    if c:
                        last = mm(o, r_stc[c % 2][lo:lo + 64, j, :], r_qr[lo:lo + 64, j, r, 1, cb:cb + 64],
                                  start=False, stop=True)
                last.then_inc(sig("rw_yp"), 1)

            def rwkv_norm():
                pe.wait_ge(sig("rw_ycopy"), 4)
                block_sum(bank(0, 2), r_y, blk64).then_inc(sig("rw_mean"), 1)
                pe.wait_ge(sig("rw_ysq"), 1)
                block_sum(bank(2, 2), r_tmp, blk64).then_inc(sig("rw_var"), 1)

            def attention(layer, half):
                t0 = 2 * layer + half
                q, k, v = p_blocks(8 * half, 2), p_blocks(8 * half + 2, 2), p_blocks(8 * half + 4, 2)
                pe.wait_ge(sig("block2_out"), 16 * layer + 8 * half + 6)
                if t0:
                    pe.wait_ge(sig("at_y"), t0)
                if t0 != 3:
                    rot = c2(C2_R64 if layer == 0 else C2_R32, P)
                    if t0 == 0:
                        pe.wait_ge(sig("const2_in"), 16)
                    for a in range(2):
                        last = mm(M[:, a, :], rot, p_blocks(8 * half + 2 * a, 2), start=True, stop=True)
                    last.then_inc(sig("at_rot"), 1)
                for j in range(2):
                    for st in range(2):
                        last = nc.tensor.transpose(M[:, 2, S * st + P * j:S * st + P * (j + 1)],
                                                   v[:, S * j + P * st:S * j + P * (st + 1)], ident)
                last.then_inc(sig("at_vT"), 1)
                pe.wait_ge(sig("at_vtok"), t0 + 1)
                pe.wait_ge(sig("at_qk"), min(t0 + 1, 3))
                rows = 4 if t0 == 2 else 2
                kd = P // rows
                if t0 == 2:
                    pe.wait_ge(sig("block2_out"), 2 * KT)
                for t in range(2):
                    w = P * (t + 1)
                    for i in range(rows):
                        lo = kd * i
                        for j in range(2):
                            last = mm(logit_banks(rows, t)[i][:, w * j:w * (j + 1)],
                                      q[lo:lo + kd, S * j + P * t:S * j + P * (t + 1)],
                                      k[lo:lo + kd, S * j:S * j + w], start=True, stop=True)
                    last.then_inc(sig("at_logits"), 1)
                if t0 == 3:
                    pe.wait_ge(sig("stick_exp"), 1)
                else:
                    pe.wait_ge(sig("at_prob"), t0 + 1)
                for t in range(2):
                    for hd in range(4):
                        for st in range(t + 1):
                            n = 4 * t + hd * (t + 1) + st
                            src = diff_tmp(t) if t0 == 2 else prob(t)
                            last = nc.tensor.transpose(bank(0, 3)[:, P * n:P * (n + 1)],
                                                       src[:, am(hd), P * st:P * (st + 1)], ident)
                last.then_inc(sig("at_turned"), 1)
                pe.wait_ge(sig("at_PT"), t0 + 1)
                for t in range(2):
                    for hd in range(4):
                        lo, j = 64 * (hd % 2), hd // 2
                        o = M[lo:lo + 64, 3, S * j + P * t:S * j + P * (t + 1)]
                        for st in range(t + 1):
                            n = 4 * t + hd * (t + 1) + st
                            last = mm(o, p_vtok[:, S * st + 64 * hd:S * st + 64 * hd + 64],
                                      p_probT[:, P * n:P * (n + 1)], start=st == 0, stop=st == t)
                last.then_inc(sig("at_o"), 1)
                if t0 == 2:
                    pe.wait_ge(sig("at_osq"), 1)
                    block_sum(M[:, 4, :], p_sq, blk64).then_inc(sig("at_oss"), 1)

            pe.wait_ge(sig("const1_in"), 16)
            norm_sum(0)
            project(G_IN_A, 0, 1, ("h_ready", 0))
            project(G_IN_A + 4, 4, 2)
            nsa_compress()
            nsa_norms()
            project(G_IN_B, 12, 1)
            nsa_small()
            project(G_IN_B + 4, 16, 1)
            nsa_bias()
            nsa_scores(0)
            project(G_IN_B + 8, 20, 1)
            nsa_turn(0)
            project(G_IN_B + 12, 24, 1)
            nsa_values(0)
            nsa_scores(1)
            project(G_IN_B + 16, 28, 1)
            nsa_turn(1)
            project(G_IN_B + 20, 32, 1)
            nsa_values(1)
            lru_gates()
            project(G_IN_B + 24, 36, 1)
            gla_decay()
            project(G_IN_B + 28, 40, 1)
            gla_scores()
            gla_states()
            for u in range(3):
                pe.wait_ge(sig("block_out"), 44 + u - 1)
                slab(G_IN_B + 32 + u, stream[:, u % 2, 0:S], h)
            gla_out()

            gates_run = []

            def gates(n):
                e = sum(gates_run)
                project(G_GATES + 4 * e, N_MIX + 4 * e, n)
                gates_run.append(n)

            gates(1)
            rwkv_lora()
            rwkv_sums()
            for r in range(2):
                rwkv_pair(r)
                for n in range(6):
                    rwkv_level(r, n)
                    if n % 3 == 2:
                        gates(1)
                for c in (2 * r, 2 * r + 1):
                    rwkv_chunk_a(c)
                    rwkv_chunk_b(c)
                    rwkv_chunk_c(c)
                    if c < 3:
                        gates(1)
            rwkv_norm()
            gates(N_GATES // 4 - sum(gates_run))

            pe.wait_ge(sig("rwkv_y"), 1)

            def branch(u, it):
                b = 2 * (u % 2)
                g = G_BRANCH + u
                pe.wait_ge(sig("merge_read"), u - 1 + 4 * it + 2)
                pe.wait_ge(slot_in(g), fill(g, it))
                for n in range(4):
                    for k in range(4):
                        last = mm(bank(b, 2)[:, S * n:S * (n + 1)], ring[:, g % RING, 4 * n + k, :],
                                  y_sb[:, 4 * n + k, :], start=k == 0, stop=k == 3)
                last.then_inc(sig("slab_done"), 1)

            with pe.Fori(0, KT // 4) as it:
                for u in range(4):
                    branch(u, it)
            pe.wait_ge(sig("merged"), KT)
            with pe.Fori(0, KT // 4) as it:
                for u in range(4):
                    pe.wait_ge(sig("res_add"), u - 1 + 4 * it + 2)
                    slab(G_OUT + u, stream[:, u % 2, 0:S], h, it)
            norm_sum(1)
            pe.wait_ge(sig("h_ready"), 2 * KT)
            with pe.Fori(0, FB // 2) as it:
                for u in range(4):
                    if u % 2 == 0:
                        pe.wait_ge(sig("up_read"), 2 * it + u // 2 + 1)
                    slab(G_UP + u, up_bank[u], h, it)
            act = G[:, 0:FB * S].rearrange("p (k t) -> p k t", k=FB)
            pe.wait_ge(sig("ffn_act"), FB + 2)
            with pe.Fori(0, KT // 2) as it:
                for u in range(8):
                    n, part = u // 4, u % 4
                    if part == 0:
                        pe.wait_ge(sig("res_add"), KT + 2 + n - 1 + 2 * it)
                    slab(G_DOWN + u, stream[:, n, 0:S], lambda k: act[:, DOWN_K * part + k, :],
                         2 * it, DOWN_K, start=part == 0, stop=part == 3)
            norm_sum(2)
            for layer in range(2):
                pe.wait_ge(sig("h_ready"), (2 + layer) * KT + KT)
                for e in range(KT):
                    if layer or e >= 2:
                        pe.wait_ge(sig("block2_out"), 16 * layer + e - 1)
                    slab(G_IN2[layer] + e, stream[:, e % 2, 0:S], h)
                attention(layer, 0)
                attention(layer, 1)
                pe.wait_ge(sig("at_y"), 2 * layer + 2)
                for s in range(4):
                    g = G_OUT2[layer] + s
                    if s >= 2:
                        pe.wait_ge(sig("res_add"), 2 + 2 * KT + KT * layer + 4 * (s - 1))
                    pe.wait_ge(slot_in(g), fill(g))
                    for n in range(4):
                        for k in range(4):
                            last = mm(bank(2 * (s % 2), 2)[:, S * n:S * (n + 1)], ring[:, g % RING, 4 * n + k, :],
                                      p_y[:, S * k:S * (k + 1)], start=k == 0, stop=k == 3)
                    last.then_inc(sig("slab_done"), 1)
                norm_sum(3 + layer)

        @block.scalar
        def _(act):
            f = nc.scalar.activation

            def norm_root(k):
                act.wait_ge(sig("norm_sum"), k + 1)
                f(rs[:, :], M[:, 0, 0:S], ACT.Sqrt, bias=eps_col, scale=1.0 / D).then_inc(sig("norm_root"), 1)

            def copy_blocks(g0, e0, n, dst, e_dst, name="block_out", ahead=0):
                def one(u, it):
                    act.wait_ge(sig("slab_done"), g0 + u + 1 + RING * it)
                    nc.scalar.copy(dst[:, bass.ds(S * (e_dst + u) + S * RING * it, S)]
                                   if not isinstance(it, int) else dst[:, S * (e_dst + u):S * (e_dst + u + 1)],
                                   stream[:, (e0 + u) % 2, 0:S]).then_inc(sig(name), 1)
                if n <= RING:
                    for u in range(n):
                        one(u, 0)
                else:
                    with act.Fori(0, n // RING) as it:
                        for u in range(RING):
                            one(u, it)

            mixers = W[:, PRE:PRE + 256 * N_MIX]

            def nsa_norms():
                act.wait_ge(sig("block_out"), 12)
                f(n_sq[:, 0:1024], blocks(B_Q, 4), ACT.Square).then_inc(sig("nsa_sq"), 1)
                f(n_sq[:, 1024:1280], blocks(B_KV + 2), ACT.Square).then_inc(sig("nsa_sq"), 1)
                f(n_sq[:, 1280:1536], blocks(B_KV + 4), ACT.Square).then_inc(sig("nsa_sq"), 1)
                act.wait_ge(sig("nsa_ssq"), 1)
                f(n_rs, bank(2, 3), ACT.Sqrt, bias=eps_col, scale=1.0 / P).then_inc(sig("nsa_root"), 1)
                act.wait_ge(sig("nsa_vT"), 1)
                nc.scalar.copy(g_at(1024, 512), M[:, 5, :]).then_inc(sig("nsa_vtok"), 1)
                f(n_hk[:, 0:15], M[:, 0, 0:15], ACT.Gelu_apprx_tanh).then_inc(sig("cmp_hidden"), 1)
                f(n_hv[:, 0:15], M[:, 1, 0:15], ACT.Gelu_apprx_tanh).then_inc(sig("cmp_hidden"), 1)

            def nsa_small():
                act.wait_ge(sig("nsa_small"), 1)
                f(n_gate.rearrange("p (t g) -> p t g", t=2),
                  M[:, 3, 0:256].rearrange("p (t g) -> p t g", t=2)[:, :, GATE_ROW:GATE_ROW + 12],
                  ACT.Sigmoid).then_inc(sig("nsa_gates"), 1)
                nc.scalar.copy(n_vc[0:15, :], M[0:15, 1, 0:P]).then_inc(sig("nsa_vc"), 1)
                f(n_kc2[:, 0:15], M[:, 0, 0:15], ACT.Square).then_inc(sig("kc_sq"), 1)
                act.wait_ge(sig("kc_ssq"), 1)
                f(n_kc[:, 0:15], M[:, 4, 0:15], ACT.Sqrt, bias=eps_col, scale=1.0 / P).then_inc(sig("kc_root"), 1)

            def nsa_bias():
                act.wait_ge(sig("nsa_skew"), 1)
                nc.scalar.copy(g_at(0, 512), M[:, 5, :])
                nc.scalar.copy(g_at(512, 512), M[:, 3, :]).then_inc(sig("nsa_bias"), 1)

            def nsa_exp(t):
                pr = n_prob.rearrange("p (a h s) -> p a h s", a=2, h=4)
                act.wait_ge(sig("nsa_max"), t + 1)
                for hd in range(4):
                    pc = n_pc[:, 16 * hd:16 * hd + 15]
                    f(pc, pc, ACT.Exp, bias=n_nmax[:, hd:hd + 1], accum_out=n_sum[:, hd:hd + 1])
                for a in range(2):
                    for hd in range(4):
                        m = 4 + 4 * a + hd
                        pm = pr[:, a, hd, 0:P * (t + 1)]
                        last = f(pm, pm, ACT.Exp, bias=n_nmax[:, m:m + 1], accum_out=n_sum[:, m:m + 1])
                last.then_inc(sig("nsa_exp"), 1)

            def nsa_turn(t):
                act.wait_ge(sig("nsa_turned"), t + 1)
                n = 4 * P * (t + 1)
                nc.scalar.copy(n_probT[:, 0:n], bank(0, 4)[:, 0:n])
                nc.scalar.copy(n_pcT[0:15, 0:512], M[0:15, 4, :]).then_inc(sig("nsa_PT"), 1)

            def nsa_y(t):
                act.wait_ge(sig("nsa_o"), t + 1)
                nc.scalar.copy(y_sb[:, 8:12, P * t:P * (t + 1)],
                               M[:, 5, :].rearrange("p (h t) -> p h t", h=4)).then_inc(sig("nsa_y"), 1)

            def lru():
                lam, t1, t2, c8 = col("lam", 0, 4), tiny[:, 0:4], tiny[:, 4:8], tiny[:, 8:12]
                f(t1, lam, ACT.Abs).then_inc(sig("act_step"), 1)
                act.wait_ge(sig("act_step"), nth("act_step"))
                f(t1, t1, ACT.Exp, scale=-1.0).then_inc(sig("act_step"), 1)
                act.wait_ge(sig("act_step"), nth("act_step"))
                f(t1, t1, ACT.Ln, bias=1.0).then_inc(sig("lru_ln"), 1)
                act.wait_ge(sig("lru_pre"), 1)
                for j in range(4):
                    last = f(l_a[:, S * j:S * (j + 1)], bank(0, 2)[:, S * j:S * (j + 1)], ACT.Sigmoid,
                             bias=col("b_a", j))
                last.then_inc(sig("lru_gated"), 1)
                act.wait_ge(sig("lru_gated"), nth("lru_gated"))
                for j in range(4):
                    last = f(l_u[:, S * j:S * (j + 1)], bank(2, 2)[:, S * j:S * (j + 1)], ACT.Sigmoid,
                             bias=col("b_i", j))
                last.then_inc(sig("lru_gated"), 1)
                act.wait_ge(sig("lru_c8"), 1)
                for j in range(4):
                    last = f(l_t[:, S * j:S * (j + 1)], l_a[:, S * j:S * (j + 1)], ACT.Tanh, scale=tiny[:, 12 + j:13 + j])
                last.then_inc(sig("lru_tanh"), 1)
                act.wait_ge(sig("lru_tanh"), nth("lru_tanh"))
                for j in range(4):
                    last = f(l_a[:, S * j:S * (j + 1)], l_a[:, S * j:S * (j + 1)], ACT.Exp, scale=tiny[:, 8 + j:9 + j])
                last.then_inc(sig("lru_decay"), 1)
                f(blocks(B_LG, 4), blocks(B_LG, 4), ACT.Gelu_apprx_tanh).then_inc(sig("lru_gelu"), 1)
                act.wait_ge(sig("lru_ratio"), 1)
                f(l_t, l_t, ACT.Sqrt, scale=2.0).then_inc(sig("lru_root"), 1)

            def gla_a():
                act.wait_ge(sig("gla_z"), 1)
                act.wait_ge(sig("nsa_y"), 2)
                for j in range(2):
                    last = f(a_b[:, S * j:S * (j + 1)], M[:, 0, S * j:S * (j + 1)], ACT.Identity, bias=col("gk_b", j))
                last.then_inc(sig("gla_zb"), 1)
                act.wait_ge(sig("gla_zb"), nth("gla_zb"))
                f(a_e1, a_b, ACT.Abs).then_inc(sig("act_step"), 1)
                act.wait_ge(sig("act_step"), nth("act_step"))
                f(a_e1, a_e1, ACT.Exp, scale=-1.0).then_inc(sig("act_step"), 1)
                act.wait_ge(sig("act_step"), nth("act_step"))
                f(a_e1, a_e1, ACT.Ln, bias=1.0).then_inc(sig("gla_ln"), 1)
                act.wait_ge(sig("gla_vT"), 1)
                nc.scalar.copy(g_at(4608, 1024), bank(2, 2)).then_inc(sig("gla_vtok"), 1)
                act.wait_ge(sig("gla_cum"), 1)
                f(a_e1, a_bm, ACT.Exp, scale=1.0 / 16)
                f(a_e2, a_bm, ACT.Exp, scale=-1.0 / 16)
                f(a_eb, a_b, ACT.Exp, scale=1.0 / 16)
                f(a_kl, a_kl, ACT.Exp, scale=1.0 / 16).then_inc(sig("gla_exp"), 1)
                f(blocks(B_GG, 2), blocks(B_GG, 2), ACT.Silu).then_inc(sig("act_step"), 1)
                act.wait_ge(sig("act_step"), nth("act_step"))

            def gla_b():
                act.wait_ge(sig("gla_klT"), 1)
                nc.scalar.copy(g_at(4096, 512), M[:, 4, :]).then_inc(sig("gla_kltok"), 1)

            def gla_c():
                f(blocks(B_GG + 2, 2), blocks(B_GG + 2, 2), ACT.Silu).then_inc(sig("gla_silu"), 1)
                act.wait_ge(sig("gla_o"), 1)
                ov = a_o.rearrange("p (j i t) -> p j i t", j=2, i=2)
                nc.scalar.copy(ov[:, :, 0, :], M[:, 0, :].rearrange("p (j t) -> p j t", j=2))
                nc.scalar.copy(ov[:, :, 1, :], M[:, 1, :].rearrange("p (j t) -> p j t", j=2)) \
                    .then_inc(sig("gla_ocopy"), 1)
                act.wait_ge(sig("gla_ocopy"), nth("gla_ocopy"))
                f(a_sq, a_o, ACT.Square).then_inc(sig("gla_osq"), 1)
                act.wait_ge(sig("gla_ssq"), 1)
                f(a_sq, bank(2, 2), ACT.Sqrt, bias=eps_col, scale=1.0 / P).then_inc(sig("gla_root"), 1)

            def rwkv_a():
                act.wait_ge(sig("rw_mixed"), 1)
                f(blocks(B_XW)[0:96, :], blocks(B_XW)[0:96, :], ACT.Tanh).then_inc(sig("rw_act"), 1)
                f(blocks(B_XG, 2), blocks(B_XG, 2), ACT.Sigmoid).then_inc(sig("rw_act"), 1)
                act.wait_ge(sig("rw_lora"), 1)
                for j in range(4):
                    f(r_sig[:, S * j:S * (j + 1)], bank(0, 2)[:, S * j:S * (j + 1)], ACT.Sigmoid, bias=col("w0", j))
                for j in range(4):
                    f(r_a[:, S * j:S * (j + 1)], bank(2, 2)[:, S * j:S * (j + 1)], ACT.Sigmoid, bias=col("a0", j))
                nc.scalar.copy(r_g, bank(4, 2)).then_inc(sig("rw_sig"), 1)
                act.wait_ge(sig("rw_cum"), 2)
                f(w_at(4096, 1024), r_cs, ACT.Exp, scale=KAPPA)
                f(w_at(5120, 1024), r_kt, ACT.Exp, scale=KAPPA)
                f(r_p, r_cs, ACT.Exp, scale=-KAPPA).then_inc(sig("rw_exp"), 1)
                act.wait_ge(sig("rw_kk"), 1)
                f(r_tmp, r_kk, ACT.Square).then_inc(sig("rw_kksq"), 1)
                act.wait_ge(sig("rw_kkmax"), 1)
                f(r_tmp, r_tmp, ACT.Sqrt).then_inc(sig("rw_kkroot"), 1)

            def rwkv_tokens(r):
                for n, (b, dst) in enumerate(((4, r_ptok), (5, r_ktok), (4, r_vtok))):
                    act.wait_ge(sig("rw_turned"), 3 * r + n + 1)
                    nc.scalar.copy(dst, M[:, b, :]).then_inc(sig("rw_tok"), 1)

            def rwkv_level(r, n):
                if n:
                    act.wait_ge(sig("rw_t1p"), 6 * r + n + 1)
                    nc.scalar.copy(r_t1, bank(0, 2)).then_inc(sig("rw_t1"), 1)

            def rwkv_y(c):
                act.wait_ge(sig("rw_yp"), c + 1)
                nc.scalar.copy(r_y.rearrange("p (j t) -> p j t", j=4)[:, :, 64 * c:64 * c + 64],
                               M[:, 2, 0:256].rearrange("p (j t) -> p j t", j=4)).then_inc(sig("rw_ycopy"), 1)

            def rwkv_norm():
                act.wait_ge(sig("rw_centred"), 1)
                f(r_tmp, r_y, ACT.Square).then_inc(sig("rw_ysq"), 1)
                act.wait_ge(sig("rw_var"), 1)
                f(r_tmp, bank(2, 2), ACT.Sqrt, bias=gn_col, scale=1.0 / 64).then_inc(sig("rw_yroot"), 1)

            def attention(layer, half):
                t0 = 2 * layer + half
                if half == 0:
                    act.wait_ge(sig("block2_out"), 16 * layer + 16)
                act.wait_ge(sig("at_vT"), t0 + 1)
                nc.scalar.copy(p_vtok, M[:, 2, :]).then_inc(sig("at_vtok"), 1)
                gate = p_blocks(8 * half + 6, 2)
                f(gate, gate, ACT.Silu).then_inc(sig("at_silu"), 1)
                if t0 < 3:
                    maps = 8 if t0 == 2 else 4
                    for t in range(2):
                        act.wait_ge(sig("at_max"), 2 * t0 + t + 1)
                        pm = prob_maps(maps, t)
                        for m in range(maps):
                            i = maps * t + m
                            last = f(pm[:, m, :], pm[:, m, :], ACT.Exp, bias=p_stat[:, i:i + 1],
                                     accum_out=p_stat[:, 32 + i:33 + i])
                        last.then_inc(sig("at_exp"), 1)
                else:
                    z = G[:, 4096:4096 + 1536]
                    act.wait_ge(sig("at_z"), 2)
                    f(p_tmp[:, 0:1536], z, ACT.Abs).then_inc(sig("act_step"), 1)
                    act.wait_ge(sig("act_step"), nth("act_step"))
                    f(p_tmp[:, 0:1536], p_tmp[:, 0:1536], ACT.Exp, scale=-1.0).then_inc(sig("act_step"), 1)
                    act.wait_ge(sig("act_step"), nth("act_step"))
                    f(p_tmp[:, 0:1536], p_tmp[:, 0:1536], ACT.Ln, bias=1.0).then_inc(sig("stick_ln"), 1)
                    act.wait_ge(sig("stick_log"), 1)
                    f(z, z, ACT.Exp).then_inc(sig("stick_exp"), 1)
                act.wait_ge(sig("at_turned"), t0 + 1)
                nc.scalar.copy(p_probT, bank(0, 3)).then_inc(sig("at_PT"), 1)
                if t0 == 2:
                    act.wait_ge(sig("at_o"), 3)
                    f(p_sq, M[:, 3, :], ACT.Square).then_inc(sig("at_osq"), 1)
                    act.wait_ge(sig("at_oss"), 1)
                    f(p_sq, M[:, 4, :], ACT.Sqrt, bias=eps_col, scale=1.0 / 64).then_inc(sig("at_oroot"), 1)

            eps_col, gn_col = tiny[:, 20:21], tiny[:, 21:22]
            act.wait_ge(sig("x_in"), 16)
            act.wait_ge(sig("tiny_set"), 1)
            f(W[:, 0:4096], x_sb[:, :, :].rearrange("p k t -> p (k t)"), ACT.Square).then_inc(sig("x_squares"), 1)
            norm_root(0)
            copy_blocks(0, 0, 4, mixers, 0)
            copy_blocks(4, 4, 8, mixers, 4)
            nsa_norms()
            copy_blocks(G_IN_B, 12, 4, mixers, 12)
            nsa_small()
            copy_blocks(G_IN_B + 4, 16, 4, mixers, 16)
            nsa_bias()
            nsa_exp(0)
            copy_blocks(G_IN_B + 8, 20, 4, mixers, 20)
            nsa_turn(0)
            copy_blocks(G_IN_B + 12, 24, 4, mixers, 24)
            nsa_y(0)
            nsa_exp(1)
            copy_blocks(G_IN_B + 16, 28, 4, mixers, 28)
            nsa_turn(1)
            copy_blocks(G_IN_B + 20, 32, 4, mixers, 32)
            nsa_y(1)
            lru()
            copy_blocks(G_IN_B + 24, 36, 4, mixers, 36)
            gla_a()
            copy_blocks(G_IN_B + 28, 40, 4, mixers, 40)
            gla_b()
            copy_blocks(G_IN_B + 32, 44, 3, mixers, 44)
            gla_c()
            act.wait_ge(sig("gla_done"), 1)
            gates_run = []

            def gates(n):
                e = sum(gates_run)
                copy_blocks(G_GATES + 4 * e, N_MIX + 4 * e, 4 * n, G, 4 * e)
                gates_run.append(n)

            gates(1)
            rwkv_a()
            for r in range(2):
                rwkv_tokens(r)
                for n in range(6):
                    rwkv_level(r, n)
                    if n % 3 == 2:
                        gates(1)
                for c in (2 * r, 2 * r + 1):
                    rwkv_y(c)
                    if c < 3:
                        gates(1)
            rwkv_norm()
            act.wait_ge(sig("rwkv_y"), 1)
            gates(N_GATES // 4 - sum(gates_run))

            act.wait_ge(sig("block_out"), N_MIX + N_GATES)
            gv = G[:, :].rearrange("p (b n t) -> p b n t", b=4, n=KT)
            with act.Fori(0, KT) as it:
                f(gv[:, :, it, :], gv[:, :, it, :], ACT.Sigmoid).then_inc(sig("gate_sig"), 1)
            norm_root(1)
            with act.Fori(0, FB // 2) as it:
                for u in range(2):
                    act.wait_ge(sig("slab_done"), G_UP + 2 * u + 2 + 4 * it)
                    act.wait_ge(sig("ffn_act"), u + 1 + 2 * it)
                    for v in range(2):
                        b = up_bank[2 * u + v]
                        i = u + 2 * it
                        f(ffn_buf[:, u, v, :], b, ACT.Identity,
                          bias=cv[:, bass.ds(COLS["fconv_b"][0] + FB * v + i, 1)],
                          scale=cv[:, bass.ds(COLS["fconv_w"][0] + 2 * 2 * FB + FB * v + i, 1)]) \
                            .then_inc(sig("ffn_tap"), 1)
                    act.wait_ge(sig("up_read"), 2 + u + 1 + 2 * it)
                    f(ffn_buf[:, u, 0, :], ffn_buf[:, u, 0, :], ACT.Silu).then_inc(sig("ffn_silu"), 1)
            norm_root(2)
            for layer in range(2):
                for e in range(KT):
                    act.wait_ge(sig("slab_done"), G_IN2[layer] + e + 1)
                    nc.scalar.copy(p_blocks(e), stream[:, e % 2, 0:S]).then_inc(sig("block2_out"), 1)
                if layer == 1:
                    act.wait_ge(sig("lam_dot"), 1)
                    f(tiny[:, 24:26], tiny[:, 24:26], ACT.Exp).then_inc(sig("lam_exp"), 1)
                attention(layer, 0)
                attention(layer, 1)
                norm_root(3 + layer)

        @block.vector
        def _(dve):
            v = nc.vector

            def norm_apply(k, gain):
                dve.wait_ge(sig("norm_root"), k + 1)
                v.reciprocal(rs[:, :], rs[:, :]).then_inc(sig("dve_step"), 1)
                dve.wait_ge(sig("dve_step"), nth("dve_step"))
                for n in range(KT):
                    v.scalar_tensor_tensor(h_sb[:, n, :], x_sb[:, n, :], col(gain, n), rs[:, :], ALU.mult,
                                           ALU.mult).then_inc(sig("h_ready"), 1)

            def nsa_blocks():
                dve.wait_ge(sig("block_out"), B_KV + 2)
                for a in range(2):
                    x = blocks(B_KV + a)
                    o = n_blk[:, 480 * a:480 * (a + 1)].rearrange("p (l n) -> p l n", n=15)
                    for half in range(2):
                        win = x[:, 16 * half:16 * half + 240].rearrange("p (n l) -> p l n", l=16)
                        v.tensor_tensor(o[:, 16 * half:16 * half + 16, :], win,
                                        spread(col("pos", 16 * half, 16), 15), ALU.add).then_inc(sig("cmp_in"), 1)
                        dve.wait_ge(sig("cmp_in"), nth("cmp_in"))

            def nsa_norms():
                dve.wait_ge(sig("nsa_root"), 1)
                v.reciprocal(n_rs, n_rs).then_inc(sig("nsa_rs"), 1)
                dve.wait_ge(sig("nsa_rs"), nth("nsa_rs"))
                v.scalar_tensor_tensor(blocks(B_Q, 4), blocks(B_Q, 4), col("q_gain"), n_rs[:, 0:1024],
                                       ALU.mult, ALU.mult).then_inc(sig("nsa_qk"), 1)
                for a in range(2):
                    k = blocks(B_KV + 2 + 2 * a)
                    v.scalar_tensor_tensor(k, k, col("k_gain"), n_rs[:, 1024 + S * a:1024 + S * (a + 1)],
                                           ALU.mult, ALU.mult).then_inc(sig("nsa_qk"), 1)

            def nsa_small():
                dve.wait_ge(sig("nsa_small"), 1)
                v.tensor_tensor(n_ext[0:4, :], M[0:4, 2, :], n_hot[0:4, 512:1024], ALU.add) \
                    .then_inc(sig("bias_row"), 1)
                dve.wait_ge(sig("bias_row"), nth("bias_row"))
                dve.wait_ge(sig("kc_root"), 1)
                v.reciprocal(n_kc[:, 0:15], n_kc[:, 0:15]).then_inc(sig("dve_step"), 1)
                dve.wait_ge(sig("dve_step"), nth("dve_step"))
                v.scalar_tensor_tensor(n_kc[:, 0:15], M[:, 0, 0:15], col("k_gain"), n_kc[:, 0:15],
                                       ALU.mult, ALU.mult).then_inc(sig("nsa_qk"), 1)
                dve.wait_ge(sig("nsa_qk"), 4)

            def nsa_softmax(t):
                pr = n_prob.rearrange("p (a h s) -> p a h s", a=2, h=4)
                scale = P ** -0.5
                w = P * (t + 1)
                dve.wait_ge(sig("nsa_logits"), t + 1)
                if t == 0:
                    dve.wait_ge(sig("nsa_bias"), 1)
                pc = n_pc.rearrange("p (h n) -> p h n", h=4)
                v.memset(n_pc, NEG).then_inc(sig("dve_step"), 1)
                dve.wait_ge(sig("dve_step"), nth("dve_step"))
                lo, n = (31 + P, 7) if t == 0 else (31, 15)
                bias_c = n_bias[:, :, lo:lo + 16 * (n - 1) + 1:16]
                v.scalar_tensor_tensor(pc[:, :, 0:n], M[:, 4, 0:64].rearrange("p (h n) -> p h n", h=4)[:, :, 0:n],
                                       scale, bias_c, ALU.mult, ALU.add)
                for a in range(2):
                    o = bank(2 * a, 2).rearrange("p (h s) -> p h s", h=4)
                    last = v.scalar_tensor_tensor(pr[:, a, :, 0:w], o[:, :, 0:w], scale, n_bias[:, :, S - w:S],
                                                  ALU.mult, ALU.add)
                last.then_inc(sig("dve_step"), 1)
                dve.wait_ge(sig("dve_step"), nth("dve_step"))
                v.tensor_reduce(n_nmax[:, 0:4], pc[:, :, 0:15], AX.X, ALU.max, negate=True)
                last = v.tensor_reduce(n_nmax[:, 4:12].rearrange("p (a h) -> p a h", a=2), pr[:, :, :, 0:w], AX.X,
                                       ALU.max, negate=True)
                last.then_inc(sig("dve_step"), 1)
                dve.wait_ge(sig("dve_step"), nth("dve_step"))
                v.tensor_scalar(n_nmax[:, 0:4], n_nmax[:, 0:4], 1.0e8, None, ALU.min).then_inc(sig("nsa_max"), 1)
                dve.wait_ge(sig("nsa_max"), nth("nsa_max"))
                dve.wait_ge(sig("nsa_exp"), t + 1)
                if t == 0:
                    dve.wait_ge(sig("nsa_gates"), 1)
                v.tensor_scalar(n_sum, n_sum, 1.0e-30, None, ALU.max).then_inc(sig("dve_step"), 1)
                dve.wait_ge(sig("dve_step"), nth("dve_step"))
                v.reciprocal(n_wt, n_sum).then_inc(sig("dve_step"), 1)
                dve.wait_ge(sig("dve_step"), nth("dve_step"))
                v.tensor_tensor(n_wt, n_wt, n_gate[:, 12 * t:12 * t + 12], ALU.mult).then_inc(sig("dve_step"), 1)
                dve.wait_ge(sig("dve_step"), nth("dve_step"))
                v.tensor_tensor(pc, pc, spread(n_wt[:, 0:4], 16), ALU.mult)
                for a in range(2):
                    last = v.tensor_tensor(pr[:, a, :, 0:w], pr[:, a, :, 0:w], spread(n_wt[:, 4 + 4 * a:8 + 4 * a], w),
                                           ALU.mult)
                last.then_inc(sig("nsa_weighted"), 1)
                dve.wait_ge(sig("nsa_weighted"), nth("nsa_weighted"))
                dve.wait_ge(sig("nsa_turned"), t + 1)
                n = 4 * P * (t + 1)
                v.tensor_copy(n_probT[:, n:2 * n], bank(0, 4)[:, n:2 * n]).then_inc(sig("nsa_PT_dve"), 1)
                dve.wait_ge(sig("nsa_PT_dve"), nth("nsa_PT_dve"))

            def lru():
                dve.wait_ge(sig("block_out"), B_LG + 4)
                for j in range(4):
                    b = S * j
                    v.tensor_scalar(l_xc[:, b:b + S], blocks(B_LX + j), col("conv_w", 12 + j), col("conv_b", j),
                                    ALU.mult, ALU.add).then_inc(sig("dve_step"), 1)
                    dve.wait_ge(sig("dve_step"), nth("dve_step"))
                    for back in (1, 2, 3):
                        ins = v.scalar_tensor_tensor(l_xc[:, b + back:b + S], blocks(B_LX + j)[:, 0:S - back],
                                                     col("conv_w", 4 * (3 - back) + j), l_xc[:, b + back:b + S],
                                                     ALU.mult, ALU.add)
                        ins.then_inc(sig("lru_conv"), 1)
                        dve.wait_ge(sig("lru_conv"), nth("lru_conv"))

            def lru_b():
                dve.wait_ge(sig("lru_ln"), 1)
                lam, t1, c8 = col("lam", 0, 4), tiny[:, 0:4], tiny[:, 8:12]
                v.scalar_tensor_tensor(t1, lam, 0.0, t1, ALU.min, ALU.subtract).then_inc(sig("dve_step"), 1)
                dve.wait_ge(sig("dve_step"), nth("dve_step"))
                v.tensor_scalar(c8, t1, 8.0, None, ALU.mult).then_inc(sig("dve_step"), 1)
                dve.wait_ge(sig("dve_step"), nth("dve_step"))
                v.tensor_scalar(tiny[:, 12:16], t1, -8.0, None, ALU.mult).then_inc(sig("lru_c8"), 1)
                dve.wait_ge(sig("lru_c8"), nth("lru_c8"))
                dve.wait_ge(sig("lru_gated"), 2)
                v.tensor_tensor(l_u, l_u, l_xc, ALU.mult).then_inc(sig("dve_step"), 1)
                dve.wait_ge(sig("dve_step"), nth("dve_step"))
                dve.wait_ge(sig("lru_tanh"), 1)
                v.tensor_scalar(l_xc, l_t, 1.0, None, ALU.add).then_inc(sig("dve_step"), 1)
                dve.wait_ge(sig("dve_step"), nth("dve_step"))
                v.reciprocal(l_xc, l_xc).then_inc(sig("dve_step"), 1)
                dve.wait_ge(sig("dve_step"), nth("dve_step"))
                v.tensor_tensor(l_t, l_t, l_xc, ALU.mult).then_inc(sig("lru_ratio"), 1)
                dve.wait_ge(sig("lru_ratio"), nth("lru_ratio"))
                dve.wait_ge(sig("lru_root"), 1)
                v.tensor_tensor(l_u, l_u, l_t, ALU.mult).then_inc(sig("dve_step"), 1)
                dve.wait_ge(sig("dve_step"), nth("dve_step"))
                dve.wait_ge(sig("lru_decay"), 1)
                for j in range(4):
                    b = S * j
                    last = v.tensor_tensor_scan(l_t[:, b:b + S], l_a[:, b:b + S], l_u[:, b:b + S], 0.0, ALU.mult,
                                                ALU.add)
                last.then_inc(sig("dve_step"), 1)
                dve.wait_ge(sig("dve_step"), nth("dve_step"))
                dve.wait_ge(sig("lru_gelu"), 1)
                v.tensor_tensor(y_sb[:, 4:8, :].rearrange("p k t -> p (k t)"), l_t, blocks(B_LG, 4), ALU.mult) \
                    .then_inc(sig("dve_step"), 1)
                dve.wait_ge(sig("dve_step"), nth("dve_step"))

            def gla():
                dve.wait_ge(sig("gla_ln"), 1)
                v.scalar_tensor_tensor(a_e2, a_b, 0.0, a_e1, ALU.min, ALU.subtract).then_inc(sig("dve_step"), 1)
                dve.wait_ge(sig("dve_step"), nth("dve_step"))
                for j in range(2):
                    last = v.tensor_tensor_scan(a_b[:, S * j:S * (j + 1)], reset, a_e2[:, S * j:S * (j + 1)], 0.0,
                                                ALU.mult, ALU.add)
                last.then_inc(sig("dve_step"), 1)
                dve.wait_ge(sig("dve_step"), nth("dve_step"))
                bc = a_b.rearrange("p (c t) -> p c t", t=64)
                v.tensor_tensor(a_bm.rearrange("p (c t) -> p c t", t=64), bc,
                                bc[:, :, 31:32].to_broadcast([P, 8, 64]), ALU.subtract)
                last = v.tensor_tensor(a_kl.rearrange("p (c t) -> p c t", t=64),
                                       bc[:, :, 63:64].to_broadcast([P, 8, 64]), bc, ALU.subtract)
                last.then_inc(sig("dve_step"), 1)
                dve.wait_ge(sig("dve_step"), nth("dve_step"))
                v.tensor_scalar(a_bm, a_bm, 640.0, -640.0, ALU.min, ALU.max).then_inc(sig("gla_cum"), 1)
                dve.wait_ge(sig("gla_cum"), nth("gla_cum"))
                dve.wait_ge(sig("gla_exp"), 1)
                dve.wait_ge(sig("block_out"), B_GV)
                q, k = blocks(B_GQ, 2), blocks(B_GK, 2)
                sc = 64.0 ** -0.5
                v.scalar_tensor_tensor(a_qs, q, sc, a_e1, ALU.mult, ALU.mult).then_inc(sig("gla_qk"), 1)
                v.tensor_tensor(a_ks, k, a_e2, ALU.mult).then_inc(sig("gla_qk"), 1)
                v.scalar_tensor_tensor(a_qi, q, sc, a_eb, ALU.mult, ALU.mult).then_inc(sig("gla_qk"), 1)
                v.tensor_tensor(a_kl, k, a_kl, ALU.mult).then_inc(sig("gla_qk"), 1)
                dve.wait_ge(sig("gla_qk"), 4)
                v.tensor_copy(tiny[:, 32:40], a_eb.rearrange("p (c t) -> p c t", t=64)[:, :, 63]) \
                    .then_inc(sig("dve_step"), 1)
                dve.wait_ge(sig("dve_step"), nth("dve_step"))
                dve.wait_ge(sig("gla_sc"), 1)
                v.tensor_tensor(a_sc.rearrange("p h r t -> p (h r) t"),
                                bank(0, 2).rearrange("p (n t) -> p n t", n=8), over(incl, 8), ALU.mult) \
                                    .then_inc(sig("gla_masked"), 1)
                dve.wait_ge(sig("gla_masked"), nth("gla_masked"))
                dve.wait_ge(sig("gla_dS"), 1)
                v.tensor_copy(a_st[:, :, 0:3:2, :], M[:, 4, :].rearrange("p (j c v) -> p j c v", j=2, c=2))
                v.tensor_copy(a_st[:, :, 1, :], M[:, 5, :].rearrange("p (j c v) -> p j c v", j=2, c=2)[:, :, 0, :]) \
                    .then_inc(sig("dve_step"), 1)
                dve.wait_ge(sig("dve_step"), nth("dve_step"))
                for c in (1, 2):
                    for j in range(2):
                        last = v.scalar_tensor_tensor(a_st[:, j, c, :], a_st[:, j, c - 1, :],
                                                      tiny[:, 32 + 4 * j + c:33 + 4 * j + c], a_st[:, j, c, :],
                                                      ALU.mult, ALU.add)
                    last.then_inc(sig("gla_S" if c == 2 else "dve_step"), 1)
                    dve.wait_ge(sig("gla_S" if c == 2 else "dve_step"), nth("gla_S" if c == 2 else "dve_step"))
                dve.wait_ge(sig("gla_ocopy"), 1)
                dve.wait_ge(sig("gla_root"), 1)
                v.reciprocal(a_sq, a_sq).then_inc(sig("dve_step"), 1)
                dve.wait_ge(sig("dve_step"), nth("dve_step"))
                v.scalar_tensor_tensor(a_o, a_o, col("gla_gain"), a_sq, ALU.mult, ALU.mult) \
                    .then_inc(sig("dve_step"), 1)
                dve.wait_ge(sig("dve_step"), nth("dve_step"))
                dve.wait_ge(sig("gla_silu"), 1)
                v.tensor_tensor(y_sb[:, 0:4, :].rearrange("p k t -> p (k t)"), a_o, blocks(B_GG, 4), ALU.mult) \
                    .then_inc(sig("gla_done"), 1)
                dve.wait_ge(sig("gla_done"), nth("gla_done"))

            def rwkv_feat():
                dve.wait_ge(sig("block_out"), N_MIX)
                sh = r_shift.rearrange("p (k t) -> p k t", k=16)
                fe = blocks(B_R, 16).rearrange("p (k t) -> p k t", k=16)
                v.tensor_tensor(sh, fe, spread(col("mu", 0, 16), S), ALU.mult).then_inc(sig("dve_step"), 1)
                dve.wait_ge(sig("dve_step"), nth("dve_step"))
                v.tensor_tensor(fe, fe, sh, ALU.subtract).then_inc(sig("dve_step"), 1)
                dve.wait_ge(sig("dve_step"), nth("dve_step"))
                v.tensor_tensor(fe[:, :, 1:S], fe[:, :, 1:S], sh[:, :, 0:S - 1], ALU.add).then_inc(sig("rw_mixed"), 1)
                dve.wait_ge(sig("rw_mixed"), nth("rw_mixed"))

                def four(ap):
                    return ap.rearrange("p (j t) -> p j t", j=4)

                k, r_ = blocks(B_K, 4), blocks(B_R, 4)
                v.tensor_tensor(four(r_kk), four(k), spread(col("k_k", 0, 4), S), ALU.mult).then_inc(sig("rw_kk0"), 1)
                dve.wait_ge(sig("rw_kk0"), nth("rw_kk0"))
                dve.wait_ge(sig("rw_sig"), 1)
                for j in range(4):
                    last = v.tensor_tensor_scan(r_cs[:, S * j:S * (j + 1)], reset, r_sig[:, S * j:S * (j + 1)], 0.0,
                                                ALU.mult, ALU.add)
                last.then_inc(sig("rw_cum"), 1)
                dve.wait_ge(sig("rw_cum"), nth("rw_cum"))
                v.tensor_tensor(r_kt, r_cs, r_sig, ALU.subtract).then_inc(sig("rw_cum"), 1)
                dve.wait_ge(sig("rw_cum"), nth("rw_cum"))
                v.scalar_tensor_tensor(four(r_bonus), four(r_a), -1.0, spread(col("k_a", 0, 4), S), ALU.add,
                                       ALU.mult).then_inc(sig("dve_step"), 1)
                dve.wait_ge(sig("dve_step"), nth("dve_step"))
                v.scalar_tensor_tensor(k, r_bonus, 1.0, k, ALU.add, ALU.mult).then_inc(sig("rw_kk"), 1)
                dve.wait_ge(sig("rw_kk"), nth("rw_kk"))
                v.tensor_tensor(four(r_bonus), four(k), spread(col("r_k", 0, 4), S), ALU.mult) \
                    .then_inc(sig("dve_step"), 1)
                dve.wait_ge(sig("dve_step"), nth("dve_step"))
                v.tensor_tensor(r_bonus, r_bonus, r_, ALU.mult).then_inc(sig("rw_rk"), 1)
                dve.wait_ge(sig("rw_rk"), nth("rw_rk"))
                dve.wait_ge(sig("rw_kkss"), 1)
                v.tensor_scalar(r_tmp, bank(0, 2), 1.0e-24, None, ALU.max).then_inc(sig("rw_kkmax"), 1)
                dve.wait_ge(sig("rw_kkmax"), nth("rw_kkmax"))
                dve.wait_ge(sig("rw_kkroot"), 1)
                v.reciprocal(r_tmp, r_tmp).then_inc(sig("dve_step"), 1)
                dve.wait_ge(sig("dve_step"), nth("dve_step"))
                v.tensor_tensor(r_kk, r_kk, r_tmp, ALU.mult).then_inc(sig("dve_step"), 1)
                dve.wait_ge(sig("dve_step"), nth("dve_step"))
                dve.wait_ge(sig("rw_rks"), 1)
                v.tensor_tensor(r_bonus, bank(2, 2), blocks(B_V, 4), ALU.mult).then_inc(sig("dve_step"), 1)
                dve.wait_ge(sig("dve_step"), nth("dve_step"))
                dve.wait_ge(sig("rw_exp"), 1)
                e1, e3 = w_at(4096, 1024), w_at(5120, 1024)
                v.tensor_copy(r_dec, four(e1)[:, :, 63::64])
                v.tensor_tensor(r_tmp, r_, e1, ALU.mult)
                last = v.tensor_tensor(r_y2, r_kk, e3, ALU.mult)
                last.then_inc(sig("dve_step"), 1)
                dve.wait_ge(sig("dve_step"), nth("dve_step"))
                v.tensor_tensor(r_kt, k, r_p, ALU.mult)
                v.tensor_tensor(r_a, r_a, r_kk, ALU.mult).then_inc(sig("dve_step"), 1)
                dve.wait_ge(sig("dve_step"), nth("dve_step"))
                v.tensor_tensor(r_p, r_a, r_p, ALU.mult)
                v.memset(r_u, 0.0)
                v.tensor_copy(r_qr[:, :, :, 1, :], r_tmp.rearrange("p (j r t) -> p j r t", j=4, r=2))
                v.tensor_copy(r_qr[:, :, :, 0, :], r_y2.rearrange("p (j r t) -> p j r t", j=4, r=2)) \
                    .then_inc(sig("rw_feat"), 1)
                dve.wait_ge(sig("rw_feat"), nth("rw_feat"))

            def rwkv_pair(r):
                for n, dst in enumerate((r_ar, r_bk)):
                    dve.wait_ge(sig("rw_scores"), 2 * r + n + 1)
                    v.tensor_tensor(dst, bank(0, 4).rearrange("p (h t) -> p h t", h=8), over(strict_incl, 8),
                                    ALU.mult).then_inc(sig("rw_ar" if n == 0 else "rw_bk"), 1)
                    dve.wait_ge(sig("rw_ar" if n == 0 else "rw_bk"), nth("rw_ar" if n == 0 else "rw_bk"))

            def eight(ap):
                return ap.rearrange("p (h t) -> p h t", h=8)

            def rwkv_mask(n):
                v.tensor_tensor(eight(r_mt), r_ar[:, :, 0:P], over(level(n), 8), ALU.mult).then_inc(sig("rw_mt"), 1)
                dve.wait_ge(sig("rw_mt"), nth("rw_mt"))

            def rwkv_levels(r):
                rwkv_mask(0)
                v.tensor_tensor(eight(r_xt), over(ident, 8), eight(r_mt), ALU.subtract).then_inc(sig("dve_step"), 1)
                dve.wait_ge(sig("dve_step"), nth("dve_step"))
                dve.wait_ge(sig("rw_t1p"), 6 * r + 1)
                v.tensor_tensor(eight(r_x), over(ident, 8), bank(0, 2).rearrange("p (h t) -> p h t", h=8),
                                ALU.subtract).then_inc(sig("rw_x"), 1)
                dve.wait_ge(sig("rw_x"), nth("rw_x"))
                rwkv_mask(1)
                for n in range(1, 6):
                    dve.wait_ge(sig("rw_dx"), 5 * r + n)
                    if n < 5:
                        v.tensor_tensor(r_x, r_x, bank(2, 2), ALU.subtract)
                    v.tensor_tensor(r_xt, r_xt, bank(4, 2), ALU.subtract) \
                        .then_inc(sig("rw_x" if n < 5 else "rw_xt"), 1)
                    dve.wait_ge(sig("rw_x" if n < 5 else "rw_xt"), nth("rw_x" if n < 5 else "rw_xt"))
                    if n < 5:
                        rwkv_mask(n + 1)

            def rwkv_chunk(c):
                cb = 64 * (c % 2)
                rows = slice(cb, cb + 64)
                dve.wait_ge(sig("rw_rhsp"), c + 1)
                v.tensor_scalar(r_rhs[rows, :].rearrange("p (i n) -> p i n", i=2), M[rows, 0:2, 0:256], -1.0, None,
                                ALU.mult).then_inc(sig("rw_rhs"), 1)
                dve.wait_ge(sig("rw_rhs"), nth("rw_rhs"))
                dve.wait_ge(sig("rw_up"), c + 1)
                v.tensor_copy(r_u[rows, :], M[rows, 4, :]).then_inc(sig("rw_u"), 1)
                dve.wait_ge(sig("rw_u"), nth("rw_u"))
                if c == 3:
                    return
                dve.wait_ge(sig("rw_sp"), c + 1)
                sp_ = M[:, 3, 0:256].rearrange("p (j i) -> p j i", j=4)
                new = r_stc[(c + 1) % 2]
                dec = r_dec[:, :, c:c + 1].to_broadcast([P, 4, 64])
                if c == 0:
                    v.tensor_tensor(new, sp_, dec, ALU.mult).then_inc(sig("rw_state"), 1)
                    dve.wait_ge(sig("rw_state"), nth("rw_state"))
                else:
                    v.tensor_tensor(r_ssum, r_stc[c % 2], sp_, ALU.add).then_inc(sig("dve_step"), 1)
                    dve.wait_ge(sig("dve_step"), nth("dve_step"))
                    v.tensor_tensor(new, r_ssum, dec, ALU.mult).then_inc(sig("rw_state"), 1)
                    dve.wait_ge(sig("rw_state"), nth("rw_state"))

            def rwkv_norm():
                def four(ap):
                    return ap.rearrange("p (j t) -> p j t", j=4)
                dve.wait_ge(sig("rw_mean"), 1)
                dve.wait_ge(sig("rw_ycopy"), 4)
                v.scalar_tensor_tensor(r_y, bank(0, 2), -1.0 / 64, r_y, ALU.mult, ALU.add) \
                    .then_inc(sig("rw_centred"), 1)
                dve.wait_ge(sig("rw_centred"), nth("rw_centred"))
                dve.wait_ge(sig("rw_yroot"), 1)
                v.reciprocal(r_tmp, r_tmp).then_inc(sig("dve_step"), 1)
                dve.wait_ge(sig("dve_step"), nth("dve_step"))
                v.tensor_tensor(r_y, r_y, r_tmp, ALU.mult).then_inc(sig("dve_step"), 1)
                dve.wait_ge(sig("dve_step"), nth("dve_step"))
                v.tensor_tensor(four(r_y), four(r_y), spread(col("ln_w", 0, 4), S), ALU.mult) \
                    .then_inc(sig("dve_step"), 1)
                dve.wait_ge(sig("dve_step"), nth("dve_step"))
                v.tensor_tensor(four(r_y), four(r_y), spread(col("ln_b", 0, 4), S), ALU.add) \
                    .then_inc(sig("dve_step"), 1)
                dve.wait_ge(sig("dve_step"), nth("dve_step"))
                v.tensor_tensor(r_y, r_y, r_bonus, ALU.add).then_inc(sig("dve_step"), 1)
                dve.wait_ge(sig("dve_step"), nth("dve_step"))
                v.tensor_tensor(y_sb[:, 12:16, :].rearrange("p k t -> p (k t)"), r_y, r_g, ALU.mult) \
                    .then_inc(sig("rwkv_y"), 1)
                dve.wait_ge(sig("rwkv_y"), nth("rwkv_y"))

            def attention(layer, half):
                t0 = 2 * layer + half
                q = p_blocks(8 * half, 4)
                qv = q.rearrange("p (b t) -> p b t", b=4)
                if t0 < 3:
                    dve.wait_ge(sig("at_rot"), t0 + 1)
                    cs, sn = (C2_COS64, C2_SIN64) if layer == 0 else (C2_COS32, C2_SIN32)
                    tmp = p_tmp[:, 0:1024]
                    if t0 == 0:
                        dve.wait_ge(sig("const2_in"), 16)
                    v.tensor_tensor(tmp.rearrange("p (b t) -> p b t", b=4),
                                    bank(0, 2).rearrange("p (b t) -> p b t", b=4), over(c2(sn, S), 4), ALU.mult)
                    v.tensor_tensor(qv, qv, over(c2(cs, S), 4), ALU.mult).then_inc(sig("dve_step"), 1)
                    dve.wait_ge(sig("dve_step"), nth("dve_step"))
                    v.tensor_tensor(q, q, tmp, ALU.add).then_inc(sig("at_qk"), 1)
                    dve.wait_ge(sig("at_qk"), nth("at_qk"))
                maps = 8 if t0 == 2 else 4
                scale = 32.0 ** -0.5 if t0 == 2 else 64.0 ** -0.5
                for t in range(2):
                    w = P * (t + 1)
                    dve.wait_ge(sig("at_logits"), 2 * t0 + t + 1)
                    pm = prob_maps(maps, t) if t0 < 3 else stick_z(t)
                    rows = maps // 2
                    ps = [b[:, 0:2 * w].rearrange("p (j s) -> p j s", j=2) for b in logit_banks(rows, t)]
                    if t0 < 3:
                        mask = c2(C2_DIL if t0 == 0 else C2_CAUSAL, S)[:, S - w:S]
                        for i in range(rows):
                            last = v.scalar_tensor_tensor(pm[:, 2 * i:2 * i + 2, :], ps[i], scale, over(mask, 2),
                                                          ALU.mult, ALU.add)
                        last.then_inc(sig("dve_step"), 1)
                        dve.wait_ge(sig("dve_step"), nth("dve_step"))
                        v.tensor_reduce(p_stat[:, maps * t:maps * (t + 1)], pm, AX.X, ALU.max, negate=True) \
                            .then_inc(sig("at_max"), 1)
                        dve.wait_ge(sig("at_max"), nth("at_max"))
                    else:
                        v.tensor_scalar(pm[:, 0:2, :], ps[0], scale, None, ALU.mult)
                        v.tensor_scalar(pm[:, 2:4, :], ps[1], scale, None, ALU.mult).then_inc(sig("at_z"), 1)
                        dve.wait_ge(sig("at_z"), nth("at_z"))
                if t0 < 3:
                    dve.wait_ge(sig("at_exp"), 2 * t0 + 2)
                    inv = p_stat[:, 64:64 + 2 * maps]
                    v.reciprocal(inv, p_stat[:, 32:32 + 2 * maps]).then_inc(sig("dve_step"), 1)
                    dve.wait_ge(sig("dve_step"), nth("dve_step"))
                    if t0 == 2:
                        dve.wait_ge(sig("lam_exp"), 1)
                        l = tiny[:, 26:27]
                        v.tensor_tensor(l, tiny[:, 25:26], tiny[:, 24:25], ALU.subtract).then_inc(sig("dve_step"), 1)
                        dve.wait_ge(sig("dve_step"), nth("dve_step"))
                        v.tensor_scalar(l, l, -LAMBDA_INIT, None, ALU.add).then_inc(sig("dve_step"), 1)
                        dve.wait_ge(sig("dve_step"), nth("dve_step"))
                        odd = inv.rearrange("p (m i j) -> p m i j", i=2, j=2)[:, :, 1, :]
                        v.tensor_scalar(odd, odd, l, None, ALU.mult).then_inc(sig("dve_step"), 1)
                        dve.wait_ge(sig("dve_step"), nth("dve_step"))
                    for t in range(2):
                        pm = prob_maps(maps, t)
                        ins = v.tensor_tensor(pm, pm, spread(inv[:, maps * t:maps * (t + 1)], P * (t + 1)), ALU.mult)
                        if t0 != 2:
                            if t == 1:
                                ins.then_inc(sig("at_prob"), 1)
                                dve.wait_ge(sig("at_prob"), nth("at_prob"))
                        else:
                            ins.then_inc(sig("dve_step"), 1)
                            dve.wait_ge(sig("dve_step"), nth("dve_step"))
                    if t0 == 2:
                        for t in range(2):
                            pm = p_probs[t].rearrange("p (h i n) -> p h i n", h=2, i=2)
                            v.tensor_tensor(diff_tmp(t).rearrange("p (h j) s -> p h (j s)", h=2),
                                            pm[:, :, 0, :], pm[:, :, 1, :], ALU.add) \
                                                .then_inc(sig("at_prob" if t == 1 else "dve_step"), 1)
                            dve.wait_ge(sig("at_prob" if t == 1 else "dve_step"), nth("at_prob" if t == 1 else "dve_step"))
                else:
                    dve.wait_ge(sig("stick_ln"), 1)
                    for t in range(2):
                        w = P * (t + 1)
                        z, sp_ = stick_z(t), stick_s(t)
                        v.scalar_tensor_tensor(sp_, z, 0.0, sp_, ALU.max, ALU.add).then_inc(sig("dve_step"), 1)
                        dve.wait_ge(sig("dve_step"), nth("dve_step"))
                        v.tensor_tensor(sp_, sp_, over(c2(C2_BEFORE, S)[:, S - w:S], 4), ALU.mult) \
                            .then_inc(sig("dve_step"), 1)
                        dve.wait_ge(sig("dve_step"), nth("dve_step"))
                        for hd in range(4):
                            last = v.tensor_tensor_scan(stick_r(t)[:, hd, ::-1], ones_row[:, 0:w], sp_[:, hd, ::-1],
                                                        0.0, ALU.mult, ALU.add)
                        last.then_inc(sig("dve_step"), 1)
                        dve.wait_ge(sig("dve_step"), nth("dve_step"))
                        v.tensor_tensor(z, z, stick_r(t), ALU.subtract).then_inc(sig("dve_step"), 1)
                        dve.wait_ge(sig("dve_step"), nth("dve_step"))
                        v.tensor_tensor(z, z, over(c2(C2_STRICT, S)[:, S - w:S], 4), ALU.add) \
                            .then_inc(sig("stick_log" if t == 1 else "dve_step"), 1)
                        dve.wait_ge(sig("stick_log" if t == 1 else "dve_step"), nth("stick_log" if t == 1 else "dve_step"))
                y = p_y[:, 512 * half:512 * (half + 1)]
                gate = p_blocks(8 * half + 6, 2)
                dve.wait_ge(sig("at_silu"), t0 + 1)
                if t0 == 2:
                    dve.wait_ge(sig("at_oroot"), 1)
                    v.reciprocal(p_sq, p_sq).then_inc(sig("dve_step"), 1)
                    dve.wait_ge(sig("dve_step"), nth("dve_step"))
                    v.tensor_scalar(p_sq, p_sq, col("subln"), 1.0 - LAMBDA_INIT, ALU.mult, ALU.mult) \
                        .then_inc(sig("dve_step"), 1)
                    dve.wait_ge(sig("dve_step"), nth("dve_step"))
                    v.tensor_tensor(p_sq, p_sq, gate, ALU.mult).then_inc(sig("dve_step"), 1)
                    dve.wait_ge(sig("dve_step"), nth("dve_step"))
                    v.tensor_tensor(y, M[:, 3, :], p_sq, ALU.mult).then_inc(sig("at_y"), 1)
                    dve.wait_ge(sig("at_y"), nth("at_y"))
                else:
                    dve.wait_ge(sig("at_o"), t0 + 1)
                    v.tensor_tensor(y, M[:, 3, :], gate, ALU.mult).then_inc(sig("at_y"), 1)
                    dve.wait_ge(sig("at_y"), nth("at_y"))

            v.memset(tiny[:, 0:96], 0.0).then_inc(sig("tiny_zero"), 1)
            dve.wait_ge(sig("tiny_zero"), 1)
            v.memset(tiny[:, 20:21], EPS)
            v.memset(tiny[:, 21:22], 64e-5)
            v.memset(tiny[:, 22:23], 1.0).then_inc(sig("tiny_set"), 1)
            v.memset(tiny[:, 80:81], 0.0).then_inc(sig("merge_read"), 2)
            v.memset(tiny[:, 81:82], 0.0).then_inc(sig("res_add"), 2)
            v.memset(tiny[:, 82:83], 0.0).then_inc(sig("up_read"), 2)
            v.memset(tiny[:, 83:84], 0.0).then_inc(sig("ffn_act"), 2)
            dve.wait_ge(sig("x_squares"), 1)
            v.tensor_reduce(sq_sum[:, :], W[:, 0:4096].rearrange("p (k t) -> p t k", k=KT), AX.X, ALU.add) \
                .then_inc(sig("x_sq"), 1)
            dve.wait_ge(sig("x_sq"), nth("x_sq"))
            dve.wait_ge(sig("cols_in"), 16)
            norm_apply(0, "attn_norm")
            nsa_blocks()
            dve.wait_ge(sig("const1_in"), 16)
            dve.wait_ge(sig("block_out"), 12)
            nsa_norms()
            nsa_small()
            nsa_softmax(0)
            nsa_softmax(1)
            lru()
            lru_b()
            gla()
            rwkv_feat()
            for r in range(2):
                rwkv_pair(r)
                rwkv_levels(r)
                for c in (2 * r, 2 * r + 1):
                    rwkv_chunk(c)
            rwkv_norm()
            gv = G[:, :].rearrange("p (b n t) -> p b n t", b=4, n=KT)
            with dve.Fori(0, KT // 2) as it:
                for u in range(2):
                    n = u + 2 * it
                    dve.wait_ge(sig("gate_sig"), n + 1)
                    dve.wait_ge(sig("slab_done"), G_BRANCH + u + 1 + 2 * it)
                    v.tensor_tensor(merge_tmp, bank(2 * u, 2).rearrange("p (b t) -> p b t", b=4), gv[:, :, n, :],
                                    ALU.mult).then_inc(sig("merge_read"), 1)
                    dve.wait_ge(sig("merge_read"), u + 3 + 2 * it)
                    v.tensor_reduce(h_sb[:, n, :], merge_tmp.rearrange("p b t -> p t b"), AX.X, ALU.add) \
                        .then_inc(sig("merged"), 1)
                    dve.wait_ge(sig("merged"), u + 1 + 2 * it)

            def add_blocks(g_first, per, nth):
                with dve.Fori(0, KT // 2) as it:
                    for u in range(2):
                        n = u + 2 * it
                        dve.wait_ge(sig("slab_done"), g_first + per * (u + 1) + 2 * per * it)
                        v.tensor_tensor(x_sb[:, n, :], x_sb[:, n, :], stream[:, u, 0:S], ALU.add) \
                            .then_inc(sig("res_add"), 1)
                dve.wait_ge(sig("res_add"), 2 + KT * (nth + 1))

            add_blocks(G_OUT, 1, 0)
            norm_apply(1, "ffn_norm")
            act_v = G[:, 0:FB * S].rearrange("p (k t) -> p k t", k=FB)
            with dve.Fori(0, FB // 2) as it:
                for u in range(2):
                    i = u + 2 * it
                    dve.wait_ge(sig("ffn_tap"), 2 * u + 2 + 4 * it)
                    for back in (1, 2):
                        for w in range(2):
                            b = up_bank[2 * u + w]
                            ins = v.scalar_tensor_tensor(
                                ffn_buf[:, u, w, back:S], b[:, 0:S - back],
                                cv[:, bass.ds(COLS["fconv_w"][0] + (2 - back) * 2 * FB + FB * w + i, 1)],
                                ffn_buf[:, u, w, back:S], ALU.mult, ALU.add)
                            if (back, w) == (1, 1):
                                ins.then_inc(sig("ffn_mid"), 1)
                            if (back, w) == (2, 1):
                                ins.then_inc(sig("up_read"), 1)
                        if back == 1:
                            dve.wait_ge(sig("ffn_mid"), u + 1 + 2 * it)
                    dve.wait_ge(sig("ffn_silu"), u + 1 + 2 * it)
                    v.tensor_tensor(act_v[:, i, :], ffn_buf[:, u, 0, :], ffn_buf[:, u, 1, :], ALU.mult) \
                        .then_inc(sig("ffn_act"), 1)
            add_blocks(G_DOWN, DOWN_SLABS, 1)
            norm_apply(2, "norm2_0")
            lt = tiny[:, 40:72]
            for i in range(2):
                v.tensor_tensor(lt, col("dlam", 64 * i, 32), col("dlam", 64 * i + 32, 32), ALU.mult) \
                    .then_inc(sig("dve_step"), 1)
                dve.wait_ge(sig("dve_step"), nth("dve_step"))
                v.tensor_reduce(tiny[:, 24 + i:25 + i], lt, AX.X, ALU.add) \
                    .then_inc(sig("lam_dot0" if i == 0 else "lam_dot"), 1)
                dve.wait_ge(sig("lam_dot0" if i == 0 else "lam_dot"), nth("lam_dot0" if i == 0 else "lam_dot"))
            v.memset(ones_row, 1.0).then_inc(sig("dve_step"), 1)
            dve.wait_ge(sig("dve_step"), nth("dve_step"))
            for layer in range(2):
                attention(layer, 0)
                attention(layer, 1)
                for s in range(4):
                    dve.wait_ge(sig("slab_done"), G_OUT2[layer] + s + 1)
                    for n in range(4):
                        v.tensor_tensor(x_sb[:, 4 * s + n, :], x_sb[:, 4 * s + n, :],
                                        bank(2 * (s % 2), 2)[:, S * n:S * (n + 1)], ALU.add) \
                            .then_inc(sig("res_add"), 1)
                dve.wait_ge(sig("res_add"), 2 + KT * (3 + layer))
                norm_apply(3 + layer, "norm2_1" if layer == 0 else "final")


def _constants():
    i = np.arange(P)
    c1 = np.zeros((P, N_CONST1), np.float32)
    c1[:, C_ID:C_ID + P] = np.eye(P)
    c1[:, C_ONES:C_ONES + P] = 1.0
    s, t = i[:, None], i[None, :]
    same = s // 64 == t // 64
    c1[:, C_BLK:C_BLK + P] = same
    c1[:, C_STRICT:C_STRICT + P] = same & (s < t)
    c1[:, C_INCL:C_INCL + P] = same & (s <= t)
    for n in range(6):
        b = 1 << n
        c1[:, C_LEVEL + P * n:C_LEVEL + P * (n + 1)] = (s // (2 * b) == t // (2 * b)) & (s // b % 2 == 0) & (t // b % 2 == 1)
    c1[:, C_RESET:C_RESET + S] = (np.arange(S) % 64 != 0)

    c2 = np.zeros((P, N_CONST2), np.float32)
    tok = np.arange(S)
    for width, at_r, at_c, at_s in ((64, C2_R64, C2_COS64, C2_SIN64), (32, C2_R32, C2_COS32, C2_SIN32)):
        half = width // 2
        for p in range(P):
            first = p % width < half
            c2[p + half if first else p - half, at_r + p] = -1.0 if first else 1.0
        inv = (10000.0 ** (-np.arange(half, dtype=np.float32) / half)).astype(np.float32)
        ang = inv[i % half][:, None] * tok[None, :].astype(np.float32)
        c2[:, at_c:at_c + S] = np.cos(ang)
        c2[:, at_s:at_s + S] = np.sin(ang)
    dist = i[:, None] + P - np.arange(S)[None, :]
    c2[:, C2_CAUSAL:C2_CAUSAL + S] = np.where(dist >= 0, 0.0, NEG)
    times = (dist >= 0) * ((dist <= 128) * 1 + (dist % 4 == 0) * 1 + (dist % 16 == 0) * 1)
    c2[:, C2_DIL:C2_DIL + S] = np.where(times > 0, np.log(np.maximum(times, 1)), NEG)
    c2[:, C2_STRICT:C2_STRICT + S] = np.where(dist > 0, 0.0, NEG)
    c2[:, C2_BEFORE:C2_BEFORE + S] = dist > 0

    bucket = np.zeros((32, 1024), np.float32)
    d = 255 - np.arange(511)
    n = np.maximum(d, 0)
    nf = np.maximum(n, 1).astype(np.float32)
    large = 16 + (np.log(nf / np.float32(16)) / np.float32(math.log(128 / 16)) * np.float32(16)).astype(np.int32)
    which = np.where(n < 16, n, np.minimum(large, 31))
    bucket[which, np.arange(511)] = 1.0
    bucket[:, 512:512 + 511] = np.where(d >= 0, 0.0, NEG)[None, :]
    return c1, c2, bucket


def _slabs(w, kt):
    n = w.shape[1] // P
    return np.ascontiguousarray(w.reshape(kt, P, n, P).transpose(2, 1, 0, 3))


def kernel(**inputs):
    import concourse.bacc as _bacc
    from concourse import mybir as _mybir
    from concourse.bass_utils import run_bass_kernel_spmd as _run

    a = {k: np.asarray(v) for k, v in inputs.items()}

    def vec(x):
        x = np.asarray(x).reshape(-1)
        return x.reshape(-1, P).T

    def padded(x, n):
        o = np.zeros(n, np.float32)
        o[:x.shape[0]] = x
        return o

    w = a["w_in"][0]
    wm = np.zeros((D, N_MIX * P), np.float32)
    wm[:, 0:16] = w[:, 1536:1552]
    wm[:, GATE_ROW:GATE_ROW + 12] = w[:, 3856:3868]
    for b, lo, hi in ((B_KV, 3088, 3856), (B_Q, 2576, 3088), (B_LX, 1552, 2576), (B_GQ, 0, 1536),
                      (B_R, 3868, 5404), (B_XW, 5404, 5500), (B_XA, 5500, 5596), (B_XG, 5596, 5852)):
        wm[:, P * b:P * b + hi - lo] = w[:, lo:hi]
    mu = a["rwkv_mu"][0]
    mu = np.concatenate([mu[:1536], padded(mu[1536:1632], P), padded(mu[1632:1728], P), mu[1728:]])
    parts = {
        "attn_norm": vec(a["attn_norm"]), "ffn_norm": vec(a["ffn_norm"]), "norm2_0": vec(a["norm_g_2"][0]),
        "norm2_1": vec(a["norm_g_2"][1]), "final": vec(a["final_norm_g_2"]), "gk_b": vec(a["gla_b_gk"]),
        "gla_gain": vec(a["gla_out_norm"]), "conv_w": vec(a["lru_conv_w"]), "conv_b": vec(a["lru_conv_b"]),
        "b_a": vec(a["lru_b_a"]), "b_i": vec(a["lru_b_i"]), "lam": vec(a["lru_lambda"]),
        "q_gain": vec(a["nsa_q_norm"]), "k_gain": vec(a["nsa_k_norm"]), "mu": vec(mu), "w0": vec(a["rwkv_w0"]),
        "a0": vec(a["rwkv_a0"]), "k_k": vec(a["rwkv_k_k"]), "k_a": vec(a["rwkv_k_a"]), "r_k": vec(a["rwkv_r_k"]),
        "ln_w": vec(a["rwkv_ln_w"]), "ln_b": vec(a["rwkv_ln_b"]), "fconv_w": vec(a["ffn_conv_w"]),
        "fconv_b": vec(a["ffn_conv_b"]), "dlam": np.broadcast_to(a["diff_lam_2"].reshape(1, -1), (P, 128)),
        "subln": np.tile(a["diff_subln_g_2"].reshape(-1), 2)[:, None], "pos": a["nsa_cmp_pos"][0].T,
    }
    cols = np.zeros((P, N_COLS), np.float32)
    for name, (at, n) in COLS.items():
        cols[:, at:at + n] = parts[name]
    small = np.zeros((P, N_SMALL), np.float32)

    def put(name, x):
        at, n = SMALL[name]
        small[:x.shape[0], at:at + n] = x

    put("w_gk", a["gla_w_gk"][0])
    put("lru_a", a["lru_w_a"][0].transpose(1, 0, 2).reshape(P, 512))
    put("lru_i", a["lru_w_i"][0].transpose(1, 0, 2).reshape(P, 512))
    put("w_lora", a["rwkv_w_lora"][0])
    put("a_lora", a["rwkv_a_lora"][0])
    put("g_lora", a["rwkv_g_lora"][0].reshape(2, P, 512).transpose(1, 0, 2).reshape(P, 1024))
    put("cmp_k2", a["nsa_cmp_k2"][0])
    put("cmp_v2", a["nsa_cmp_v2"][0])
    put("rel", a["rel_bias"])
    c1, c2, bucket = _constants()

    up = _slabs(a["ffn_up"][0], KT)
    up = up.reshape(2, FB, P, KT, P).transpose(1, 0, 2, 3, 4).reshape(2 * FB, P, KT, P)
    down = _slabs(a["ffn_down"][0], FB).reshape(KT, P, DOWN_SLABS, DOWN_K, P).transpose(0, 2, 1, 3, 4)
    branch = a["w_branch"][0].reshape(4, 4, P, KT, P).transpose(3, 2, 0, 1, 4).reshape(KT, P, KT, P)
    out2 = a["w_out_2"].reshape(2, 4, P, 4, 4, P).transpose(0, 3, 2, 4, 1, 5).reshape(8, P, KT, P)
    arrays = {
        "xT": a["x"][0].T.reshape(KT, P, S).transpose(1, 0, 2),
        "cols": cols, "small": small, "const1": c1, "const2": c2, "bucket": bucket,
        "flip": np.ascontiguousarray(np.eye(P, dtype=np.float32)[::-1]),
        "w_mix": _slabs(wm, KT),
        "w_cmp": np.concatenate([a[n][0].reshape(2, KT, P, P).transpose(0, 2, 1, 3)
                                 for n in ("nsa_cmp_k1", "nsa_cmp_v1")]),
        "w_gate": _slabs(w[:, 5852:], KT), "w_branch": branch, "w_out": _slabs(a["w_out"][0], KT),
        "w_up": up, "w_down": down.reshape(KT * DOWN_SLABS, P, DOWN_K, P),
        "w_in2": np.concatenate([_slabs(a["w_in_2"][n], KT) for n in range(2)]), "w_out2": out2,
    }
    nc = _bacc.Bacc("TRN2", target_bir_lowering=False, num_devices=1)
    args = {}
    for name, x in arrays.items():
        x = np.ascontiguousarray(x)
        arrays[name] = x
        args[name] = nc.dram_tensor(name, x.shape, _mybir.dt.from_np(x.dtype), kind="ExternalInput").ap()
    args["bias_scratch"] = nc.dram_tensor("bias_scratch", (4, 512), F32, kind="Internal").ap()
    args["out"] = nc.dram_tensor("outT", (P, KT, S), F32, kind="ExternalOutput").ap()
    build(nc, **args)
    got = _run(nc, [arrays], core_ids=[0]).results[0]["outT"]
    return np.ascontiguousarray(got.transpose(1, 0, 2).reshape(D, S).T)[None]
```

```python
import math
from contextlib import ExitStack

import numpy as np

import concourse.bass as bass
from concourse import mybir

F32 = mybir.dt.float32
F32R = mybir.dt.float32r
ALU = mybir.AluOpType
ACT = mybir.ActivationFunctionType
AX = mybir.AxisListType

P = 128
S = 256
D = 2048
KT = D // P
FF = 5632
FB = FF // P
DOWN_K = 11
DOWN_SLABS = FB // DOWN_K
RING = 4
SLAB = KT * P
NEG = -1.0e9
PRE = 1280
EPS = 1e-6
KAPPA = -math.exp(-0.5)
LAMBDA_INIT = 0.8 - 0.6 * math.exp(-0.3)

B_MISC, B_KV, B_Q, B_LX, B_LG = 0, 1, 7, 11, 15
B_GQ, B_GK, B_GV, B_GG = 19, 21, 23, 27
B_R, B_K, B_V, B_XW, B_XA, B_XG = 31, 35, 39, 43, 44, 45
N_MIX = 47
N_GATES = 64
GATE_ROW = 32

G_IN_A = 0
G_CMP = 12
G_IN_B = 16
G_GATES = G_IN_B + N_MIX - 12
G_BRANCH = G_GATES + N_GATES
G_OUT = G_BRANCH + KT
G_UP = G_OUT + KT
G_DOWN = G_UP + 2 * FB
G_IN2 = [G_DOWN + KT * DOWN_SLABS, G_DOWN + KT * DOWN_SLABS + KT + 4]
G_OUT2 = [G_IN2[0] + KT, G_IN2[1] + KT]
G_END = G_OUT2[1] + 4
MIX_GATES = 36
G_SPLIT = G_GATES + MIX_GATES
UNITS = 4
ATTENTIONS = (0, 1, 3, 2)
MORE = ((2, 1, 2, 1, 2), (0, 0, 2, 0, 0), (1, 1, 4, 1, 1), (0, 0, 2, 0, 0))
CHUNK_HALVES = (2, 3, 2, 2)
DOWN_UNITS = (4, 4, 3)


def unit_tiles(g):
    return DOWN_UNITS if G_DOWN <= g < G_IN2[0] else (4, 4, 4, 4)


def units(g):
    n = 4 * (min(g, G_DOWN) - G_SPLIT)
    if g > G_DOWN:
        n += 3 * (min(g, G_IN2[0]) - G_DOWN)
    return n + (4 * (g - G_IN2[0]) if g > G_IN2[0] else 0)

ROOT = {name: i + 1 for i, name in enumerate(
    (("norm", 0), "nsa_root", "kc_root", "lru_root", "gla_root", "rw_kkroot", "rw_yroot", ("norm", 1), ("norm", 2),
     ("norm", 3), "at_oroot", ("norm", 4)))}

COLS = {}


def _columns():
    at = 0
    for name, n in (("attn_norm", 16), ("ffn_norm", 16), ("norm2_0", 16), ("norm2_1", 16), ("final", 16),
                    ("gk_b", 2), ("gla_gain", 1), ("conv_w", 16), ("conv_b", 4), ("b_a", 4), ("b_i", 4),
                    ("lam", 4), ("q_gain", 1), ("k_gain", 1), ("mu", 16), ("w0", 4), ("a0", 4), ("k_k", 4),
                    ("k_a", 4), ("r_k", 4), ("ln_w", 4), ("ln_b", 4), ("fconv_w", 6 * FB), ("fconv_b", 2 * FB),
                    ("dlam", 128), ("subln", 1), ("pos", 32)):
        COLS[name] = (at, n)
        at += n
    return at


N_COLS = _columns()

SMALL = {"w_gk": (0, 256), "lru_a": (256, 512), "lru_i": (768, 512), "w_lora": (1280, 512),
         "a_lora": (1792, 512), "g_lora": (2304, 1024), "cmp_k2": (3328, 128), "cmp_v2": (3456, 128),
         "rel": (3584, 4)}
N_SMALL = 3588

C_ID, C_ONES, C_BLK, C_STRICT, C_INCL, C_LEVEL, C_RESET = 0, 128, 256, 384, 512, 640, 1408
N_CONST1 = 1664
C2_R64, C2_R32, C2_COS64, C2_SIN64, C2_COS32, C2_SIN32 = 0, 128, 256, 512, 768, 1024
C2_CAUSAL, C2_DIL, C2_STRICT, C2_BEFORE = 1280, 1536, 1792, 2048
N_CONST2 = 2304


def build(nc, xT, cols, small, const1, const2, bucket, flip, w_mix, w_cmp, w_gate, w_branch, w_out, w_up, w_down,
          w_in2, w_out2, bias_scratch, out):
    ctx = ExitStack()
    with ctx:
        def sb(name, shape):
            return ctx.enter_context(nc.sbuf_tensor(name, shape, F32))

        signals = {}

        def sig(name):
            if name not in signals:
                signals[name] = ctx.enter_context(nc.semaphore(name))
            return signals[name]

        ring = sb("ring", [P, RING, KT, P])
        x_sb = sb("x_sb", [P, KT, S])
        c1 = sb("c1", [P, N_CONST1])
        cv = sb("cv", [P, N_COLS])
        sq_wide = sb("sq_wide", [P, 2 * S])
        rs = sq_wide[:, 0:S]
        sq_sum = sq_wide[:, S:2 * S]
        tiny = sb("tiny", [P, 96])
        z_base = nc.sbuf_base
        G = sb("G", [P, 16384])
        h_sb = sb("h_sb", [P, KT, S])
        y_sb = sb("y_sb", [P, KT, S])
        W = sb("W", [P, PRE + 256 * N_MIX])
        Q = nc.alloc_sbuf_tensor_at("Q", [P, 15872], F32, offset=z_base + 4 * 8192)

        def halves(name, a, b, k, t=S):
            return [nc.alloc_sbuf_tensor_at(name + part, [P, k, t], F32R, offset=z_base + 4 * at)
                    for part, at in (("_hi", a), ("_lo", b))]

        y2_hi, y2_lo = halves("branches", 16384, 20480, KT)
        m_hi, m_lo = halves("merged", 24576, 28672, KT)
        h_hi, h_lo = halves("normed", 0, 4096, KT)
        a_hi, a_lo = halves("ffn_act", 8192, 8192 + FB * S, FB)
        w_hi, w_lo = halves("weights", 32768, 34816, UNITS, 512)
        py_hi, py_lo = halves("attn_out", 24064, 25088, 4)
        stream = ctx.enter_context(nc.psum_tensor("stream", [P, 2, 512], F32))
        M = ctx.enter_context(nc.psum_tensor("M", [P, 6, 512], F32))

        ident = c1[:, C_ID:C_ID + P]
        ones = c1[:, C_ONES:C_ONES + P]
        blk64 = c1[:, C_BLK:C_BLK + P]
        strict_incl = c1[:, C_STRICT:C_STRICT + 256]
        incl = c1[:, C_INCL:C_INCL + P]
        reset = c1[:, C_RESET:C_RESET + S]

        def level(n):
            return c1[:, C_LEVEL + P * n:C_LEVEL + P * (n + 1)]

        def col(name, i=0, n=1):
            a = COLS[name][0] + i
            return cv[:, a:a + n]

        def spread(ap, n):
            return ap.unsqueeze(2).to_broadcast([P, ap.shape[1], n])

        def over(ap, n):
            return ap.unsqueeze(1).to_broadcast([P, n, ap.shape[1]])

        def blocks(b, n=1):
            return W[:, PRE + 256 * b:PRE + 256 * (b + n)]

        def g_at(a, n):
            return G[:, a:a + n]

        def w_at(a, n):
            return W[:, a:a + n]

        def bank(a, n=1):
            return M[:, a:a + n, :].rearrange("p a b -> p (a b)")

        sm0 = 12796

        def small_w(name, a=0, n=None):
            o, w = SMALL[name]
            return G[:, sm0 + o + a:sm0 + o + (a + n if n is not None else w)]

        n_bias = g_at(0, 1024).rearrange("p (h s) -> p h s", h=4)
        n_vtok = g_at(1024, 512).rearrange("p (a t d) -> p a t d", a=2, t=2)
        n_prob = g_at(1536, 2048)
        n_probT = g_at(3584, 2048)
        n_sq, n_rs = g_at(1536, 1536), g_at(3584, 1536)
        n_hot, n_ext = g_at(5120, 1024), g_at(6144, 512)
        n_blk = g_at(5632 + 1536 + 4096, 960)
        n_pcT = g_at(5632, 1024)
        n_vc, n_hk, n_hv, n_kc, n_kc2 = (g_at(6656, 128), g_at(6784, 16), g_at(6800, 16), g_at(6816, 16),
                                         g_at(6832, 16))
        n_gate = g_at(6848, 24)
        n_hT = g_at(8192, 2 * P)
        n_pc = g_at(6872, 64)
        n_nmax, n_sum, n_wt = g_at(6936, 12), g_at(6948, 12), g_at(6960, 12)
        n_flip, n_skew = g_at(12224, P), g_at(7168, 1024)
        l_xc, l_a, l_u, l_t = g_at(7168, 1024), g_at(8192, 1024), g_at(9216, 1024), g_at(10240, 1024)
        a_b, a_e1, a_e2, a_eb = g_at(0, 512), g_at(512, 512), g_at(1024, 512), g_at(1536, 512)
        a_qs, a_ks, a_qi, a_kl = g_at(2048, 512), g_at(2560, 512), g_at(3072, 512), g_at(3584, 512)
        a_kltok = g_at(4096, 512).rearrange("p (r f) -> p r f", r=2)
        a_vtok = g_at(4608, 1024).rearrange("p (r h v) -> p r h v", r=2, h=4)
        a_sc = g_at(5632, 1024).rearrange("p (h r t) -> p h r t", h=4, r=2)
        a_st = g_at(6656, 768).rearrange("p (j c v) -> p j c v", j=2, c=3)
        a_o, a_sq = g_at(512, 1024), g_at(1536, 1024)
        a_bm = g_at(7424, 512)
        r_sig, r_a, r_g, r_kk = w_at(0, 1024), w_at(1024, 1024), w_at(2048, 1024), w_at(3072, 1024)
        r_qr = w_at(4096, 2048).rearrange("p (j r q t) -> p j r q t", j=4, r=2, q=2)
        r_p, r_kt, r_bonus = w_at(6144, 1024), w_at(7168, 1024), w_at(8192, 1024)
        r_rhs = blocks(B_XG, 2)
        r_shift = g_at(8192, 4096)
        r_cs = blocks(B_XG - 2, 4)
        r_ar = g_at(8192, 2048).rearrange("p (h t) -> p h t", h=8)
        r_bk = g_at(10240, 2048).rearrange("p (h t) -> p h t", h=8)
        r_x, r_xt, r_t1 = g_at(12796, 1024), g_at(13820, 1024), g_at(14844, 1024)
        r_stc = [blocks(b).rearrange("p (j i) -> p j i", j=4) for b in (B_XW, B_XA)]
        r_dec = g_at(16124, 16).rearrange("p (j c) -> p j c", j=4)
        r_mt = r_kk

        def hm(hd):
            return 4 * (hd % 2) + hd // 2

        r_vtok, r_ptok = w_at(1024, 512), w_at(1536, 512)
        r_ktok = blocks(B_R, 2)
        r_u = blocks(B_R + 2, 2)
        r_y = blocks(B_K, 4)
        r_tmp = w_at(0, 1024)

        def c2(a, n):
            return W[:, 1536 + a:1536 + a + n]

        def q_at(a, n):
            return Q[:, a:a + n]

        def p_blocks(b, n=1):
            return q_at(S * b, S * n)

        p_probs = [q_at(4096, 1024), q_at(5120, 2048)]
        p_probT, p_vtok = q_at(7168, 1536), q_at(8704, 512)
        p_o, p_sq, p_tmp = q_at(11264, 1024), q_at(12288, 512), q_at(12800, 3072)
        p_stat = q_at(10240, 96)

        def prob(t):
            return two_tiles(q_at(4096, 1536), t)

        def prob_maps(maps, t):
            return p_probs[t].rearrange("p (m s) -> p m s", m=8) if maps == 8 else prob(t)

        def logit_banks(rows, t):
            if rows == 4:
                return [M[:, 0, :], M[:, 1, :], stream[:, 0, :], stream[:, 1, :]] if t == 0 else \
                    [M[:, 2 + i, :] for i in range(4)]
            return [M[:, 1, :], M[:, 3, :]] if t == 0 else [M[:, 4, :], M[:, 5, :]]

        def am(hd):
            return 2 * (hd % 2) + hd // 2

        p_stick = W[:, 3840:5376]

        def two_tiles(ap, t):
            return ap[:, 512 * t:512 + 1024 * t].rearrange("p (m s) -> p m s", m=4)

        def stick_z(t):
            return two_tiles(q_at(4096, 1536), t)

        def stick_s(t):
            return two_tiles(p_tmp[:, 0:1536], t)

        def stick_r(t):
            return two_tiles(p_stick, t)

        def diff_tmp(t):
            return two_tiles(p_tmp[:, 0:1536], t)

        ones_row = W[:, 5376:5632]
        pair_sq = W[:, 12288:13312].rearrange("p (u t) -> p u t", u=2)
        pool_sq = W[:, 13056:13312]
        act32 = W[:, 7424:7936].rearrange("p (u t) -> p u t", u=2)
        norm_tmp = W[:, 12288:13312].rearrange("p (u t) -> p u t", u=4)
        o_sb = q_at(0, 4096).rearrange("p (k t) -> p k t", k=KT)
        merge_tmp = W[:, 12288:13312].rearrange("p (b t) -> p b t", b=4)
        ffn_buf = W[:, 6144:7168].rearrange("p (u v t) -> p u v t", u=2, v=2)
        up_bank = [stream[:, 0, 0:S], stream[:, 1, 0:S], M[:, 2, 0:S], M[:, 3, 0:S]]
        r_y2, r_ssum = g_at(11264, 1024), w_at(0, 256).rearrange("p (j i) -> p j i", j=4)
        written = {}

        def nth(name):
            written[name] = written.get(name, 0) + 1
            return written[name]

        def fill(g, it=0):
            return 16 * (g // RING + 1) + 16 * it

        def slot_in(g):
            return sig(f"slab_in_slot{g % RING}")

        def unit(g, j, it=0, step=RING):
            return units(g) + j + (units(g + step) - units(g)) * it

        def slab_done(g, it=0, step=RING):
            return UNITS + unit(g, len(unit_tiles(g)), it, step)

        def pair_sums(layer, m):
            return 2 * (2 * KT - 1) + (KT // 2 - 1) * layer + m

        block = ctx.enter_context(nc.Block())

        @block.sync
        def _(sp):
            sp.dma_start(x_sb[:], xT).then_inc(sig("x_in"), 16)
            sp.dma_start(cv[:], cols).then_inc(sig("cols_in"), 16)
            sp.dma_start(c1[:], const1).then_inc(sig("const1_in"), 16)

            def load(g, src, it=0, free=0, n=KT):
                if free or g >= RING:
                    sp.wait_ge(sig("slab_done"), g - RING + 1 + RING * it)
                sp.dma_start(ring[:, g % RING, 0:n, :], src).then_inc(slot_in(g), 16)

            def load_run(g0, dram, first, groups, n=KT):
                with sp.Fori(0, groups) as it:
                    for u in range(RING):
                        src = dram[first + u + RING * it]
                        load(g0 + u, src, it, 1, n)

            for b in range(RING):
                load(G_IN_A + b, w_mix[b])
            sp.dma_start(G[:, sm0:sm0 + N_SMALL], small).then_inc(sig("small_in"), 16)
            load_run(G_IN_A + RING, w_mix, RING, 2)
            load_run(G_CMP, w_cmp, 0, 1)
            load_run(G_IN_B, w_mix, 12, 8)
            for b in range(44, N_MIX):
                load(G_IN_B + b - 12, w_mix[b])
            load_run(G_GATES, w_gate, 0, MIX_GATES // RING)

            def load_split(g, src, it=0, n=KT, step=RING):
                if g - RING < G_SPLIT:
                    sp.wait_ge(sig("slab_done"), g - RING + 1)
                else:
                    sp.wait_ge(sig("lo_ready"), unit(g - RING, len(unit_tiles(g - RING)), it, step))
                sp.dma_start(ring[:, g % RING, 0:n, :], src).then_inc(slot_in(g), 16)

            def load_split_run(g0, dram, first, groups, n=KT):
                for u in range(RING):
                    load_split(g0 + u, dram[first + u], 0, n)
                if groups == 1:
                    return
                with sp.Fori(0, groups - 1) as it:
                    for u in range(RING):
                        load_split(g0 + RING + u, dram[first + RING + u + RING * it], it, n)

            load_split_run(G_SPLIT, w_gate, MIX_GATES, (N_GATES - MIX_GATES) // RING)
            load_split_run(G_BRANCH, w_branch, 0, KT // RING)
            load_split_run(G_OUT, w_out, 0, KT // RING)
            load_split_run(G_UP, w_up, 0, 2 * FB // RING)
            load_split_run(G_DOWN, w_down, 0, KT * DOWN_SLABS // RING, DOWN_K)
            for layer in range(2):
                load_split_run(G_IN2[layer], w_in2, KT * layer, KT // RING)
                load_split_run(G_OUT2[layer], w_out2, 4 * layer, 1)
            for q in range(4):
                sp.wait_ge(sig("h_ready"), KT * 4 + 4 * (q + 1))
                sp.dma_start(out[:, 4 * q:4 * q + 4, :], o_sb[:, 4 * q:4 * q + 4, :]).then_inc(sig("out_done"), 16)
            sp.wait_ge(sig("out_done"), 64)

        @block.gpsimd
        def _(pool):
            pool.dma_start(n_hot[0:32, :], bucket).then_inc(sig("tables_in"), 16)
            pool.dma_start(n_flip, flip).then_inc(sig("tables_in"), 16)
            pool.wait_ge(sig("bias_row"), 1)
            pool.dma_start(bias_scratch, n_ext[0:4, :]).then_inc(sig("bias_out"), 16)
            pool.wait_ge(sig("bias_out"), 16)
            skewed = bass.AP(bias_scratch.tensor, 0, [[1, P], [512, 4], [1, S]])
            pool.dma_start(n_skew.rearrange("p (h s) -> p h s", h=4), skewed).then_inc(sig("bias_in"), 16)
            gv = G.rearrange("p (b n t) -> p b n t", b=4, n=KT)
            with pool.Fori(0, KT) as it:
                pool.wait_ge(sig("merge_read"), 3 + it)
                nc.gpsimd.tensor_tensor(merge_tmp[:, 0:2, :], merge_tmp[:, 0:2, :], merge_tmp[:, 2:4, :], ALU.add) \
                    .then_inc(sig("merge_half"), 1)
                pool.wait_ge(sig("merge_half"), 1 + it)
                nc.gpsimd.tensor_tensor(gv[:, 0, it, :], merge_tmp[:, 0, :], merge_tmp[:, 1, :], ALU.add) \
                    .then_inc(sig("merge_sum"), 1)

            done = [0]

            def squares(first, n):
                pool.wait_ge(sig("norm_sum"), first // KT + 1)

                def one(u, it):
                    pool.wait_ge(sig("res_add"), 2 + first + u + 1 + it)
                    xb = x_sb[:, u + it, :]
                    if u == 0:
                        nc.gpsimd.tensor_tensor(sq_sum[:, :], xb, xb, ALU.mult).then_inc(sig("pool_sq"), 1)
                        return
                    pool.wait_ge(sig("pool_sq"), done[0] + 1 + 2 * (u - 1) + 2 * it)
                    nc.gpsimd.tensor_tensor(pool_sq[:, :], xb, xb, ALU.mult).then_inc(sig("pool_sq"), 1)
                    pool.wait_ge(sig("pool_sq"), done[0] + 2 + 2 * (u - 1) + 2 * it)
                    nc.gpsimd.tensor_tensor(sq_sum[:, :], sq_sum[:, :], pool_sq[:, :], ALU.add) \
                        .then_inc(sig("pool_sq"), 1)
                one(0, 0)
                with pool.Fori(0, n - 1) as it:
                    one(1, it)
                done[0] += 2 * n - 1

            for n in range(2):
                squares(KT * n, KT)
                if n == 1:
                    pool.wait_ge(sig("norm_sum"), 3)
                    pool.dma_start(c2(0, N_CONST2), const2).then_inc(sig("const2_in"), 16)
            for layer in range(2):
                for m in range(1, KT // 2):
                    pool.wait_ge(sig("x_squares"), 4 + KT // 2 * layer + m + 1)
                    if m > 1:
                        pool.wait_ge(sig("pool_sq"), pair_sums(layer, m - 1))
                    nc.gpsimd.tensor_tensor(sq_wide[:, :], sq_wide[:, :], pair_sq[:, m % 2, :], ALU.add) \
                        .then_inc(sig("pool_sq"), 1)

        @block.tensor
        def _(pe):
            mm = nc.tensor.matmul

            def block_sum(dst, src, w):
                n = src.shape[1]
                for a in range(0, n, 512):
                    last = mm(dst[:, a:min(a + 512, n)], w, src[:, a:min(a + 512, n)], start=True, stop=True)
                return last

            def norm_sum(k):
                if k == 0:
                    for q in range(4):
                        pe.wait_ge(sig("x_sq"), q + 1)
                        last = mm(M[:, 0, 0:S], ones, W[:, 4096 + S * q:4096 + S * (q + 1)], start=q == 0, stop=q == 3)
                    last.then_inc(sig("norm_sum"), 1)
                    return
                if k < 3:
                    pe.wait_ge(sig("pool_sq"), (2 * KT - 1) * k)
                else:
                    pe.wait_ge(sig("pool_sq"), pair_sums(k - 3, KT // 2 - 1))
                    mm(M[:, 0, 0:S], ones, sq_wide[:, 0:S], start=True, stop=False)
                mm(M[:, 0, 0:S], ones, sq_sum, start=k < 3, stop=True).then_inc(sig("norm_sum"), 1)

            def slab(g, out_ap, rhs, it=0, n=KT, start=True, stop=True, ready=None):
                pe.wait_ge(slot_in(g), fill(g, it))
                for k in range(n):
                    if ready is not None:
                        pe.wait_ge(sig(ready[0]), ready[1] + k + 1)
                    last = mm(out_ap, ring[:, g % RING, k, :], rhs(k), start=start and k == 0,
                              stop=stop and k == n - 1)
                last.then_inc(sig("slab_done"), 1)

            def h(k):
                return h_sb[:, k, :]

            halves_run = [0]

            def gate_halves(n):
                for _ in range(n):
                    e, part = halves_run[0] // 2, halves_run[0] % 2
                    g = G_GATES + e
                    if part == 0:
                        pe.wait_ge(sig("block_out"), N_MIX + e - 1)
                        pe.wait_ge(slot_in(g), fill(g))
                    for k in range(KT // 2 * part, KT // 2 * (part + 1)):
                        last = mm(stream[:, (N_MIX + e) % 2, 0:S], ring[:, g % RING, k, :], h(k), start=k == 0,
                                  stop=k == KT - 1)
                    if part == 1:
                        last.then_inc(sig("slab_done"), 1)
                    halves_run[0] += 1

            def project(g0, e0, groups, norm=None):
                def one(u, it):
                    if e0 + u >= 2:
                        pe.wait_ge(sig("block_out"), e0 + u - 1 + RING * it)
                    slab(g0 + u, stream[:, (e0 + u) % 2, 0:S], h, it,
                         ready=norm if isinstance(it, int) and u == 0 else None)
                if groups == 1:
                    for u in range(RING):
                        one(u, 0)
                else:
                    with pe.Fori(0, groups) as it:
                        for u in range(RING):
                            one(u, it)

            def nsa_compress():
                pe.wait_ge(sig("cmp_in"), 4)
                for a in range(2):
                    x = n_blk[:, 480 * a:480 * (a + 1)].rearrange("p (l n) -> p l n", n=15)
                    for half in range(2):
                        g = G_CMP + 2 * a + half
                        pe.wait_ge(slot_in(g), fill(g))
                        for k in range(KT):
                            last = mm(M[0:15, a, 0:P], x[:, 16 * half + k, :], ring[:, g % RING, k, :],
                                      start=half == 0 and k == 0, stop=half == 1 and k == KT - 1)
                        last.then_inc(sig("slab_done"), 1)

            def nsa_norms():
                pe.wait_ge(sig("nsa_sq"), 3)
                block_sum(bank(2, 3), n_sq, ones).then_inc(sig("nsa_ssq"), 1)
                for a in range(2):
                    v = blocks(B_KV + 3 + 2 * a)
                    for t in range(2):
                        last = nc.tensor.transpose(M[:, 5, 256 * a + 128 * t:256 * a + 128 * (t + 1)],
                                                   v[:, 128 * t:128 * (t + 1)], ident)
                last.then_inc(sig("nsa_vT"), 1)

            def nsa_small():
                pe.wait_ge(sig("cmp_hidden"), 2)
                for a in range(2):
                    last = mm(M[:, a, 0:15], n_hT[0:15, P * a:P * (a + 1)], ident[0:15, 0:15], start=True, stop=True)
                last.then_inc(sig("cmp_turned"), 1)
                pe.wait_ge(sig("cmp_hidden"), 4)
                pe.wait_ge(sig("nsa_rs"), 1)
                pe.wait_ge(sig("small_in"), 16)
                mm(M[:, 0, 0:15], small_w("cmp_k2"), n_hk[:, 0:15], start=True, stop=True)
                mm(M[0:15, 1, 0:P], n_hv[:, 0:15], small_w("cmp_v2"), start=True, stop=True)
                pe.wait_ge(sig("tables_in"), 32)
                mm(M[0:4, 2, :], small_w("rel")[0:32, :], n_hot[0:32, 0:512], start=True, stop=True)
                for t in range(2):
                    last = nc.tensor.transpose(M[:, 3, 128 * t:128 * (t + 1)],
                                               blocks(B_MISC)[:, 128 * t:128 * (t + 1)], ident)
                last.then_inc(sig("nsa_small"), 1)
                pe.wait_ge(sig("kc_sq"), 1)
                mm(M[:, 4, 0:15], ones, n_kc2[:, 0:15], start=True, stop=True).then_inc(sig("kc_ssq"), 1)

            def nsa_bias():
                pe.wait_ge(sig("bias_in"), 16)
                pe.wait_ge(sig("nsa_vtok"), 1)
                mm(M[:, 5, :], n_flip, n_skew[:, 0:512], start=True, stop=True)
                mm(M[:, 3, :], n_flip, n_skew[:, 512:1024], start=True, stop=True).then_inc(sig("nsa_skew"), 1)

            def nsa_scores(t):
                w = P * (t + 1)
                pe.wait_ge(sig("nsa_qk"), 4)
                pe.wait_ge(sig("nsa_bias"), 1)
                if t == 1:
                    pe.wait_ge(sig("nsa_PT"), 1), pe.wait_ge(sig("nsa_PT_dve"), 1)
                for a in range(2):
                    k = blocks(B_KV + 2 + 2 * a)
                    o = bank(2 * a, 2).rearrange("p (h s) -> p h s", h=4)
                    for hd in range(4):
                        mm(o[:, hd, 0:w], blocks(B_Q + hd)[:, P * t:P * (t + 1)], k[:, 0:w],
                           start=True, stop=True)
                for hd in range(4):
                    last = mm(M[:, 4, 16 * hd:16 * hd + 15], blocks(B_Q + hd)[:, P * t:P * (t + 1)],
                              n_kc[:, 0:15], start=True, stop=True)
                last.then_inc(sig("nsa_logits"), 1)

            def nsa_turn(t):
                pe.wait_ge(sig("nsa_weighted"), t + 1)
                pr = n_prob.rearrange("p (a h s) -> p a h s", a=2, h=4)
                n = 0
                for a in range(2):
                    for hd in range(4):
                        for st in range(t + 1):
                            nc.tensor.transpose(bank(0, 4)[:, P * n:P * (n + 1)],
                                                pr[:, a, hd, P * st:P * (st + 1)], ident)
                            n += 1
                for hd in range(4):
                    last = nc.tensor.transpose(M[0:16, 4, P * hd:P * (hd + 1)], n_pc[:, 16 * hd:16 * hd + 16],
                                               ident)
                last.then_inc(sig("nsa_turned"), 1)

            def nsa_values(t):
                pe.wait_ge(sig("nsa_PT"), t + 1)
                pe.wait_ge(sig("nsa_PT_dve"), t + 1)
                if t == 1:
                    pe.wait_ge(sig("nsa_y"), 1)
                if t == 0:
                    pe.wait_ge(sig("nsa_vtok"), 1)
                for hd in range(4):
                    o = M[:, 5, P * hd:P * (hd + 1)]
                    mm(o, n_vc[0:15, :], n_pcT[0:15, P * hd:P * (hd + 1)], start=True, stop=False)
                    for a in range(2):
                        for st in range(t + 1):
                            n = (a * 4 + hd) * (t + 1) + st
                            last = mm(o, n_vtok[:, a, st, :], n_probT[:, P * n:P * (n + 1)], start=False,
                                      stop=a == 1 and st == t)
                last.then_inc(sig("nsa_o"), 1)

            def lru_gates():
                pe.wait_ge(sig("lru_conv"), 12)
                pe.wait_ge(sig("nsa_y"), 2)
                for j in range(4):
                    mm(bank(0, 2)[:, S * j:S * (j + 1)], small_w("lru_a", P * j, P), l_xc[:, S * j:S * (j + 1)],
                       start=True, stop=True)
                for j in range(4):
                    last = mm(bank(2, 2)[:, S * j:S * (j + 1)], small_w("lru_i", P * j, P),
                              l_xc[:, S * j:S * (j + 1)], start=True, stop=True)
                last.then_inc(sig("lru_pre"), 1)

            def gla_decay():
                pe.wait_ge(sig("lru_gated"), 2)
                for j in range(2):
                    last = mm(M[:, 0, S * j:S * (j + 1)], small_w("w_gk", P * j, P)[0:16, :],
                              blocks(B_MISC)[0:16, :], start=True, stop=True)
                last.then_inc(sig("gla_z"), 1)
                pe.wait_ge(sig("block_out"), B_GV + 4)
                for hd in range(4):
                    for r in range(2):
                        last = nc.tensor.transpose(bank(2, 2)[:, 512 * r + P * hd:512 * r + P * (hd + 1)],
                                                   blocks(B_GV + hd)[:, P * r:P * (r + 1)], ident)
                last.then_inc(sig("gla_vT"), 1)

            def gla_scores():
                pe.wait_ge(sig("gla_qk"), 4)
                for hd in range(4):
                    lo, j = 64 * (hd % 2), hd // 2
                    for r in range(2):
                        c = S * j + P * r
                        last = mm(M[:, hd % 2, (2 * j + r) * P:(2 * j + r + 1) * P], a_ks[lo:lo + 64, c:c + P],
                                  a_qs[lo:lo + 64, c:c + P], start=True, stop=True)
                last.then_inc(sig("gla_sc"), 1)
                for j in range(2):
                    for r in range(2):
                        last = nc.tensor.transpose(M[:, 4, S * r + P * j:S * r + P * (j + 1)],
                                                   a_kl[:, S * j + P * r:S * j + P * (r + 1)], ident)
                last.then_inc(sig("gla_klT"), 1)

            def gla_states():
                pe.wait_ge(sig("gla_kltok"), 1)
                pe.wait_ge(sig("gla_vtok"), 1)
                for hd in range(4):
                    lo, j = 64 * (hd % 2), hd // 2
                    for c in range(3):
                        cb, r = 64 * (c % 2), c // 2
                        last = mm(M[lo:lo + 64, 4 + c % 2, S * j + P * r:S * j + P * (r + 1)],
                                  a_kltok[cb:cb + 64, r, 64 * hd:64 * hd + 64], a_vtok[cb:cb + 64, r, hd, :],
                                  start=True, stop=True)
                last.then_inc(sig("gla_dS"), 1)

            def gla_out():
                pe.wait_ge(sig("gla_masked"), 1)
                pe.wait_ge(sig("gla_S"), 1)
                for hd in range(4):
                    lo, j = 64 * (hd % 2), hd // 2
                    for r in range(2):
                        o = M[:, hd % 2, S * j + P * r:S * j + P * (r + 1)]
                        mm(o, a_vtok[:, r, hd, :], a_sc[:, 2 * (hd % 2) + j, r, :], start=True, stop=False)
                        for c in (2 * r, 2 * r + 1):
                            if c:
                                last = mm(o[:, 64 * (c % 2):64 * (c % 2) + 64], a_st[lo:lo + 64, j, c - 1, :],
                                          a_qi[lo:lo + 64, S * j + 64 * c:S * j + 64 * (c + 1)],
                                          start=False, stop=c == 2 * r + 1)
                last.then_inc(sig("gla_o"), 1)
                gate_halves(2)
                pe.wait_ge(sig("gla_osq"), 1)
                block_sum(bank(2, 2), a_sq, ones).then_inc(sig("gla_ssq"), 1)

            def rwkv_lora():
                gate_halves(4)
                pe.wait_ge(sig("gla_done"), 1)
                gate_halves(2)
                pe.wait_ge(sig("rw_act"), 2)
                for j in range(4):
                    mm(bank(0, 2)[:, S * j:S * (j + 1)], small_w("w_lora", P * j, P)[0:96, :],
                       blocks(B_XW)[0:96, :], start=True, stop=True)
                for j in range(4):
                    mm(bank(2, 2)[:, S * j:S * (j + 1)], small_w("a_lora", P * j, P)[0:96, :],
                       blocks(B_XA)[0:96, :], start=True, stop=True)
                for j in range(4):
                    for k in range(2):
                        last = mm(bank(4, 2)[:, S * j:S * (j + 1)], small_w("g_lora", 512 * k + P * j, P),
                                  blocks(B_XG + k), start=k == 0, stop=k == 1)
                last.then_inc(sig("rw_lora"), 1)
                gate_halves(3)

            def rwkv_sums():
                pe.wait_ge(sig("rw_sig"), 1)
                pe.wait_ge(sig("rw_kksq"), 1)
                block_sum(bank(0, 2), r_tmp, blk64).then_inc(sig("rw_kkss"), 1)
                gate_halves(1)
                pe.wait_ge(sig("rw_rk"), 1)
                block_sum(bank(2, 2), r_bonus, blk64).then_inc(sig("rw_rks"), 1)
                gate_halves(4)

            def rwkv_pair(r):
                pe.wait_ge(sig("rw_feat"), 1)
                if r == 1:
                    pe.wait_ge(sig("rw_state"), 2), pe.wait_ge(sig("rw_ycopy"), 2)
                for n, src in enumerate((r_p, r_kt)):
                    if n == 1:
                        pe.wait_ge(sig("rw_ar"), r + 1)
                    for hd in range(8):
                        lo, j = 64 * (hd % 2), hd // 2
                        last = mm(bank(0, 4)[:, S * hm(hd):S * (hm(hd) + 1)], src[lo:lo + 64, S * j + P * r:S * j + P * (r + 1)],
                                  r_qr[lo:lo + 64, j, r, :, :].rearrange("p q t -> p (q t)"),
                                  start=True, stop=True)
                    last.then_inc(sig("rw_scores"), 1)
                    gate_halves(1)
                for n, src in enumerate((r_p, r_kt, blocks(B_V, 4))):
                    if n == 2:
                        pe.wait_ge(sig("rw_tok"), 3 * r + 1)
                    b = (4, 5, 4)[n]
                    for j in range(4):
                        last = nc.tensor.transpose(M[:, b, P * j:P * (j + 1)], src[:, S * j + P * r:S * j + P * (r + 1)],
                                                   ident)
                    last.then_inc(sig("rw_turned"), 1)
                    if n:
                        gate_halves(1)

            def rwkv_level(r, n):
                pe.wait_ge(sig("rw_mt"), 6 * r + n + 1)
                if n == 0:
                    pe.wait_ge(sig("rw_bk"), r + 1)
                    pe.wait_ge(sig("rw_tok"), 3 * r + 3)
                else:
                    pe.wait_ge(sig("rw_x"), 5 * r + n)
                for hd in range(8):
                    rhs = ident if n == 0 else r_x[:, P * hd:P * (hd + 1)]
                    last = mm(bank(0, 2)[:, P * hd:P * (hd + 1)], r_mt[:, P * hd:P * (hd + 1)], rhs,
                              start=True, stop=True)
                last.then_inc(sig("rw_t1p"), 1)
                gate_halves(1)
                if n == 0:
                    return
                pe.wait_ge(sig("rw_t1"), 5 * r + n)
                if n < 5:
                    for hd in range(8):
                        mm(bank(2, 2)[:, P * hd:P * (hd + 1)], r_xt[:, P * hd:P * (hd + 1)],
                           r_t1[:, P * hd:P * (hd + 1)], start=True, stop=True)
                for hd in range(8):
                    last = mm(bank(4, 2)[:, P * hd:P * (hd + 1)], r_t1[:, P * hd:P * (hd + 1)],
                              r_xt[:, P * hd:P * (hd + 1)], start=True, stop=True)
                last.then_inc(sig("rw_dx"), 1)
                gate_halves(1)

            def rwkv_chunk_a(c):
                r, cb = c // 2, 64 * (c % 2)
                if c % 2 == 0:
                    pe.wait_ge(sig("rw_xt"), r + 1)
                else:
                    pe.wait_ge(sig("rw_state"), c), pe.wait_ge(sig("rw_ycopy"), c)
                for hd in range(8):
                    lo, j = 64 * (hd % 2), hd // 2
                    o = M[cb:cb + 64, hd % 2, 64 * j:64 * j + 64]
                    if c:
                        mm(o, r_qr[lo:lo + 64, j, r, 0, cb:cb + 64], r_stc[c % 2][lo:lo + 64, j, :], start=True, stop=False)
                    last = mm(o, r_bk[:, hm(hd), cb:cb + 64], r_vtok[:, 64 * hd:64 * hd + 64],
                              start=c == 0, stop=True)
                last.then_inc(sig("rw_rhsp"), 1)

            def rwkv_chunk_b(c):
                r, cb = c // 2, 64 * (c % 2)
                pe.wait_ge(sig("rw_rhs"), c + 1)
                for hd in range(8):
                    x0 = P * hm(hd) + cb
                    last = mm(M[cb:cb + 64, 4, 64 * hd:64 * hd + 64], r_xt[cb:cb + 64, x0:x0 + 64],
                              r_rhs[cb:cb + 64, 64 * hm(hd):64 * hm(hd) + 64], start=True, stop=True)
                last.then_inc(sig("rw_up"), 1)

            def rwkv_chunk_c(c):
                r, cb = c // 2, 64 * (c % 2)
                pe.wait_ge(sig("rw_u"), c + 1)
                if c < 3:
                    for hd in range(8):
                        lo, j = 64 * (hd % 2), hd // 2
                        o = M[lo:lo + 64, 3, 64 * j:64 * j + 64]
                        mm(o, r_ptok[cb:cb + 64, 64 * hd:64 * hd + 64], r_u[cb:cb + 64, 64 * hd:64 * hd + 64],
                           start=True, stop=False)
                        last = mm(o, r_ktok[cb:cb + 64, 64 * hd:64 * hd + 64], r_vtok[cb:cb + 64, 64 * hd:64 * hd + 64],
                                  start=False, stop=True)
                    last.then_inc(sig("rw_sp"), 1)
                for hd in range(8):
                    lo, j = 64 * (hd % 2), hd // 2
                    o = M[lo:lo + 64, 2, 64 * j:64 * j + 64]
                    mm(o, r_u[:, 64 * hd:64 * hd + 64], r_ar[:, hm(hd), P + cb:P + cb + 64],
                       start=True, stop=False)
                    last = mm(o, r_vtok[:, 64 * hd:64 * hd + 64], r_bk[:, hm(hd), P + cb:P + cb + 64],
                              start=False, stop=c == 0)
                    if c:
                        last = mm(o, r_stc[c % 2][lo:lo + 64, j, :], r_qr[lo:lo + 64, j, r, 1, cb:cb + 64],
                                  start=False, stop=True)
                last.then_inc(sig("rw_yp"), 1)

            def rwkv_norm():
                pe.wait_ge(sig("rw_ycopy"), 4)
                block_sum(bank(0, 2), r_y, blk64).then_inc(sig("rw_mean"), 1)
                gate_halves(3)
                pe.wait_ge(sig("rw_ysq"), 1)
                block_sum(bank(2, 2), r_tmp, blk64).then_inc(sig("rw_var"), 1)
                gate_halves(4)

            pe.wait_ge(sig("const1_in"), 16)
            norm_sum(0)
            project(G_IN_A, 0, 1, ("h_ready", 0))
            project(G_IN_A + 4, 4, 2)
            nsa_compress()
            nsa_norms()
            project(G_IN_B, 12, 1)
            nsa_small()
            project(G_IN_B + 4, 16, 1)
            nsa_bias()
            nsa_scores(0)
            project(G_IN_B + 8, 20, 1)
            nsa_turn(0)
            project(G_IN_B + 12, 24, 1)
            nsa_values(0)
            nsa_scores(1)
            project(G_IN_B + 16, 28, 1)
            nsa_turn(1)
            project(G_IN_B + 20, 32, 1)
            nsa_values(1)
            lru_gates()
            project(G_IN_B + 24, 36, 1)
            gla_decay()
            project(G_IN_B + 28, 40, 1)
            gla_scores()
            gla_states()
            for u in range(3):
                pe.wait_ge(sig("block_out"), 44 + u - 1)
                slab(G_IN_B + 32 + u, stream[:, u % 2, 0:S], h)
            gate_halves(2)
            gla_out()
            rwkv_lora()
            rwkv_sums()
            for r in range(2):
                rwkv_pair(r)
                for n in range(6):
                    rwkv_level(r, n)
                for c in (2 * r, 2 * r + 1):
                    rwkv_chunk_a(c)
                    gate_halves(1)
                    rwkv_chunk_b(c)
                    gate_halves(1)
                    rwkv_chunk_c(c)
                    gate_halves(CHUNK_HALVES[c])
            rwkv_norm()
            assert halves_run[0] == 2 * MIX_GATES

            def split_slab(g, out_ap, hi, lo, it=0, step=RING, start=True, stop=True, ready=None,
                           moving=None, free=None):
                k, tiles = 0, unit_tiles(g)
                for j, n in enumerate(tiles):
                    pe.wait_ge(sig("lo_ready"), unit(g, j, it, step) + 1)
                    if free is not None:
                        free(j)
                    if moving is not None:
                        pe.wait_ge(sig(moving[0]), moving[1] + moving[2] * j)
                    u = units(g) + j
                    for i in range(n):
                        if ready is not None:
                            pe.wait_ge(sig("h_ready"), ready + k + 1)
                        whi, wlo = w_hi[:, u % UNITS, P * i:P * (i + 1)], w_lo[:, u % UNITS, P * i:P * (i + 1)]
                        first, end = start(j, i), stop(j, i)
                        mm(out_ap(j, i), whi, hi(k), start=first, stop=False)
                        mm(out_ap(j, i), whi, lo(k), start=False, stop=False)
                        last = mm(out_ap(j, i), wlo, hi(k), start=False, stop=end)
                        k += 1
                    last.then_inc(sig("unit_done"), 1)

            def whole(g):
                n = len(unit_tiles(g))
                return {"start": lambda j, i: j == 0 and i == 0,
                        "stop": lambda j, i: j == n - 1 and i == unit_tiles(g)[-1] - 1}

            def nh(k):
                return h_hi[:, k, :]

            def nl(k):
                return h_lo[:, k, :]

            steps = [0]

            def more(n):
                for _ in range(n):
                    layer, e = divmod(steps[0], KT + 4)
                    if e < KT:
                        if layer or e >= 2:
                            pe.wait_ge(sig("block2_out"), 16 * layer + e - 1)
                        split_slab(G_IN2[layer] + e, lambda j, i: stream[:, e % 2, 0:S], nh, nl,
                                   ready=KT * (2 + layer) if e == 0 else None, **whole(G_UP))
                    else:
                        half, part = divmod(e - KT, 2)

                        def free(j):
                            n = 4 * part + j
                            if n >= 2 and half == 0:
                                pe.wait_ge(sig("out_half"), 8 * layer + n - 1)
                            if n < 2 and half == 1:
                                pe.wait_ge(sig("out_half"), 8 * layer + 7 + n)
                            if n >= 2 and half == 1:
                                pe.wait_ge(sig("res_add"), 2 + KT * (2 + layer) + 2 * (n - 1))

                        split_slab(G_OUT2[layer] + e - KT, lambda j, i: stream[:, j % 2, S * (i // 2):S * (i // 2 + 1)],
                                   lambda k: py_hi[:, 2 * half + k % 2, :], lambda k: py_lo[:, 2 * half + k % 2, :],
                                   start=lambda j, i: i % 2 == 0, stop=lambda j, i: i % 2 == 1, free=free,
                                   moving=("moving_split", 8 + 2 * layer + half + 1, 0))
                    steps[0] += 1

            def attention(layer, half):
                t0 = 2 * layer + half
                kind = ATTENTIONS[t0]
                more(MORE[t0][0])
                q, k, v = p_blocks(8 * half, 2), p_blocks(8 * half + 2, 2), p_blocks(8 * half + 4, 2)
                pe.wait_ge(sig("block2_out"), 16 * layer + 8 * half + 6)
                if t0:
                    pe.wait_ge(sig("at_y"), t0)
                if kind != 3:
                    rot = c2(C2_R64 if layer == 0 else C2_R32, P)
                    if t0 == 0:
                        pe.wait_ge(sig("const2_in"), 16)
                    for a in range(2):
                        last = mm(M[:, a, :], rot, p_blocks(8 * half + 2 * a, 2), start=True, stop=True)
                    last.then_inc(sig("at_rot"), 1)
                more(MORE[t0][1])
                for j in range(2):
                    for st in range(2):
                        last = nc.tensor.transpose(M[:, 2, S * st + P * j:S * st + P * (j + 1)],
                                                   v[:, S * j + P * st:S * j + P * (st + 1)], ident)
                last.then_inc(sig("at_vT"), 1)
                pe.wait_ge(sig("at_vtok"), t0 + 1)
                if kind != 3:
                    pe.wait_ge(sig("at_qk"), kind + 1)
                rows = 4 if kind == 2 else 2
                kd = P // rows
                if kind == 2:
                    pe.wait_ge(sig("block2_out"), 2 * KT)
                for t in range(2):
                    w = P * (t + 1)
                    for i in range(rows):
                        lo = kd * i
                        for j in range(2):
                            last = mm(logit_banks(rows, t)[i][:, w * j:w * (j + 1)],
                                      q[lo:lo + kd, S * j + P * t:S * j + P * (t + 1)],
                                      k[lo:lo + kd, S * j:S * j + w], start=True, stop=True)
                    last.then_inc(sig("at_logits"), 1)
                if kind == 2:
                    pe.wait_ge(sig("at_max"), 6)
                more(MORE[t0][2])
                if kind == 3:
                    pe.wait_ge(sig("stick_exp"), 1)
                else:
                    pe.wait_ge(sig("at_prob"), kind + 1)
                for t in range(2):
                    for hd in range(4):
                        for st in range(t + 1):
                            n = 4 * t + hd * (t + 1) + st
                            src = diff_tmp(t) if kind == 2 else prob(t)
                            last = nc.tensor.transpose(bank(0, 3)[:, P * n:P * (n + 1)],
                                                       src[:, am(hd), P * st:P * (st + 1)], ident)
                last.then_inc(sig("at_turned"), 1)
                more(MORE[t0][3])
                pe.wait_ge(sig("at_PT"), t0 + 1)
                for t in range(2):
                    for hd in range(4):
                        lo, j = 64 * (hd % 2), hd // 2
                        o = M[lo:lo + 64, 3, S * j + P * t:S * j + P * (t + 1)]
                        for st in range(t + 1):
                            n = 4 * t + hd * (t + 1) + st
                            last = mm(o, p_vtok[:, S * st + 64 * hd:S * st + 64 * hd + 64],
                                      p_probT[:, P * n:P * (n + 1)], start=st == 0, stop=st == t)
                last.then_inc(sig("at_o"), 1)
                more(MORE[t0][4])
                if kind == 2:
                    pe.wait_ge(sig("at_osq"), 1)
                    block_sum(M[:, 4, :], p_sq, blk64).then_inc(sig("at_oss"), 1)

            each = {"start": lambda j, i: i == 0, "stop": lambda j, i: i == 3}
            e0 = N_MIX + MIX_GATES
            with pe.Fori(0, (N_GATES - MIX_GATES) // 4) as it:
                for u in range(4):
                    pe.wait_ge(sig("block_out"), e0 + u - 1 + 4 * it)
                    split_slab(G_SPLIT + u, lambda j, i: stream[:, (e0 + u) % 2, 0:S], lambda k: m_hi[:, k, :],
                               lambda k: m_lo[:, k, :], it, moving=("moving_split", 1, 1), **whole(G_SPLIT))
            pe.wait_ge(sig("moving_split"), 8)
            with pe.Fori(0, KT // 4) as it:
                for u in range(4):
                    pe.wait_ge(sig("merge_read"), u + 1 + 4 * it)
                    split_slab(G_BRANCH + u, lambda j, i: bank(2 * (u % 2), 2)[:, S * j:S * (j + 1)],
                               lambda k: y2_hi[:, k, :], lambda k: y2_lo[:, k, :], it, **each)
            with pe.Fori(0, KT // 4) as it:
                for u in range(4):
                    pe.wait_ge(sig("res_add"), u + 1 + 4 * it)
                    split_slab(G_OUT + u, lambda j, i: stream[:, u % 2, 0:S], lambda k: m_hi[:, k, :],
                               lambda k: m_lo[:, k, :], it, moving=("merged", 4, 4), **whole(G_OUT))
            norm_sum(1)

            def up(u, it, ready=None):
                if u % 2 == 0:
                    pe.wait_ge(sig("up_read"), 2 * it + u // 2 + 1)
                split_slab(G_UP + u, lambda j, i: up_bank[u % 4], nh, nl, it, ready=ready, **whole(G_UP))

            up(0, 0, KT)
            for u in range(1, 4):
                up(u, 0)
            with pe.Fori(0, FB // 2 - 1) as it:
                for u in range(4):
                    pe.wait_ge(sig("up_read"), 2 * it + u // 2 + 3)
                    split_slab(G_UP + 4 + u, lambda j, i: up_bank[u], nh, nl, it, **whole(G_UP))
            with pe.Fori(0, KT // 2) as it:
                for u in range(8):
                    n, part = u // 4, u % 4
                    if part == 0:
                        pe.wait_ge(sig("res_add"), KT + 1 + n + 2 * it)
                    if n == 0:
                        pe.wait_ge(sig("ffn_act"), DOWN_K * (part + 1) + 2)
                    split_slab(G_DOWN + u, lambda j, i: stream[:, n, 0:S], lambda k: a_hi[:, DOWN_K * part + k, :],
                               lambda k: a_lo[:, DOWN_K * part + k, :], it, 8,
                               start=lambda j, i: part == 0 and j == 0 and i == 0,
                               stop=lambda j, i: part == 3 and j == 2 and i == 2)
            norm_sum(2)
            for layer in range(2):
                more(8)
                attention(layer, 0)
                attention(layer, 1)
                more(2)
                norm_sum(3 + layer)

        @block.scalar
        def _(act):
            f = nc.scalar.activation

            def norm_root(k):
                act.wait_ge(sig("norm_sum"), k + 1)
                f(rs[:, :], M[:, 0, 0:S], ACT.Sqrt, bias=eps_col, scale=1.0 / D).then_inc(sig("root_ready"), 1)

            def copy_blocks(g0, e0, n, dst, e_dst):
                def one(u, it):
                    act.wait_ge(sig("slab_done"), g0 + u + 1 + RING * it)
                    nc.scalar.copy(dst[:, bass.ds(S * (e_dst + u) + S * RING * it, S)]
                                   if not isinstance(it, int) else dst[:, S * (e_dst + u):S * (e_dst + u + 1)],
                                   stream[:, (e0 + u) % 2, 0:S]).then_inc(sig("block_out"), 1)
                if n <= RING:
                    for u in range(n):
                        one(u, 0)
                else:
                    with act.Fori(0, n // RING) as it:
                        for u in range(RING):
                            one(u, it)

            mixers = W[:, PRE:PRE + 256 * N_MIX]
            halves_run = [0]

            def gate_halves(n):
                for _ in range(n):
                    e, part = halves_run[0] // 2, halves_run[0] % 2
                    if part == 1:
                        act.wait_ge(sig("slab_done"), G_GATES + e + 1)
                        f(G[:, S * e:S * (e + 1)], stream[:, (N_MIX + e) % 2, 0:S], ACT.Sigmoid) \
                            .then_inc(sig("block_out"), 1)
                    halves_run[0] += 1

            def nsa_norms():
                act.wait_ge(sig("block_out"), 12)
                f(n_sq[:, 0:1024], blocks(B_Q, 4), ACT.Square).then_inc(sig("nsa_sq"), 1)
                f(n_sq[:, 1024:1280], blocks(B_KV + 2), ACT.Square).then_inc(sig("nsa_sq"), 1)
                f(n_sq[:, 1280:1536], blocks(B_KV + 4), ACT.Square).then_inc(sig("nsa_sq"), 1)
                act.wait_ge(sig("nsa_ssq"), 1)
                f(n_rs, bank(2, 3), ACT.Sqrt, bias=eps_col, scale=1.0 / P).then_inc(sig("root_ready"), 1)
                act.wait_ge(sig("nsa_vT"), 1)
                nc.scalar.copy(g_at(1024, 512), M[:, 5, :]).then_inc(sig("nsa_vtok"), 1)
                for a in range(2):
                    f(n_hT[0:15, P * a:P * (a + 1)], M[0:15, a, 0:P], ACT.Gelu_apprx_tanh).then_inc(sig("cmp_hidden"), 1)

            def nsa_small():
                act.wait_ge(sig("cmp_turned"), 1)
                nc.scalar.copy(n_hk[:, 0:15], M[:, 0, 0:15]).then_inc(sig("cmp_hidden"), 1)
                nc.scalar.copy(n_hv[:, 0:15], M[:, 1, 0:15]).then_inc(sig("cmp_hidden"), 1)
                act.wait_ge(sig("nsa_small"), 1)
                f(n_gate.rearrange("p (t g) -> p t g", t=2),
                  M[:, 3, 0:256].rearrange("p (t g) -> p t g", t=2)[:, :, GATE_ROW:GATE_ROW + 12],
                  ACT.Sigmoid).then_inc(sig("nsa_gates"), 1)
                nc.scalar.copy(n_vc[0:15, :], M[0:15, 1, 0:P])
                f(n_kc2[:, 0:15], M[:, 0, 0:15], ACT.Square).then_inc(sig("kc_sq"), 1)
                act.wait_ge(sig("kc_ssq"), 1)
                f(n_kc[:, 0:15], M[:, 4, 0:15], ACT.Sqrt, bias=eps_col, scale=1.0 / P).then_inc(sig("root_ready"), 1)

            def nsa_bias():
                act.wait_ge(sig("nsa_skew"), 1)
                nc.scalar.copy(g_at(0, 512), M[:, 5, :])
                nc.scalar.copy(g_at(512, 512), M[:, 3, :]).then_inc(sig("nsa_bias"), 1)

            def nsa_exp(t):
                pr = n_prob.rearrange("p (a h s) -> p a h s", a=2, h=4)
                act.wait_ge(sig("nsa_max"), t + 1)
                for hd in range(4):
                    pc = n_pc[:, 16 * hd:16 * hd + 15]
                    f(pc, pc, ACT.Exp, bias=n_nmax[:, hd:hd + 1], accum_out=n_sum[:, hd:hd + 1])
                for a in range(2):
                    for hd in range(4):
                        m = 4 + 4 * a + hd
                        pm = pr[:, a, hd, 0:P * (t + 1)]
                        last = f(pm, pm, ACT.Exp, bias=n_nmax[:, m:m + 1], accum_out=n_sum[:, m:m + 1])
                last.then_inc(sig("nsa_exp"), 1)

            def nsa_turn(t):
                act.wait_ge(sig("nsa_turned"), t + 1)
                n = 4 * P * (t + 1)
                nc.scalar.copy(n_probT[:, 0:n], bank(0, 4)[:, 0:n])
                nc.scalar.copy(n_pcT[0:15, 0:512], M[0:15, 4, :]).then_inc(sig("nsa_PT"), 1)

            def nsa_y(t):
                act.wait_ge(sig("nsa_o"), t + 1)
                nc.scalar.copy(y_sb[:, 8:12, P * t:P * (t + 1)],
                               M[:, 5, :].rearrange("p (h t) -> p h t", h=4)).then_inc(sig("nsa_y"), 1)

            def lru():
                lam, t1, t2, c8 = col("lam", 0, 4), tiny[:, 0:4], tiny[:, 4:8], tiny[:, 8:12]
                f(t1, lam, ACT.Abs).then_inc(sig("act_step"), 1)
                act.wait_ge(sig("act_step"), nth("act_step"))
                f(t1, t1, ACT.Exp, scale=-1.0).then_inc(sig("act_step"), 1)
                act.wait_ge(sig("act_step"), nth("act_step"))
                f(t1, t1, ACT.Ln, bias=1.0).then_inc(sig("lru_ln"), 1)
                act.wait_ge(sig("lru_pre"), 1)
                for j in range(4):
                    last = f(l_a[:, S * j:S * (j + 1)], bank(0, 2)[:, S * j:S * (j + 1)], ACT.Sigmoid,
                             bias=col("b_a", j))
                last.then_inc(sig("lru_gated"), 1)
                act.wait_ge(sig("lru_gated"), nth("lru_gated"))
                for j in range(4):
                    last = f(l_u[:, S * j:S * (j + 1)], bank(2, 2)[:, S * j:S * (j + 1)], ACT.Sigmoid,
                             bias=col("b_i", j))
                last.then_inc(sig("lru_gated"), 1)
                act.wait_ge(sig("lru_c8"), 1)
                for j in range(4):
                    last = f(l_t[:, S * j:S * (j + 1)], l_a[:, S * j:S * (j + 1)], ACT.Tanh, scale=tiny[:, 12 + j:13 + j])
                last.then_inc(sig("lru_tanh"), 1)
                act.wait_ge(sig("lru_tanh"), nth("lru_tanh"))
                for j in range(4):
                    last = f(l_a[:, S * j:S * (j + 1)], l_a[:, S * j:S * (j + 1)], ACT.Exp, scale=tiny[:, 8 + j:9 + j])
                last.then_inc(sig("lru_decay"), 1)
                f(blocks(B_LG, 4), blocks(B_LG, 4), ACT.Gelu_apprx_tanh).then_inc(sig("lru_gelu"), 1)
                act.wait_ge(sig("lru_ratio"), 1)
                f(l_t, l_t, ACT.Sqrt, scale=2.0).then_inc(sig("root_ready"), 1)

            def gla_a():
                act.wait_ge(sig("gla_z"), 1)
                act.wait_ge(sig("nsa_y"), 2)
                for j in range(2):
                    last = f(a_b[:, S * j:S * (j + 1)], M[:, 0, S * j:S * (j + 1)], ACT.Identity, bias=col("gk_b", j))
                last.then_inc(sig("act_step"), 1)
                act.wait_ge(sig("act_step"), nth("act_step"))
                f(a_e1, a_b, ACT.Abs).then_inc(sig("act_step"), 1)
                act.wait_ge(sig("act_step"), nth("act_step"))
                f(a_e1, a_e1, ACT.Exp, scale=-1.0).then_inc(sig("act_step"), 1)
                act.wait_ge(sig("act_step"), nth("act_step"))
                f(a_e1, a_e1, ACT.Ln, bias=1.0).then_inc(sig("gla_ln"), 1)
                act.wait_ge(sig("gla_vT"), 1)
                nc.scalar.copy(g_at(4608, 1024), bank(2, 2)).then_inc(sig("gla_vtok"), 1)
                act.wait_ge(sig("gla_cum"), 1)
                f(a_e1, a_bm, ACT.Exp, scale=1.0 / 16)
                f(a_e2, a_bm, ACT.Exp, scale=-1.0 / 16)
                f(a_eb, a_b, ACT.Exp, scale=1.0 / 16)
                f(a_kl, a_kl, ACT.Exp, scale=1.0 / 16).then_inc(sig("gla_exp"), 1)
                f(blocks(B_GG, 2), blocks(B_GG, 2), ACT.Silu).then_inc(sig("act_step"), 1)
                act.wait_ge(sig("act_step"), nth("act_step"))

            def gla_b():
                act.wait_ge(sig("gla_klT"), 1)
                nc.scalar.copy(g_at(4096, 512), M[:, 4, :]).then_inc(sig("gla_kltok"), 1)

            def gla_c():
                f(blocks(B_GG + 2, 2), blocks(B_GG + 2, 2), ACT.Silu).then_inc(sig("gla_silu"), 1)
                act.wait_ge(sig("gla_o"), 1)
                ov = a_o.rearrange("p (j i t) -> p j i t", j=2, i=2)
                nc.scalar.copy(ov[:, :, 0, :], M[:, 0, :].rearrange("p (j t) -> p j t", j=2))
                nc.scalar.copy(ov[:, :, 1, :], M[:, 1, :].rearrange("p (j t) -> p j t", j=2)) \
                    .then_inc(sig("gla_ocopy"), 1)
                act.wait_ge(sig("gla_ocopy"), nth("gla_ocopy"))
                f(a_sq, a_o, ACT.Square).then_inc(sig("gla_osq"), 1)
                act.wait_ge(sig("gla_ssq"), 1)
                f(a_sq, bank(2, 2), ACT.Sqrt, bias=eps_col, scale=1.0 / P).then_inc(sig("root_ready"), 1)

            def rwkv_a():
                act.wait_ge(sig("rw_mixed"), 1)
                f(blocks(B_XW)[0:96, :], blocks(B_XW)[0:96, :], ACT.Tanh).then_inc(sig("rw_act"), 1)
                f(blocks(B_XG, 2), blocks(B_XG, 2), ACT.Sigmoid).then_inc(sig("rw_act"), 1)
                gate_halves(2)
                act.wait_ge(sig("rw_lora"), 1)
                for j in range(4):
                    f(r_sig[:, S * j:S * (j + 1)], bank(0, 2)[:, S * j:S * (j + 1)], ACT.Sigmoid, bias=col("w0", j))
                for j in range(4):
                    f(r_a[:, S * j:S * (j + 1)], bank(2, 2)[:, S * j:S * (j + 1)], ACT.Sigmoid, bias=col("a0", j))
                nc.scalar.copy(r_g, bank(4, 2)).then_inc(sig("rw_sig"), 1)
                gate_halves(3)
                act.wait_ge(sig("rw_cum"), 2)
                f(w_at(4096, 1024), r_cs, ACT.Exp, scale=KAPPA)
                f(w_at(5120, 1024), r_kt, ACT.Exp, scale=KAPPA)
                f(r_p, r_cs, ACT.Exp, scale=-KAPPA).then_inc(sig("rw_exp"), 1)
                act.wait_ge(sig("rw_kk"), 1)
                f(r_tmp, r_kk, ACT.Square).then_inc(sig("rw_kksq"), 1)
                act.wait_ge(sig("rw_kkmax"), 1)
                f(r_tmp, r_tmp, ACT.Sqrt).then_inc(sig("root_ready"), 1)
                gate_halves(5)

            def rwkv_tokens(r):
                for n, (b, dst) in enumerate(((4, r_ptok), (5, r_ktok), (4, r_vtok))):
                    act.wait_ge(sig("rw_turned"), 3 * r + n + 1)
                    nc.scalar.copy(dst, M[:, b, :]).then_inc(sig("rw_tok"), 1)
                    if n:
                        gate_halves(1)

            def rwkv_level(r, n):
                if n:
                    act.wait_ge(sig("rw_t1p"), 6 * r + n + 1)
                    nc.scalar.copy(r_t1, bank(0, 2)).then_inc(sig("rw_t1"), 1)
                    gate_halves(1)
                gate_halves(1)

            def rwkv_y(c):
                act.wait_ge(sig("rw_yp"), c + 1)
                nc.scalar.copy(r_y.rearrange("p (j t) -> p j t", j=4)[:, :, 64 * c:64 * c + 64],
                               M[:, 2, 0:256].rearrange("p (j t) -> p j t", j=4)).then_inc(sig("rw_ycopy"), 1)

            def rwkv_norm():
                act.wait_ge(sig("rw_centred"), 1)
                f(r_tmp, r_y, ACT.Square).then_inc(sig("rw_ysq"), 1)
                gate_halves(3)
                act.wait_ge(sig("rw_var"), 1)
                f(r_tmp, bank(2, 2), ACT.Sqrt, bias=gn_col, scale=1.0 / 64).then_inc(sig("root_ready"), 1)
                gate_halves(4)

            eps_col, gn_col = tiny[:, 20:21], tiny[:, 21:22]
            act.wait_ge(sig("x_in"), 16)
            act.wait_ge(sig("tiny_set"), 1)
            for q in range(4):
                f(W[:, 1024 * q:1024 * (q + 1)], x_sb[:, 4 * q:4 * q + 4, :].rearrange("p k t -> p (k t)"),
                  ACT.Square).then_inc(sig("x_squares"), 1)
            norm_root(0)
            copy_blocks(0, 0, 4, mixers, 0)
            copy_blocks(4, 4, 8, mixers, 4)
            nsa_norms()
            copy_blocks(G_IN_B, 12, 4, mixers, 12)
            nsa_small()
            copy_blocks(G_IN_B + 4, 16, 4, mixers, 16)
            nsa_bias()
            nsa_exp(0)
            copy_blocks(G_IN_B + 8, 20, 4, mixers, 20)
            nsa_turn(0)
            copy_blocks(G_IN_B + 12, 24, 4, mixers, 24)
            nsa_y(0)
            nsa_exp(1)
            copy_blocks(G_IN_B + 16, 28, 4, mixers, 28)
            nsa_turn(1)
            copy_blocks(G_IN_B + 20, 32, 4, mixers, 32)
            nsa_y(1)
            lru()
            copy_blocks(G_IN_B + 24, 36, 4, mixers, 36)
            gla_a()
            copy_blocks(G_IN_B + 28, 40, 4, mixers, 40)
            gla_b()
            copy_blocks(G_IN_B + 32, 44, 3, mixers, 44)
            gla_c()
            gate_halves(4)
            act.wait_ge(sig("gla_done"), 1)
            gate_halves(4)
            rwkv_a()
            for r in range(2):
                gate_halves(2)
                rwkv_tokens(r)
                for n in range(6):
                    rwkv_level(r, n)
                for c in (2 * r, 2 * r + 1):
                    gate_halves(2)
                    rwkv_y(c)
                    gate_halves(CHUNK_HALVES[c])
            rwkv_norm()
            act.wait_ge(sig("rwkv_y"), 1)

            def hi(g, it=0, step=RING, then=None):
                act.wait_ge(slot_in(g), fill(g) + 4 * step * it)
                k = 0
                for j, n in enumerate(unit_tiles(g)):
                    act.wait_ge(sig("unit_done"), unit(g, j, it, step) + 1)
                    u = (units(g) + j) % UNITS
                    nc.scalar.copy(w_hi[:, u, 0:P * n], ring[:, g % RING, k:k + n, :].rearrange("p k f -> p (k f)")) \
                        .then_inc(sig("hi_ready"), 1)
                    if then:
                        then(j)
                    k += n

            def norm_hi(k):
                for n in range(KT):
                    act.wait_ge(sig("norm_tmp"), KT * (k - 1) + n + 1)
                    nc.scalar.copy(h_hi[:, n, :], norm_tmp[:, n % 4, :]).then_inc(sig("norm_hi"), 1)

            def h_hi4(q):
                nc.scalar.copy(m_hi[:, 4 * q:4 * q + 4, :], h_sb[:, 4 * q:4 * q + 4, :]).then_inc(sig("moving_hi"), 1)

            steps = [0]

            def more(n, also=None):
                for _ in range(n):
                    layer, e = divmod(steps[0], KT + 4)
                    g = G_IN2[layer] + e

                    def pair(m):
                        act.wait_ge(sig("res_add"), 2 + KT * (2 + layer) + 2 * m + 2)
                        if m == 0:
                            act.wait_ge(sig("norm_sum"), 3 + layer)
                        if m > 2:
                            act.wait_ge(sig("pool_sq"), pair_sums(layer, m - 2))
                        f(sq_wide[:, :] if m == 0 else pair_sq[:, m % 2, :],
                          x_sb[:, 2 * m:2 * m + 2, :].rearrange("p k t -> p (k t)"), ACT.Square) \
                            .then_inc(sig("x_squares"), 1)

                    def beside(j):
                        if also and j in also:
                            also[j]()
                        if e >= KT + 2 and 4 * (e - KT - 2) + j > 0:
                            pair(4 * (e - KT - 2) + j - 1)

                    if g + 1 < G_END:
                        hi(g + 1, then=beside)
                    else:
                        for j in range(4):
                            beside(j)
                    if e == KT + 3:
                        pair(KT // 2 - 1)
                    if e < KT:
                        act.wait_ge(sig("unit_done"), slab_done(g))
                        nc.scalar.copy(Q[:, S * e:S * (e + 1)], stream[:, e % 2, 0:S]).then_inc(sig("block2_out"), 1)
                    steps[0] += 1

            def attention(layer, half):
                t0 = 2 * layer + half
                kind = ATTENTIONS[t0]
                more(MORE[t0][0] + MORE[t0][1])
                act.wait_ge(sig("block2_out"), 16 * layer + 8 * half + 8)
                act.wait_ge(sig("at_vT"), t0 + 1)
                nc.scalar.copy(p_vtok, M[:, 2, :]).then_inc(sig("at_vtok"), 1)
                gate = p_blocks(8 * half + 6, 2)
                f(gate, gate, ACT.Silu).then_inc(sig("at_silu"), 1)
                if kind != 3:
                    def exps(t):
                        maps = 8 if kind == 2 else 4
                        act.wait_ge(sig("at_max"), 2 * kind + t + 1)
                        pm = prob_maps(maps, t)
                        for m in range(maps):
                            i = maps * t + m
                            last = f(pm[:, m, :], pm[:, m, :], ACT.Exp, bias=p_stat[:, i:i + 1],
                                     accum_out=p_stat[:, 32 + i:33 + i])
                        last.then_inc(sig("at_exp"), 1)

                    more(1, {0: lambda: exps(0), 2: lambda: exps(1)})
                    more(MORE[t0][2] - 1)
                else:
                    z = q_at(4096, 1536)

                    def absolute():
                        act.wait_ge(sig("at_z"), 2)
                        f(p_tmp[:, 0:1536], z, ACT.Abs).then_inc(sig("act_step"), 1)

                    def exponential():
                        act.wait_ge(sig("act_step"), nth("act_step"))
                        f(p_tmp[:, 0:1536], p_tmp[:, 0:1536], ACT.Exp, scale=-1.0).then_inc(sig("act_step"), 1)

                    def logarithm():
                        act.wait_ge(sig("act_step"), nth("act_step"))
                        f(p_tmp[:, 0:1536], p_tmp[:, 0:1536], ACT.Ln, bias=1.0).then_inc(sig("stick_ln"), 1)

                    more(1, {0: absolute, 1: exponential, 2: logarithm})
                    more(MORE[t0][2] - 2)
                    act.wait_ge(sig("stick_log"), 1)
                    f(z, z, ACT.Exp).then_inc(sig("stick_exp"), 1)
                    more(1)
                act.wait_ge(sig("at_turned"), t0 + 1)
                nc.scalar.copy(p_probT, bank(0, 3)).then_inc(sig("at_PT"), 1)
                more(MORE[t0][3] + MORE[t0][4])
                if kind == 2:
                    act.wait_ge(sig("at_o"), t0 + 1)
                    f(p_sq, M[:, 3, :], ACT.Square).then_inc(sig("at_osq"), 1)
                    act.wait_ge(sig("at_oss"), 1)
                    f(p_sq, M[:, 4, :], ACT.Sqrt, bias=eps_col, scale=1.0 / 64).then_inc(sig("root_ready"), 1)

            hi(G_SPLIT, then=h_hi4)
            e0 = N_MIX + MIX_GATES

            def late_gate(u, it):
                hi(G_SPLIT + u + 1, it)
                act.wait_ge(sig("unit_done"), slab_done(G_SPLIT + u, it))
                a = S * (MIX_GATES + u)
                f(G[:, bass.ds(a + S * 4 * it, S)], stream[:, (e0 + u) % 2, 0:S], ACT.Sigmoid) \
                    .then_inc(sig("block_out"), 1)

            late_gate(0, 0)
            act.wait_ge(sig("moving_split"), 4)
            for q in range(4):
                nc.scalar.copy(y2_hi[:, 4 * q:4 * q + 4, :], y_sb[:, 4 * q:4 * q + 4, :]).then_inc(sig("moving_hi"), 1)
            for u in range(1, 4):
                late_gate(u, 0)
            with act.Fori(1, (N_GATES - MIX_GATES) // 4) as it:
                for u in range(4):
                    late_gate(u, it)

            gv = G.rearrange("p (b n t) -> p b n t", b=4, n=KT)

            def merge(u, it, first=False):
                n = u + 4 * it
                hi(G_BRANCH + u + 1, it)
                if not first:
                    act.wait_ge(sig("merge_sum"), 1 + u + 4 * it)
                    nc.scalar.copy(m_hi[:, n - 1, :], gv[:, 0, n - 1, :]).then_inc(sig("merge_hi"), 1)

            for u in range(4):
                merge(u, 0, u == 0)
            with act.Fori(1, KT // 4) as it:
                for u in range(4):
                    merge(u, it)
            act.wait_ge(sig("merge_sum"), 1 + KT)
            nc.scalar.copy(m_hi[:, KT - 1, :], gv[:, 0, KT - 1, :]).then_inc(sig("merge_hi"), 1)
            with act.Fori(0, KT // 4) as it:
                for u in range(4):
                    hi(G_OUT + u + 1, it)
            norm_root(1)
            norm_hi(1)

            def tap(i, p):
                act.wait_ge(sig("unit_done"), slab_done(G_UP + 1) + 8 * i)
                act.wait_ge(sig("ffn_act"), i + 1)
                for v in range(2):
                    f(ffn_buf[:, p, v, :], up_bank[2 * p + v], ACT.Identity,
                      bias=cv[:, bass.ds(i + COLS["fconv_b"][0] + FB * v, 1)],
                      scale=cv[:, bass.ds(i + COLS["fconv_w"][0] + 2 * 2 * FB + FB * v, 1)]) \
                        .then_inc(sig("ffn_tap"), 1)

            def silu(i, p):
                act.wait_ge(sig("up_read"), i + 3)
                f(ffn_buf[:, p, 0, :], ffn_buf[:, p, 0, :], ACT.Silu).then_inc(sig("ffn_silu"), 1)

            def up(i, p, it=0, peel=None):
                first = i if peel is not None else 2 + p
                hi(G_UP + 2 * first + 1, it)
                if peel is None or peel >= 1:
                    tap(i - 1, 1 - p)
                hi(G_UP + 2 * first + 2, it)
                if peel is None or peel >= 1:
                    silu(i - 1, 1 - p)

            up(0, 0, peel=0)
            up(1, 1, peel=1)
            with act.Fori(0, FB // 2 - 2) as it:
                for p in range(2):
                    up(2 + p + 2 * it, p, it)
            up(FB - 2, 0, peel=FB - 2)
            up(FB - 1, 1, peel=FB - 1)
            tap(FB - 1, 1)
            silu(FB - 1, 1)
            with act.Fori(0, KT // 2 - 1) as it:
                for u in range(8):
                    hi(G_DOWN + u + 1, it, 8)
            for u in range(8 * (KT // 2 - 1), 8 * (KT // 2)):
                hi(G_DOWN + u + 1)
            norm_root(2)
            norm_hi(2)
            for layer in range(2):
                more(8)
                if layer == 1:
                    act.wait_ge(sig("lam_dot"), 1)
                    f(tiny[:, 24:26], tiny[:, 24:26], ACT.Exp).then_inc(sig("lam_exp"), 1)
                attention(layer, 0)
                attention(layer, 1)
                more(2)
                norm_root(3 + layer)
                if layer == 0:
                    norm_hi(3)

        @block.vector
        def _(dve):
            v = nc.vector

            def norm_apply(k, gain, dst):
                dve.wait_ge(sig("root_ready"), ROOT["norm", k])
                v.reciprocal(rs[:, :], rs[:, :]).then_inc(sig("dve_step"), 1)
                dve.wait_ge(sig("dve_step"), nth("dve_step"))
                for n in range(KT):
                    v.scalar_tensor_tensor(dst[:, n, :], x_sb[:, n, :], col(gain, n), rs[:, :], ALU.mult,
                                           ALU.mult).then_inc(sig("h_ready"), 1)

            def norm_split(k, gain):
                dve.wait_ge(sig("root_ready"), ROOT["norm", k])
                v.reciprocal(rs[:, :], rs[:, :]).then_inc(sig("dve_step"), 1)
                dve.wait_ge(sig("dve_step"), nth("dve_step"))
                for n in range(KT + 1):
                    if n < KT:
                        v.scalar_tensor_tensor(norm_tmp[:, n % 4, :], x_sb[:, n, :], col(gain, n), rs[:, :], ALU.mult,
                                               ALU.mult).then_inc(sig("norm_tmp"), 1)
                    if n:
                        dve.wait_ge(sig("norm_hi"), KT * (k - 1) + n)
                        v.tensor_tensor(h_lo[:, n - 1, :], norm_tmp[:, (n - 1) % 4, :],
                                        h_hi[:, n - 1, :].bitcast(F32), ALU.subtract).then_inc(sig("h_ready"), 1)

            def lo(g, it=0, step=RING, then=None):
                k = 0
                for j, n in enumerate(unit_tiles(g)):
                    dve.wait_ge(sig("hi_ready"), unit(g, j, it, step) + 1)
                    u = (units(g) + j) % UNITS
                    v.tensor_tensor(w_lo[:, u, 0:P * n], ring[:, g % RING, k:k + n, :].rearrange("p k f -> p (k f)"),
                                    w_hi[:, u, 0:P * n].bitcast(F32), ALU.subtract).then_inc(sig("lo_ready"), 1)
                    if then:
                        then(j)
                    k += n

            def nsa_blocks():
                dve.wait_ge(sig("block_out"), B_KV + 2)
                for a in range(2):
                    x = blocks(B_KV + a)
                    o = n_blk[:, 480 * a:480 * (a + 1)].rearrange("p (l n) -> p l n", n=15)
                    for half in range(2):
                        win = x[:, 16 * half:16 * half + 240].rearrange("p (n l) -> p l n", l=16)
                        v.tensor_tensor(o[:, 16 * half:16 * half + 16, :], win,
                                        spread(col("pos", 16 * half, 16), 15), ALU.add).then_inc(sig("cmp_in"), 1)
                        dve.wait_ge(sig("cmp_in"), nth("cmp_in"))

            def nsa_norms():
                dve.wait_ge(sig("root_ready"), ROOT["nsa_root"])
                v.reciprocal(n_rs, n_rs).then_inc(sig("nsa_rs"), 1)
                dve.wait_ge(sig("nsa_rs"), nth("nsa_rs"))
                v.scalar_tensor_tensor(blocks(B_Q, 4), blocks(B_Q, 4), col("q_gain"), n_rs[:, 0:1024],
                                       ALU.mult, ALU.mult).then_inc(sig("nsa_qk"), 1)
                for a in range(2):
                    k = blocks(B_KV + 2 + 2 * a)
                    v.scalar_tensor_tensor(k, k, col("k_gain"), n_rs[:, 1024 + S * a:1024 + S * (a + 1)],
                                           ALU.mult, ALU.mult).then_inc(sig("nsa_qk"), 1)

            def nsa_small():
                dve.wait_ge(sig("nsa_small"), 1)
                v.tensor_tensor(n_ext[0:4, :], M[0:4, 2, :], n_hot[0:4, 512:1024], ALU.add) \
                    .then_inc(sig("bias_row"), 1)
                dve.wait_ge(sig("bias_row"), nth("bias_row"))
                dve.wait_ge(sig("root_ready"), ROOT["kc_root"])
                v.reciprocal(n_kc[:, 0:15], n_kc[:, 0:15]).then_inc(sig("dve_step"), 1)
                dve.wait_ge(sig("dve_step"), nth("dve_step"))
                v.scalar_tensor_tensor(n_kc[:, 0:15], M[:, 0, 0:15], col("k_gain"), n_kc[:, 0:15],
                                       ALU.mult, ALU.mult).then_inc(sig("nsa_qk"), 1)
                dve.wait_ge(sig("nsa_qk"), 4)

            def nsa_softmax(t):
                pr = n_prob.rearrange("p (a h s) -> p a h s", a=2, h=4)
                scale = P ** -0.5
                w = P * (t + 1)
                dve.wait_ge(sig("nsa_logits"), t + 1)
                if t == 0:
                    dve.wait_ge(sig("nsa_bias"), 1)
                pc = n_pc.rearrange("p (h n) -> p h n", h=4)
                v.memset(n_pc, NEG).then_inc(sig("dve_step"), 1)
                dve.wait_ge(sig("dve_step"), nth("dve_step"))
                lo, n = (31 + P, 7) if t == 0 else (31, 15)
                bias_c = n_bias[:, :, lo:lo + 16 * (n - 1) + 1:16]
                v.scalar_tensor_tensor(pc[:, :, 0:n], M[:, 4, 0:64].rearrange("p (h n) -> p h n", h=4)[:, :, 0:n],
                                       scale, bias_c, ALU.mult, ALU.add)
                for a in range(2):
                    o = bank(2 * a, 2).rearrange("p (h s) -> p h s", h=4)
                    last = v.scalar_tensor_tensor(pr[:, a, :, 0:w], o[:, :, 0:w], scale, n_bias[:, :, S - w:S],
                                                  ALU.mult, ALU.add)
                last.then_inc(sig("dve_step"), 1)
                dve.wait_ge(sig("dve_step"), nth("dve_step"))
                v.tensor_reduce(n_nmax[:, 0:4], pc[:, :, 0:15], AX.X, ALU.max, negate=True)
                last = v.tensor_reduce(n_nmax[:, 4:12].rearrange("p (a h) -> p a h", a=2), pr[:, :, :, 0:w], AX.X,
                                       ALU.max, negate=True)
                last.then_inc(sig("dve_step"), 1)
                dve.wait_ge(sig("dve_step"), nth("dve_step"))
                v.tensor_scalar(n_nmax[:, 0:4], n_nmax[:, 0:4], 1.0e8, None, ALU.min).then_inc(sig("nsa_max"), 1)
                dve.wait_ge(sig("nsa_max"), nth("nsa_max"))
                dve.wait_ge(sig("nsa_exp"), t + 1)
                if t == 0:
                    dve.wait_ge(sig("nsa_gates"), 1)
                v.tensor_scalar(n_sum, n_sum, 1.0e-30, None, ALU.max).then_inc(sig("dve_step"), 1)
                dve.wait_ge(sig("dve_step"), nth("dve_step"))
                v.reciprocal(n_wt, n_sum).then_inc(sig("dve_step"), 1)
                dve.wait_ge(sig("dve_step"), nth("dve_step"))
                v.tensor_tensor(n_wt, n_wt, n_gate[:, 12 * t:12 * t + 12], ALU.mult).then_inc(sig("dve_step"), 1)
                dve.wait_ge(sig("dve_step"), nth("dve_step"))
                v.tensor_tensor(pc, pc, spread(n_wt[:, 0:4], 16), ALU.mult)
                for a in range(2):
                    last = v.tensor_tensor(pr[:, a, :, 0:w], pr[:, a, :, 0:w], spread(n_wt[:, 4 + 4 * a:8 + 4 * a], w),
                                           ALU.mult)
                last.then_inc(sig("nsa_weighted"), 1)
                dve.wait_ge(sig("nsa_weighted"), nth("nsa_weighted"))
                dve.wait_ge(sig("nsa_turned"), t + 1)
                n = 4 * P * (t + 1)
                v.tensor_copy(n_probT[:, n:2 * n], bank(0, 4)[:, n:2 * n]).then_inc(sig("nsa_PT_dve"), 1)
                dve.wait_ge(sig("nsa_PT_dve"), nth("nsa_PT_dve"))

            def lru():
                dve.wait_ge(sig("block_out"), B_LG + 4)
                for j in range(4):
                    b = S * j
                    v.tensor_scalar(l_xc[:, b:b + S], blocks(B_LX + j), col("conv_w", 12 + j), col("conv_b", j),
                                    ALU.mult, ALU.add).then_inc(sig("dve_step"), 1)
                    dve.wait_ge(sig("dve_step"), nth("dve_step"))
                    for back in (1, 2, 3):
                        ins = v.scalar_tensor_tensor(l_xc[:, b + back:b + S], blocks(B_LX + j)[:, 0:S - back],
                                                     col("conv_w", 4 * (3 - back) + j), l_xc[:, b + back:b + S],
                                                     ALU.mult, ALU.add)
                        ins.then_inc(sig("lru_conv"), 1)
                        dve.wait_ge(sig("lru_conv"), nth("lru_conv"))

            def lru_b():
                dve.wait_ge(sig("lru_ln"), 1)
                lam, t1, c8 = col("lam", 0, 4), tiny[:, 0:4], tiny[:, 8:12]
                v.scalar_tensor_tensor(t1, lam, 0.0, t1, ALU.min, ALU.subtract).then_inc(sig("dve_step"), 1)
                dve.wait_ge(sig("dve_step"), nth("dve_step"))
                v.tensor_scalar(c8, t1, 8.0, None, ALU.mult).then_inc(sig("dve_step"), 1)
                dve.wait_ge(sig("dve_step"), nth("dve_step"))
                v.tensor_scalar(tiny[:, 12:16], t1, -8.0, None, ALU.mult).then_inc(sig("lru_c8"), 1)
                dve.wait_ge(sig("lru_c8"), nth("lru_c8"))
                dve.wait_ge(sig("lru_gated"), 2)
                v.tensor_tensor(l_u, l_u, l_xc, ALU.mult).then_inc(sig("dve_step"), 1)
                dve.wait_ge(sig("dve_step"), nth("dve_step"))
                dve.wait_ge(sig("lru_tanh"), 1)
                v.tensor_scalar(l_xc, l_t, 1.0, None, ALU.add).then_inc(sig("dve_step"), 1)
                dve.wait_ge(sig("dve_step"), nth("dve_step"))
                v.reciprocal(l_xc, l_xc).then_inc(sig("dve_step"), 1)
                dve.wait_ge(sig("dve_step"), nth("dve_step"))
                v.tensor_tensor(l_t, l_t, l_xc, ALU.mult).then_inc(sig("lru_ratio"), 1)
                dve.wait_ge(sig("lru_ratio"), nth("lru_ratio"))
                dve.wait_ge(sig("root_ready"), ROOT["lru_root"])
                v.tensor_tensor(l_u, l_u, l_t, ALU.mult).then_inc(sig("dve_step"), 1)
                dve.wait_ge(sig("dve_step"), nth("dve_step"))
                dve.wait_ge(sig("lru_decay"), 1)
                for j in range(4):
                    b = S * j
                    last = v.tensor_tensor_scan(l_t[:, b:b + S], l_a[:, b:b + S], l_u[:, b:b + S], 0.0, ALU.mult,
                                                ALU.add)
                last.then_inc(sig("dve_step"), 1)
                dve.wait_ge(sig("dve_step"), nth("dve_step"))
                dve.wait_ge(sig("lru_gelu"), 1)
                v.tensor_tensor(y_sb[:, 4:8, :].rearrange("p k t -> p (k t)"), l_t, blocks(B_LG, 4), ALU.mult) \
                    .then_inc(sig("dve_step"), 1)
                dve.wait_ge(sig("dve_step"), nth("dve_step"))

            def gla():
                dve.wait_ge(sig("gla_ln"), 1)
                v.scalar_tensor_tensor(a_e2, a_b, 0.0, a_e1, ALU.min, ALU.subtract).then_inc(sig("dve_step"), 1)
                dve.wait_ge(sig("dve_step"), nth("dve_step"))
                for j in range(2):
                    last = v.tensor_tensor_scan(a_b[:, S * j:S * (j + 1)], reset, a_e2[:, S * j:S * (j + 1)], 0.0,
                                                ALU.mult, ALU.add)
                last.then_inc(sig("dve_step"), 1)
                dve.wait_ge(sig("dve_step"), nth("dve_step"))
                bc = a_b.rearrange("p (c t) -> p c t", t=64)
                v.tensor_tensor(a_bm.rearrange("p (c t) -> p c t", t=64), bc,
                                bc[:, :, 31:32].to_broadcast([P, 8, 64]), ALU.subtract)
                last = v.tensor_tensor(a_kl.rearrange("p (c t) -> p c t", t=64),
                                       bc[:, :, 63:64].to_broadcast([P, 8, 64]), bc, ALU.subtract)
                last.then_inc(sig("dve_step"), 1)
                dve.wait_ge(sig("dve_step"), nth("dve_step"))
                v.tensor_scalar(a_bm, a_bm, 640.0, -640.0, ALU.min, ALU.max).then_inc(sig("gla_cum"), 1)
                dve.wait_ge(sig("gla_cum"), nth("gla_cum"))
                dve.wait_ge(sig("gla_exp"), 1)
                dve.wait_ge(sig("block_out"), B_GV)
                q, k = blocks(B_GQ, 2), blocks(B_GK, 2)
                sc = 64.0 ** -0.5
                v.scalar_tensor_tensor(a_qs, q, sc, a_e1, ALU.mult, ALU.mult).then_inc(sig("gla_qk"), 1)
                v.tensor_tensor(a_ks, k, a_e2, ALU.mult).then_inc(sig("gla_qk"), 1)
                v.scalar_tensor_tensor(a_qi, q, sc, a_eb, ALU.mult, ALU.mult).then_inc(sig("gla_qk"), 1)
                v.tensor_tensor(a_kl, k, a_kl, ALU.mult).then_inc(sig("gla_qk"), 1)
                dve.wait_ge(sig("gla_qk"), 4)
                v.tensor_copy(tiny[:, 32:40], a_eb.rearrange("p (c t) -> p c t", t=64)[:, :, 63]) \
                    .then_inc(sig("dve_step"), 1)
                dve.wait_ge(sig("dve_step"), nth("dve_step"))
                dve.wait_ge(sig("gla_sc"), 1)
                v.tensor_tensor(a_sc.rearrange("p h r t -> p (h r) t"),
                                bank(0, 2).rearrange("p (n t) -> p n t", n=8), over(incl, 8), ALU.mult) \
                                    .then_inc(sig("gla_masked"), 1)
                dve.wait_ge(sig("gla_masked"), nth("gla_masked"))
                dve.wait_ge(sig("gla_dS"), 1)
                v.tensor_copy(a_st[:, :, 0:3:2, :], M[:, 4, :].rearrange("p (j c v) -> p j c v", j=2, c=2))
                v.tensor_copy(a_st[:, :, 1, :], M[:, 5, :].rearrange("p (j c v) -> p j c v", j=2, c=2)[:, :, 0, :]) \
                    .then_inc(sig("dve_step"), 1)
                dve.wait_ge(sig("dve_step"), nth("dve_step"))
                for c in (1, 2):
                    for j in range(2):
                        last = v.scalar_tensor_tensor(a_st[:, j, c, :], a_st[:, j, c - 1, :],
                                                      tiny[:, 32 + 4 * j + c:33 + 4 * j + c], a_st[:, j, c, :],
                                                      ALU.mult, ALU.add)
                    last.then_inc(sig("gla_S" if c == 2 else "dve_step"), 1)
                    dve.wait_ge(sig("gla_S" if c == 2 else "dve_step"), nth("gla_S" if c == 2 else "dve_step"))
                dve.wait_ge(sig("gla_ocopy"), 1)
                dve.wait_ge(sig("root_ready"), ROOT["gla_root"])
                v.reciprocal(a_sq, a_sq).then_inc(sig("dve_step"), 1)
                dve.wait_ge(sig("dve_step"), nth("dve_step"))
                v.scalar_tensor_tensor(a_o, a_o, col("gla_gain"), a_sq, ALU.mult, ALU.mult) \
                    .then_inc(sig("dve_step"), 1)
                dve.wait_ge(sig("dve_step"), nth("dve_step"))
                dve.wait_ge(sig("gla_silu"), 1)
                v.tensor_tensor(y_sb[:, 0:4, :].rearrange("p k t -> p (k t)"), a_o, blocks(B_GG, 4), ALU.mult) \
                    .then_inc(sig("gla_done"), 1)
                dve.wait_ge(sig("gla_done"), nth("gla_done"))

            def rwkv_feat():
                dve.wait_ge(sig("block_out"), N_MIX)
                sh = r_shift.rearrange("p (k t) -> p k t", k=16)
                fe = blocks(B_R, 16).rearrange("p (k t) -> p k t", k=16)
                v.tensor_tensor(sh, fe, spread(col("mu", 0, 16), S), ALU.mult).then_inc(sig("dve_step"), 1)
                dve.wait_ge(sig("dve_step"), nth("dve_step"))
                v.tensor_tensor(fe, fe, sh, ALU.subtract).then_inc(sig("dve_step"), 1)
                dve.wait_ge(sig("dve_step"), nth("dve_step"))
                v.tensor_tensor(fe[:, :, 1:S], fe[:, :, 1:S], sh[:, :, 0:S - 1], ALU.add).then_inc(sig("rw_mixed"), 1)
                dve.wait_ge(sig("rw_mixed"), nth("rw_mixed"))

                def four(ap):
                    return ap.rearrange("p (j t) -> p j t", j=4)

                k, r_ = blocks(B_K, 4), blocks(B_R, 4)
                v.tensor_tensor(four(r_kk), four(k), spread(col("k_k", 0, 4), S), ALU.mult).then_inc(sig("dve_step"), 1)
                dve.wait_ge(sig("dve_step"), nth("dve_step"))
                dve.wait_ge(sig("rw_sig"), 1)
                for j in range(4):
                    last = v.tensor_tensor_scan(r_cs[:, S * j:S * (j + 1)], reset, r_sig[:, S * j:S * (j + 1)], 0.0,
                                                ALU.mult, ALU.add)
                last.then_inc(sig("rw_cum"), 1)
                dve.wait_ge(sig("rw_cum"), nth("rw_cum"))
                v.tensor_tensor(r_kt, r_cs, r_sig, ALU.subtract).then_inc(sig("rw_cum"), 1)
                dve.wait_ge(sig("rw_cum"), nth("rw_cum"))
                v.scalar_tensor_tensor(four(r_bonus), four(r_a), -1.0, spread(col("k_a", 0, 4), S), ALU.add,
                                       ALU.mult).then_inc(sig("dve_step"), 1)
                dve.wait_ge(sig("dve_step"), nth("dve_step"))
                v.scalar_tensor_tensor(k, r_bonus, 1.0, k, ALU.add, ALU.mult).then_inc(sig("rw_kk"), 1)
                dve.wait_ge(sig("rw_kk"), nth("rw_kk"))
                v.tensor_tensor(four(r_bonus), four(k), spread(col("r_k", 0, 4), S), ALU.mult) \
                    .then_inc(sig("dve_step"), 1)
                dve.wait_ge(sig("dve_step"), nth("dve_step"))
                v.tensor_tensor(r_bonus, r_bonus, r_, ALU.mult).then_inc(sig("rw_rk"), 1)
                dve.wait_ge(sig("rw_rk"), nth("rw_rk"))
                dve.wait_ge(sig("rw_kkss"), 1)
                v.tensor_scalar(r_tmp, bank(0, 2), 1.0e-24, None, ALU.max).then_inc(sig("rw_kkmax"), 1)
                dve.wait_ge(sig("rw_kkmax"), nth("rw_kkmax"))
                dve.wait_ge(sig("root_ready"), ROOT["rw_kkroot"])
                v.reciprocal(r_tmp, r_tmp).then_inc(sig("dve_step"), 1)
                dve.wait_ge(sig("dve_step"), nth("dve_step"))
                v.tensor_tensor(r_kk, r_kk, r_tmp, ALU.mult).then_inc(sig("dve_step"), 1)
                dve.wait_ge(sig("dve_step"), nth("dve_step"))
                dve.wait_ge(sig("rw_rks"), 1)
                v.tensor_tensor(r_bonus, bank(2, 2), blocks(B_V, 4), ALU.mult).then_inc(sig("dve_step"), 1)
                dve.wait_ge(sig("dve_step"), nth("dve_step"))
                dve.wait_ge(sig("rw_exp"), 1)
                e1, e3 = w_at(4096, 1024), w_at(5120, 1024)
                v.tensor_copy(r_dec, four(e1)[:, :, 63::64])
                v.tensor_tensor(r_tmp, r_, e1, ALU.mult)
                last = v.tensor_tensor(r_y2, r_kk, e3, ALU.mult)
                last.then_inc(sig("dve_step"), 1)
                dve.wait_ge(sig("dve_step"), nth("dve_step"))
                v.tensor_tensor(r_kt, k, r_p, ALU.mult)
                v.tensor_tensor(r_a, r_a, r_kk, ALU.mult).then_inc(sig("dve_step"), 1)
                dve.wait_ge(sig("dve_step"), nth("dve_step"))
                v.tensor_tensor(r_p, r_a, r_p, ALU.mult)
                v.memset(r_u, 0.0)
                v.tensor_copy(r_qr[:, :, :, 1, :], r_tmp.rearrange("p (j r t) -> p j r t", j=4, r=2))
                v.tensor_copy(r_qr[:, :, :, 0, :], r_y2.rearrange("p (j r t) -> p j r t", j=4, r=2)) \
                    .then_inc(sig("rw_feat"), 1)
                dve.wait_ge(sig("rw_feat"), nth("rw_feat"))

            def rwkv_pair(r):
                for n, dst in enumerate((r_ar, r_bk)):
                    dve.wait_ge(sig("rw_scores"), 2 * r + n + 1)
                    v.tensor_tensor(dst, bank(0, 4).rearrange("p (h t) -> p h t", h=8), over(strict_incl, 8),
                                    ALU.mult).then_inc(sig("rw_ar" if n == 0 else "rw_bk"), 1)
                    dve.wait_ge(sig("rw_ar" if n == 0 else "rw_bk"), nth("rw_ar" if n == 0 else "rw_bk"))

            def eight(ap):
                return ap.rearrange("p (h t) -> p h t", h=8)

            def rwkv_mask(n):
                v.tensor_tensor(eight(r_mt), r_ar[:, :, 0:P], over(level(n), 8), ALU.mult).then_inc(sig("rw_mt"), 1)
                dve.wait_ge(sig("rw_mt"), nth("rw_mt"))

            def rwkv_levels(r):
                rwkv_mask(0)
                v.tensor_tensor(eight(r_xt), over(ident, 8), eight(r_mt), ALU.subtract).then_inc(sig("dve_step"), 1)
                dve.wait_ge(sig("dve_step"), nth("dve_step"))
                dve.wait_ge(sig("rw_t1p"), 6 * r + 1)
                v.tensor_tensor(eight(r_x), over(ident, 8), bank(0, 2).rearrange("p (h t) -> p h t", h=8),
                                ALU.subtract).then_inc(sig("rw_x"), 1)
                dve.wait_ge(sig("rw_x"), nth("rw_x"))
                rwkv_mask(1)
                for n in range(1, 6):
                    dve.wait_ge(sig("rw_dx"), 5 * r + n)
                    if n < 5:
                        v.tensor_tensor(r_x, r_x, bank(2, 2), ALU.subtract)
                    v.tensor_tensor(r_xt, r_xt, bank(4, 2), ALU.subtract) \
                        .then_inc(sig("rw_x" if n < 5 else "rw_xt"), 1)
                    dve.wait_ge(sig("rw_x" if n < 5 else "rw_xt"), nth("rw_x" if n < 5 else "rw_xt"))
                    if n < 5:
                        rwkv_mask(n + 1)

            def rwkv_chunk(c):
                cb = 64 * (c % 2)
                rows = slice(cb, cb + 64)
                dve.wait_ge(sig("rw_rhsp"), c + 1)
                v.tensor_scalar(r_rhs[rows, :].rearrange("p (i n) -> p i n", i=2), M[rows, 0:2, 0:256], -1.0, None,
                                ALU.mult).then_inc(sig("rw_rhs"), 1)
                dve.wait_ge(sig("rw_rhs"), nth("rw_rhs"))
                dve.wait_ge(sig("rw_up"), c + 1)
                v.tensor_copy(r_u[rows, :], M[rows, 4, :]).then_inc(sig("rw_u"), 1)
                dve.wait_ge(sig("rw_u"), nth("rw_u"))
                if c == 3:
                    return
                dve.wait_ge(sig("rw_sp"), c + 1)
                sp_ = M[:, 3, 0:256].rearrange("p (j i) -> p j i", j=4)
                new = r_stc[(c + 1) % 2]
                dec = r_dec[:, :, c:c + 1].to_broadcast([P, 4, 64])
                if c == 0:
                    v.tensor_tensor(new, sp_, dec, ALU.mult).then_inc(sig("rw_state"), 1)
                    dve.wait_ge(sig("rw_state"), nth("rw_state"))
                else:
                    v.tensor_tensor(r_ssum, r_stc[c % 2], sp_, ALU.add).then_inc(sig("dve_step"), 1)
                    dve.wait_ge(sig("dve_step"), nth("dve_step"))
                    v.tensor_tensor(new, r_ssum, dec, ALU.mult).then_inc(sig("rw_state"), 1)
                    dve.wait_ge(sig("rw_state"), nth("rw_state"))

            def rwkv_norm():
                def four(ap):
                    return ap.rearrange("p (j t) -> p j t", j=4)
                dve.wait_ge(sig("rw_mean"), 1)
                dve.wait_ge(sig("rw_ycopy"), 4)
                v.scalar_tensor_tensor(r_y, bank(0, 2), -1.0 / 64, r_y, ALU.mult, ALU.add) \
                    .then_inc(sig("rw_centred"), 1)
                dve.wait_ge(sig("rw_centred"), nth("rw_centred"))
                dve.wait_ge(sig("root_ready"), ROOT["rw_yroot"])
                v.reciprocal(r_tmp, r_tmp).then_inc(sig("dve_step"), 1)
                dve.wait_ge(sig("dve_step"), nth("dve_step"))
                v.tensor_tensor(r_y, r_y, r_tmp, ALU.mult).then_inc(sig("dve_step"), 1)
                dve.wait_ge(sig("dve_step"), nth("dve_step"))
                v.tensor_tensor(four(r_y), four(r_y), spread(col("ln_w", 0, 4), S), ALU.mult) \
                    .then_inc(sig("dve_step"), 1)
                dve.wait_ge(sig("dve_step"), nth("dve_step"))
                v.tensor_tensor(four(r_y), four(r_y), spread(col("ln_b", 0, 4), S), ALU.add) \
                    .then_inc(sig("dve_step"), 1)
                dve.wait_ge(sig("dve_step"), nth("dve_step"))
                v.tensor_tensor(r_y, r_y, r_bonus, ALU.add).then_inc(sig("dve_step"), 1)
                dve.wait_ge(sig("dve_step"), nth("dve_step"))
                v.tensor_tensor(y_sb[:, 12:16, :].rearrange("p k t -> p (k t)"), r_y, r_g, ALU.mult) \
                    .then_inc(sig("rwkv_y"), 1)
                dve.wait_ge(sig("rwkv_y"), nth("rwkv_y"))

            steps = [0]

            def more(n):
                for _ in range(n):
                    layer, e = divmod(steps[0], KT + 4)
                    g = G_IN2[layer] + e
                    half, part = divmod(e - KT, 2)

                    def add(j):
                        n0 = 8 * part + 2 * j
                        dve.wait_ge(sig("unit_done"), UNITS + unit(g, j) + 1)
                        if half == 0:
                            v.tensor_tensor(x_sb[:, n0:n0 + 2, :], x_sb[:, n0:n0 + 2, :],
                                            stream[:, j % 2, :].rearrange("p (b t) -> p b t", b=2), ALU.add) \
                                .then_inc(sig("out_half"), 1)
                            return
                        if j == 0 and part == 0:
                            dve.wait_ge(sig("out_half"), 8 * layer + 8)
                        for b in range(2):
                            v.tensor_tensor(x_sb[:, n0 + b, :], x_sb[:, n0 + b, :],
                                            stream[:, j % 2, S * b:S * (b + 1)], ALU.add) \
                                .then_inc(sig("res_add"), 1)

                    if g + 1 < G_END:
                        lo(g + 1, then=add if e >= KT else None)
                    else:
                        for j in range(4):
                            add(j)
                    steps[0] += 1

            def attention(layer, half):
                t0 = 2 * layer + half
                kind = ATTENTIONS[t0]
                more(MORE[t0][0])
                q = p_blocks(8 * half, 4)
                qv = q.rearrange("p (b t) -> p b t", b=4)
                if kind != 3:
                    dve.wait_ge(sig("at_rot"), kind + 1)
                    cs, sn = (C2_COS64, C2_SIN64) if layer == 0 else (C2_COS32, C2_SIN32)
                    tmp = p_tmp[:, 0:1024]
                    if t0 == 0:
                        dve.wait_ge(sig("const2_in"), 16)
                    v.tensor_tensor(tmp.rearrange("p (b t) -> p b t", b=4),
                                    bank(0, 2).rearrange("p (b t) -> p b t", b=4), over(c2(sn, S), 4), ALU.mult)
                    v.tensor_tensor(qv, qv, over(c2(cs, S), 4), ALU.mult).then_inc(sig("dve_step"), 1)
                    dve.wait_ge(sig("dve_step"), nth("dve_step"))
                    v.tensor_tensor(q, q, tmp, ALU.add).then_inc(sig("at_qk"), 1)
                    dve.wait_ge(sig("at_qk"), nth("at_qk"))
                more(MORE[t0][1])
                maps = 8 if kind == 2 else 4
                scale = 32.0 ** -0.5 if kind == 2 else 64.0 ** -0.5
                for t in range(2):
                    w = P * (t + 1)
                    dve.wait_ge(sig("at_logits"), 2 * t0 + t + 1)
                    pm = prob_maps(maps, t) if kind != 3 else stick_z(t)
                    rows = maps // 2
                    ps = [b[:, 0:2 * w].rearrange("p (j s) -> p j s", j=2) for b in logit_banks(rows, t)]
                    if kind != 3:
                        mask = c2(C2_DIL if t0 == 0 else C2_CAUSAL, S)[:, S - w:S]
                        for i in range(rows):
                            last = v.scalar_tensor_tensor(pm[:, 2 * i:2 * i + 2, :], ps[i], scale, over(mask, 2),
                                                          ALU.mult, ALU.add)
                        last.then_inc(sig("dve_step"), 1)
                        dve.wait_ge(sig("dve_step"), nth("dve_step"))
                        v.tensor_reduce(p_stat[:, maps * t:maps * (t + 1)], pm, AX.X, ALU.max, negate=True) \
                            .then_inc(sig("at_max"), 1)
                        dve.wait_ge(sig("at_max"), nth("at_max"))
                    else:
                        v.tensor_scalar(pm[:, 0:2, :], ps[0], scale, None, ALU.mult)
                        v.tensor_scalar(pm[:, 2:4, :], ps[1], scale, None, ALU.mult).then_inc(sig("at_z"), 1)
                        dve.wait_ge(sig("at_z"), nth("at_z"))
                more(1)
                if kind != 3:
                    dve.wait_ge(sig("at_exp"), 2 * kind + 2)
                    inv = p_stat[:, 64:64 + 2 * maps]
                    v.reciprocal(inv, p_stat[:, 32:32 + 2 * maps]).then_inc(sig("dve_step"), 1)
                    dve.wait_ge(sig("dve_step"), nth("dve_step"))
                    if kind == 2:
                        dve.wait_ge(sig("lam_exp"), 1)
                        l = tiny[:, 26:27]
                        v.tensor_tensor(l, tiny[:, 25:26], tiny[:, 24:25], ALU.subtract).then_inc(sig("dve_step"), 1)
                        dve.wait_ge(sig("dve_step"), nth("dve_step"))
                        v.tensor_scalar(l, l, -LAMBDA_INIT, None, ALU.add).then_inc(sig("dve_step"), 1)
                        dve.wait_ge(sig("dve_step"), nth("dve_step"))
                        odd = inv.rearrange("p (m i j) -> p m i j", i=2, j=2)[:, :, 1, :]
                        v.tensor_scalar(odd, odd, l, None, ALU.mult).then_inc(sig("dve_step"), 1)
                        dve.wait_ge(sig("dve_step"), nth("dve_step"))
                    for t in range(2):
                        pm = prob_maps(maps, t)
                        ins = v.tensor_tensor(pm, pm, spread(inv[:, maps * t:maps * (t + 1)], P * (t + 1)), ALU.mult)
                        if kind != 2:
                            if t == 1:
                                ins.then_inc(sig("at_prob"), 1)
                                dve.wait_ge(sig("at_prob"), nth("at_prob"))
                        else:
                            ins.then_inc(sig("dve_step"), 1)
                            dve.wait_ge(sig("dve_step"), nth("dve_step"))
                    if kind == 2:
                        for t in range(2):
                            pm = p_probs[t].rearrange("p (h i n) -> p h i n", h=2, i=2)
                            v.tensor_tensor(diff_tmp(t).rearrange("p (h j) s -> p h (j s)", h=2),
                                            pm[:, :, 0, :], pm[:, :, 1, :], ALU.add) \
                                                .then_inc(sig("at_prob" if t == 1 else "dve_step"), 1)
                            dve.wait_ge(sig("at_prob" if t == 1 else "dve_step"), nth("at_prob" if t == 1 else "dve_step"))
                    more(MORE[t0][2] - 1)
                else:
                    dve.wait_ge(sig("stick_ln"), 1)
                    for t in range(2):
                        w = P * (t + 1)
                        z, sp_ = stick_z(t), stick_s(t)
                        v.scalar_tensor_tensor(sp_, z, 0.0, sp_, ALU.max, ALU.add).then_inc(sig("dve_step"), 1)
                        dve.wait_ge(sig("dve_step"), nth("dve_step"))
                        v.tensor_tensor(sp_, sp_, over(c2(C2_BEFORE, S)[:, S - w:S], 4), ALU.mult) \
                            .then_inc(sig("dve_step"), 1)
                        dve.wait_ge(sig("dve_step"), nth("dve_step"))
                        for hd in range(4):
                            last = v.tensor_tensor_scan(stick_r(t)[:, hd, ::-1], ones_row[:, 0:w], sp_[:, hd, ::-1],
                                                        0.0, ALU.mult, ALU.add)
                        last.then_inc(sig("dve_step"), 1)
                        dve.wait_ge(sig("dve_step"), nth("dve_step"))
                        v.tensor_tensor(z, z, stick_r(t), ALU.subtract).then_inc(sig("dve_step"), 1)
                        dve.wait_ge(sig("dve_step"), nth("dve_step"))
                        v.tensor_tensor(z, z, over(c2(C2_STRICT, S)[:, S - w:S], 4), ALU.add) \
                            .then_inc(sig("stick_log" if t == 1 else "dve_step"), 1)
                        dve.wait_ge(sig("stick_log" if t == 1 else "dve_step"), nth("stick_log" if t == 1 else "dve_step"))
                        more(1 if t == 0 else MORE[t0][2] - 2)
                more(MORE[t0][3])
                y = p_tmp[:, 2048 + 512 * (t0 % 2):2560 + 512 * (t0 % 2)]
                gate = p_blocks(8 * half + 6, 2)
                dve.wait_ge(sig("at_silu"), t0 + 1)
                if kind == 2:
                    dve.wait_ge(sig("root_ready"), ROOT["at_oroot"])
                    v.reciprocal(p_sq, p_sq).then_inc(sig("dve_step"), 1)
                    dve.wait_ge(sig("dve_step"), nth("dve_step"))
                    v.tensor_scalar(p_sq, p_sq, col("subln"), 1.0 - LAMBDA_INIT, ALU.mult, ALU.mult) \
                        .then_inc(sig("dve_step"), 1)
                    dve.wait_ge(sig("dve_step"), nth("dve_step"))
                    v.tensor_tensor(p_sq, p_sq, gate, ALU.mult).then_inc(sig("dve_step"), 1)
                    dve.wait_ge(sig("dve_step"), nth("dve_step"))
                    v.tensor_tensor(y, M[:, 3, :], p_sq, ALU.mult).then_inc(sig("at_y"), 1)
                    dve.wait_ge(sig("at_y"), nth("at_y"))
                else:
                    dve.wait_ge(sig("at_o"), t0 + 1)
                    v.tensor_tensor(y, M[:, 3, :], gate, ALU.mult).then_inc(sig("at_y"), 1)
                    dve.wait_ge(sig("at_y"), nth("at_y"))
                yv = y.rearrange("p (k t) -> p k t", k=2)
                v.tensor_copy(py_hi[:, 2 * half:2 * half + 2, :], yv).then_inc(sig("dve_step"), 1)
                dve.wait_ge(sig("dve_step"), nth("dve_step"))
                v.tensor_tensor(py_lo[:, 2 * half:2 * half + 2, :], yv, py_hi[:, 2 * half:2 * half + 2, :].bitcast(F32),
                                ALU.subtract).then_inc(sig("moving_split"), 1)
                more(MORE[t0][4])

            v.memset(tiny[:, 0:96], 0.0).then_inc(sig("dve_step"), 1)
            dve.wait_ge(sig("dve_step"), nth("dve_step"))
            v.memset(tiny[:, 20:21], EPS)
            v.memset(tiny[:, 21:22], 64e-5)
            v.memset(tiny[:, 22:23], 1.0).then_inc(sig("tiny_set"), 1)
            v.memset(tiny[:, 80:81], 0.0).then_inc(sig("merge_read"), 2)
            v.memset(tiny[:, 81:82], 0.0).then_inc(sig("res_add"), 2)
            v.memset(tiny[:, 82:83], 0.0).then_inc(sig("up_read"), 2)
            v.memset(tiny[:, 83:84], 0.0).then_inc(sig("ffn_act"), 2)
            v.memset(tiny[:, 84:85], 0.0).then_inc(sig("merge_sum"), 1)
            v.memset(tiny[:, 85:86], 0.0).then_inc(sig("unit_done"), UNITS)
            for q in range(4):
                dve.wait_ge(sig("x_squares"), q + 1)
                v.tensor_reduce(W[:, 4096 + S * q:4096 + S * (q + 1)],
                                W[:, 1024 * q:1024 * (q + 1)].rearrange("p (k t) -> p t k", k=4), AX.X, ALU.add) \
                    .then_inc(sig("x_sq"), 1)
            dve.wait_ge(sig("cols_in"), 16)
            norm_apply(0, "attn_norm", h_sb)
            nsa_blocks()
            dve.wait_ge(sig("const1_in"), 16)
            dve.wait_ge(sig("block_out"), 12)
            nsa_norms()
            nsa_small()
            nsa_softmax(0)
            nsa_softmax(1)
            lru()
            lru_b()
            gla()
            rwkv_feat()
            for r in range(2):
                rwkv_pair(r)
                rwkv_levels(r)
                for c in (2 * r, 2 * r + 1):
                    rwkv_chunk(c)
            rwkv_norm()
            def h_lo4(q):
                r4 = slice(4 * q, 4 * q + 4)
                dve.wait_ge(sig("moving_hi"), q + 1)
                v.tensor_tensor(m_lo[:, r4, :], h_sb[:, r4, :], m_hi[:, r4, :].bitcast(F32), ALU.subtract) \
                    .then_inc(sig("moving_split"), 1)

            lo(G_SPLIT, then=h_lo4)
            lo(G_SPLIT + 1)
            for q in range(4):
                r4 = slice(4 * q, 4 * q + 4)
                dve.wait_ge(sig("moving_hi"), 4 + q + 1)
                v.tensor_tensor(y2_lo[:, r4, :], y_sb[:, r4, :], y2_hi[:, r4, :].bitcast(F32), ALU.subtract) \
                    .then_inc(sig("moving_split"), 1)
            for u in range(1, 4):
                lo(G_SPLIT + u + 1)
            with dve.Fori(1, (N_GATES - MIX_GATES) // 4) as it:
                for u in range(4):
                    lo(G_SPLIT + u + 1, it)
            gv = G.rearrange("p (b n t) -> p b n t", b=4, n=KT)

            def merge_lo(n):
                dve.wait_ge(sig("merge_hi"), n + 1)
                v.tensor_tensor(m_lo[:, n, :], gv[:, 0, n, :], m_hi[:, n, :].bitcast(F32), ALU.subtract) \
                    .then_inc(sig("merged"), 1)

            def merge(u, it, first=False):
                n = u + 4 * it
                lo(G_BRANCH + u + 1, it)
                dve.wait_ge(sig("merge_sum"), n + 1)
                dve.wait_ge(sig("unit_done"), slab_done(G_BRANCH + u, it))
                v.tensor_tensor(merge_tmp, bank(2 * (u % 2), 2).rearrange("p (b t) -> p b t", b=4), gv[:, :, n, :],
                                ALU.mult).then_inc(sig("merge_read"), 1)
                if not first:
                    merge_lo(n - 1)

            dve.wait_ge(sig("block_out"), N_MIX + N_GATES)
            for u in range(4):
                merge(u, 0, u == 0)
            with dve.Fori(1, KT // 4) as it:
                for u in range(4):
                    merge(u, it)
            merge_lo(KT - 1)
            with dve.Fori(0, KT // 4) as it:
                for u in range(4):
                    lo(G_OUT + u + 1, it)
                    dve.wait_ge(sig("unit_done"), slab_done(G_OUT + u, it))
                    n = u + 4 * it
                    v.tensor_tensor(x_sb[:, n, :], x_sb[:, n, :], stream[:, u % 2, 0:S], ALU.add) \
                        .then_inc(sig("res_add"), 1)
            dve.wait_ge(sig("res_add"), 2 + KT)
            norm_split(1, "ffn_norm")

            def taps(i, p):
                dve.wait_ge(sig("ffn_tap"), 2 * i + 2)
                for back in (1, 2):
                    for w in range(2):
                        b = up_bank[2 * p + w]
                        ins = v.scalar_tensor_tensor(
                            ffn_buf[:, p, w, back:S], b[:, 0:S - back],
                            cv[:, bass.ds(i + COLS["fconv_w"][0] + (2 - back) * 2 * FB + FB * w, 1)],
                            ffn_buf[:, p, w, back:S], ALU.mult, ALU.add)
                    if back == 1:
                        ins.then_inc(sig("ffn_mid"), 1)
                        dve.wait_ge(sig("ffn_mid"), i + 1)
                    else:
                        ins.then_inc(sig("up_read"), 1)

            def multiply(i, p):
                dve.wait_ge(sig("ffn_silu"), i + 1)
                v.tensor_tensor(act32[:, p, :], ffn_buf[:, p, 0, :], ffn_buf[:, p, 1, :], ALU.mult) \
                    .then_inc(sig("ffn_mul"), 1)
                dve.wait_ge(sig("ffn_mul"), 2 * i + 1)
                v.tensor_copy(a_hi[:, i, :], act32[:, p, :]).then_inc(sig("ffn_mul"), 1)
                dve.wait_ge(sig("ffn_mul"), 2 * i + 2)
                v.tensor_tensor(a_lo[:, i, :], act32[:, p, :], a_hi[:, i, :].bitcast(F32), ALU.subtract) \
                    .then_inc(sig("ffn_act"), 1)

            def up(i, p, it=0, peel=None):
                first = i if peel is not None else 2 + p
                lo(G_UP + 2 * first + 1, it)
                if peel is None or peel >= 1:
                    taps(i - 1, 1 - p)
                lo(G_UP + 2 * first + 2, it)
                if peel is None or peel >= 1:
                    multiply(i - 1, 1 - p)

            up(0, 0, peel=0)
            up(1, 1, peel=1)
            with dve.Fori(0, FB // 2 - 2) as it:
                for p in range(2):
                    up(2 + p + 2 * it, p, it)
            up(FB - 2, 0, peel=FB - 2)
            up(FB - 1, 1, peel=FB - 1)
            taps(FB - 1, 1)
            multiply(FB - 1, 1)

            def down(u, n, it=0):
                lo(G_DOWN + u + 1, it, 8)
                if u % 4 == 3:
                    dve.wait_ge(sig("unit_done"), slab_done(G_DOWN + u, it, 8))
                    v.tensor_tensor(x_sb[:, n, :], x_sb[:, n, :], stream[:, u // 4 % 2, 0:S], ALU.add) \
                        .then_inc(sig("res_add"), 1)

            with dve.Fori(0, KT // 2 - 1) as it:
                for u in range(8):
                    down(u, u // 4 + 2 * it, it)
            for u in range(8 * (KT // 2 - 1), 8 * (KT // 2)):
                down(u, u // 4)
            dve.wait_ge(sig("res_add"), 2 + 2 * KT)
            norm_split(2, "norm2_0")
            lt = tiny[:, 40:72]
            for i in range(2):
                v.tensor_tensor(lt, col("dlam", 64 * i, 32), col("dlam", 64 * i + 32, 32), ALU.mult) \
                    .then_inc(sig("dve_step"), 1)
                dve.wait_ge(sig("dve_step"), nth("dve_step"))
                v.tensor_reduce(tiny[:, 24 + i:25 + i], lt, AX.X, ALU.add) \
                    .then_inc(sig("lam_dot" if i else "dve_step"), 1)
                dve.wait_ge(sig("lam_dot" if i else "dve_step"), nth("lam_dot" if i else "dve_step"))
            v.memset(ones_row, 1.0).then_inc(sig("dve_step"), 1)
            dve.wait_ge(sig("dve_step"), nth("dve_step"))
            for layer in range(2):
                more(8)
                attention(layer, 0)
                attention(layer, 1)
                more(2)
                dve.wait_ge(sig("res_add"), 2 + KT * (3 + layer))
                if layer == 0:
                    norm_split(3, "norm2_1")
                else:
                    norm_apply(4, "final", o_sb)


def _constants():
    i = np.arange(P)
    c1 = np.zeros((P, N_CONST1), np.float32)
    c1[:, C_ID:C_ID + P] = np.eye(P)
    c1[:, C_ONES:C_ONES + P] = 1.0
    s, t = i[:, None], i[None, :]
    same = s // 64 == t // 64
    c1[:, C_BLK:C_BLK + P] = same
    c1[:, C_STRICT:C_STRICT + P] = same & (s < t)
    c1[:, C_INCL:C_INCL + P] = same & (s <= t)
    for n in range(6):
        b = 1 << n
        c1[:, C_LEVEL + P * n:C_LEVEL + P * (n + 1)] = (s // (2 * b) == t // (2 * b)) & (s // b % 2 == 0) & (t // b % 2 == 1)
    c1[:, C_RESET:C_RESET + S] = (np.arange(S) % 64 != 0)

    c2 = np.zeros((P, N_CONST2), np.float32)
    tok = np.arange(S)
    for width, at_r, at_c, at_s in ((64, C2_R64, C2_COS64, C2_SIN64), (32, C2_R32, C2_COS32, C2_SIN32)):
        half = width // 2
        for p in range(P):
            first = p % width < half
            c2[p + half if first else p - half, at_r + p] = -1.0 if first else 1.0
        inv = (10000.0 ** (-np.arange(half, dtype=np.float32) / half)).astype(np.float32)
        ang = inv[i % half][:, None] * tok[None, :].astype(np.float32)
        c2[:, at_c:at_c + S] = np.cos(ang)
        c2[:, at_s:at_s + S] = np.sin(ang)
    dist = i[:, None] + P - np.arange(S)[None, :]
    c2[:, C2_CAUSAL:C2_CAUSAL + S] = np.where(dist >= 0, 0.0, NEG)
    times = (dist >= 0) * ((dist <= 128) * 1 + (dist % 4 == 0) * 1 + (dist % 16 == 0) * 1)
    c2[:, C2_DIL:C2_DIL + S] = np.where(times > 0, np.log(np.maximum(times, 1)), NEG)
    c2[:, C2_STRICT:C2_STRICT + S] = np.where(dist > 0, 0.0, NEG)
    c2[:, C2_BEFORE:C2_BEFORE + S] = dist > 0

    bucket = np.zeros((32, 1024), np.float32)
    d = 255 - np.arange(511)
    n = np.maximum(d, 0)
    nf = np.maximum(n, 1).astype(np.float32)
    large = 16 + (np.log(nf / np.float32(16)) / np.float32(math.log(128 / 16)) * np.float32(16)).astype(np.int32)
    which = np.where(n < 16, n, np.minimum(large, 31))
    bucket[which, np.arange(511)] = 1.0
    bucket[:, 512:512 + 511] = np.where(d >= 0, 0.0, NEG)[None, :]
    return c1, c2, bucket


def _slabs(w, kt):
    n = w.shape[1] // P
    return np.ascontiguousarray(w.reshape(kt, P, n, P).transpose(2, 1, 0, 3))


def kernel(**inputs):
    import concourse.bacc as _bacc
    from concourse import mybir as _mybir
    from concourse.bass_utils import run_bass_kernel_spmd as _run

    a = {k: np.asarray(v) for k, v in inputs.items()}

    def vec(x):
        x = np.asarray(x).reshape(-1)
        return x.reshape(-1, P).T

    def padded(x, n):
        o = np.zeros(n, np.float32)
        o[:x.shape[0]] = x
        return o

    w = a["w_in"][0]
    wm = np.zeros((D, N_MIX * P), np.float32)
    wm[:, 0:16] = w[:, 1536:1552]
    wm[:, GATE_ROW:GATE_ROW + 12] = w[:, 3856:3868]
    for b, lo, hi in ((B_KV, 3088, 3856), (B_Q, 2576, 3088), (B_LX, 1552, 2576), (B_GQ, 0, 1536),
                      (B_R, 3868, 5404), (B_XW, 5404, 5500), (B_XA, 5500, 5596), (B_XG, 5596, 5852)):
        wm[:, P * b:P * b + hi - lo] = w[:, lo:hi]
    mu = a["rwkv_mu"][0]
    mu = np.concatenate([mu[:1536], padded(mu[1536:1632], P), padded(mu[1632:1728], P), mu[1728:]])
    parts = {
        "attn_norm": vec(a["attn_norm"]), "ffn_norm": vec(a["ffn_norm"]), "norm2_0": vec(a["norm_g_2"][0]),
        "norm2_1": vec(a["norm_g_2"][1]), "final": vec(a["final_norm_g_2"]), "gk_b": vec(a["gla_b_gk"]),
        "gla_gain": vec(a["gla_out_norm"]), "conv_w": vec(a["lru_conv_w"]), "conv_b": vec(a["lru_conv_b"]),
        "b_a": vec(a["lru_b_a"]), "b_i": vec(a["lru_b_i"]), "lam": vec(a["lru_lambda"]),
        "q_gain": vec(a["nsa_q_norm"]), "k_gain": vec(a["nsa_k_norm"]), "mu": vec(mu), "w0": vec(a["rwkv_w0"]),
        "a0": vec(a["rwkv_a0"]), "k_k": vec(a["rwkv_k_k"]), "k_a": vec(a["rwkv_k_a"]), "r_k": vec(a["rwkv_r_k"]),
        "ln_w": vec(a["rwkv_ln_w"]), "ln_b": vec(a["rwkv_ln_b"]), "fconv_w": vec(a["ffn_conv_w"]),
        "fconv_b": vec(a["ffn_conv_b"]), "dlam": np.broadcast_to(a["diff_lam_2"].reshape(1, -1), (P, 128)),
        "subln": np.tile(a["diff_subln_g_2"].reshape(-1), 2)[:, None], "pos": a["nsa_cmp_pos"][0].T,
    }
    cols = np.zeros((P, N_COLS), np.float32)
    for name, (at, n) in COLS.items():
        cols[:, at:at + n] = parts[name]
    small = np.zeros((P, N_SMALL), np.float32)

    def put(name, x):
        at, n = SMALL[name]
        small[:x.shape[0], at:at + n] = x

    put("w_gk", a["gla_w_gk"][0])
    put("lru_a", a["lru_w_a"][0].transpose(1, 0, 2).reshape(P, 512))
    put("lru_i", a["lru_w_i"][0].transpose(1, 0, 2).reshape(P, 512))
    put("w_lora", a["rwkv_w_lora"][0])
    put("a_lora", a["rwkv_a_lora"][0])
    put("g_lora", a["rwkv_g_lora"][0].reshape(2, P, 512).transpose(1, 0, 2).reshape(P, 1024))
    put("cmp_k2", a["nsa_cmp_k2"][0])
    put("cmp_v2", a["nsa_cmp_v2"][0])
    put("rel", a["rel_bias"])
    c1, c2, bucket = _constants()

    up = _slabs(a["ffn_up"][0], KT)
    up = up.reshape(2, FB, P, KT, P).transpose(1, 0, 2, 3, 4).reshape(2 * FB, P, KT, P)
    down = _slabs(a["ffn_down"][0], FB).reshape(KT, P, DOWN_SLABS, DOWN_K, P).transpose(0, 2, 1, 3, 4)
    branch = a["w_branch"][0].reshape(4, 4, P, KT, P).transpose(3, 2, 0, 1, 4).reshape(KT, P, KT, P)
    order = np.array([[0, 1], [1, 0]])
    out2 = a["w_out_2"].reshape(2, 2, 2, P, 2, 8, P)
    out2 = np.stack([out2[n][order[n]] for n in range(2)]).transpose(0, 1, 4, 3, 5, 2, 6).reshape(8, P, KT, P)
    in2 = [_slabs(a["w_in_2"][n], KT).reshape(2, 8, P, KT, P)[order[n]].reshape(KT, P, KT, P) for n in range(2)]
    arrays = {
        "xT": a["x"][0].T.reshape(KT, P, S).transpose(1, 0, 2),
        "cols": cols, "small": small, "const1": c1, "const2": c2, "bucket": bucket,
        "flip": np.ascontiguousarray(np.eye(P, dtype=np.float32)[::-1]),
        "w_mix": _slabs(wm, KT),
        "w_cmp": np.concatenate([a[n][0].reshape(2, KT, P, P).transpose(0, 2, 1, 3)
                                 for n in ("nsa_cmp_k1", "nsa_cmp_v1")]),
        "w_gate": _slabs(w[:, 5852:], KT), "w_branch": branch, "w_out": _slabs(a["w_out"][0], KT),
        "w_up": up, "w_down": down.reshape(KT * DOWN_SLABS, P, DOWN_K, P),
        "w_in2": np.concatenate(in2), "w_out2": out2,
    }
    nc = _bacc.Bacc("TRN2", target_bir_lowering=False, num_devices=1)
    args = {}
    for name, x in arrays.items():
        x = np.ascontiguousarray(x)
        arrays[name] = x
        args[name] = nc.dram_tensor(name, x.shape, _mybir.dt.from_np(x.dtype), kind="ExternalInput").ap()
    args["bias_scratch"] = nc.dram_tensor("bias_scratch", (4, 512), F32, kind="Internal").ap()
    args["out"] = nc.dram_tensor("outT", (P, KT, S), F32, kind="ExternalOutput").ap()
    build(nc, **args)
    got = _run(nc, [arrays], core_ids=[0]).results[0]["outT"]
    return np.ascontiguousarray(got.transpose(1, 0, 2).reshape(D, S).T)[None]
```
